# Optimizing a Trainium2 kernel written in Bass

```python
import math
import jax
import jax.numpy as jnp
from jax import lax
import numpy as np

D_MODEL = 1024
BATCH = 1
SEQ = 1024
DEPTH = 1
DEC_BATCH = 8
DEC_SEQ = 8
PAST_LEN = 256
PAGE_SIZE = 128

N_META = 16
HEAD_DIM = 64
D_ATT = D_MODEL // 2
N_HEADS = D_ATT // HEAD_DIM
D_SSM = D_MODEL // 4
SSM_GROUP = 16
N_SSM_GROUPS = D_SSM // SSM_GROUP
SSM_STATE = 64
D_POOL = D_MODEL // 4
POOL_WINDOWS = (2, 4, 8, 16)
POOL_GROUP = D_POOL // len(POOL_WINDOWS)
POOL_BUF = max(POOL_WINDOWS) - 1
D_IN = 3 * D_ATT + N_HEADS + D_SSM + D_POOL
Q_BLOCK = 128
SCALE = HEAD_DIM ** -0.5
N_EXPERTS = 16
N_EXPERT_GROUPS = 4
EXPERTS_PER_GROUP = N_EXPERTS // N_EXPERT_GROUPS
TOP_K = 2
D_EXPERT = D_MODEL // 4
ALPHA = (2 * DEPTH) ** 0.25
BETA = (8 * DEPTH) ** -0.25
LN_EPS = 1e-5
NEG_INF = -1e30
DT_MIN = 1e-3
DT_MAX = 1e-1

kernel_name = 'hybrid_fox_s5_pool_moe_step'

def layer_norm(x, g, b):
    xf = x.astype(jnp.float32)
    mu = xf.mean(-1, keepdims=True)
    var = jnp.square(xf - mu).mean(-1, keepdims=True)
    y = (xf - mu) * lax.rsqrt(var + LN_EPS) * g.astype(jnp.float32) + b.astype(jnp.float32)
    return y.astype(x.dtype)

def project(x, w_in, b_f):
    z = x @ w_in
    o1, o2, o3 = D_ATT, 2 * D_ATT, 3 * D_ATT
    o4 = o3 + N_HEADS
    o5 = o4 + D_SSM
    hs = x.shape[:-1] + (N_HEADS, HEAD_DIM)
    q = z[..., :o1].reshape(hs)
    k = z[..., o1:o2].reshape(hs)
    v = z[..., o2:o3].reshape(hs)
    logf = jax.nn.log_sigmoid(z[..., o3:o4].astype(jnp.float32) + b_f.astype(jnp.float32))
    u = z[..., o4:o5].reshape(x.shape[:-1] + (N_SSM_GROUPS, SSM_GROUP))
    p = z[..., o5:]
    return q, k, v, logf, u, p

def fox_prompt(q, k, v, logf):
    B, L = q.shape[0], q.shape[1]
    lead = (-N_META) % Q_BLOCK
    tail = (-(lead + L)) % Q_BLOCK
    Lt = lead + L + tail
    pw = ((0, 0), (lead, tail), (0, 0), (0, 0))
    qp, kp, vp = jnp.pad(q, pw), jnp.pad(k, pw), jnp.pad(v, pw)
    cum = jnp.cumsum(jnp.pad(logf, pw[:3]), axis=1)
    cum_k = cum.transpose(0, 2, 1)[:, :, None, :]
    kpos = jnp.arange(Lt)
    kvalid = (kpos >= lead) & (kpos < lead + L)
    nb = Lt // Q_BLOCK
    qb = qp.reshape(B, nb, Q_BLOCK, N_HEADS, HEAD_DIM).swapaxes(0, 1)
    cb = cum.reshape(B, nb, Q_BLOCK, N_HEADS).swapaxes(0, 1)

    def block(args):
        i, qi, ci = args
        s = jnp.einsum('bqhd,bkhd->bhqk', qi, kp, preferred_element_type=jnp.float32) * SCALE
        s = s + ci.transpose(0, 2, 1)[..., None] - cum_k
        qpos = i * Q_BLOCK + jnp.arange(Q_BLOCK)
        mask = (kpos[None, :] <= qpos[:, None]) & kvalid[None, :]
        pr = jax.nn.softmax(jnp.where(mask, s, NEG_INF), axis=-1)
        return jnp.einsum('bhqk,bkhd->bqhd', pr.astype(vp.dtype), vp)

    o = lax.map(block, (jnp.arange(nb), qb, cb))
    return o.swapaxes(0, 1).reshape(B, Lt, N_HEADS, HEAD_DIM)[:, lead:lead + L]

def fox_sample(q, k, v, logf, k_past, v_past, lf_past):
    P, T = k_past.shape[1], q.shape[1]
    K = jnp.concatenate([k_past.astype(k.dtype), k], axis=1)
    V = jnp.concatenate([v_past.astype(v.dtype), v], axis=1)
    cum = jnp.cumsum(jnp.concatenate([lf_past.astype(jnp.float32), logf], axis=1), axis=1)
    s = jnp.einsum('bqhd,bkhd->bhqk', q, K, preferred_element_type=jnp.float32) * SCALE
    s = s + cum[:, P:].transpose(0, 2, 1)[..., None] - cum.transpose(0, 2, 1)[:, :, None, :]
    mask = jnp.arange(P + T)[None, :] <= (P + jnp.arange(T))[:, None]
    pr = jax.nn.softmax(jnp.where(mask, s, NEG_INF), axis=-1)
    return jnp.einsum('bhqk,bkhd->bqhd', pr.astype(V.dtype), V)

def _complex_affine_combine(e1, e2):
    a1r, a1i, b1r, b1i = e1
    a2r, a2i, b2r, b2i = e2
    return (a2r * a1r - a2i * a1i, a2r * a1i + a2i * a1r,
            a2r * b1r - a2i * b1i + b2r, a2r * b1i + a2i * b1r + b2i)

def s5_mix(u, x0_re, x0_im, lam_re, lam_im, log_dt, b_re, b_im, c_re, c_im, d, w_glu, b_glu):
    f32 = jnp.float32
    dt = jnp.exp(log_dt.astype(f32))[:, None]
    lr, li = lam_re.astype(f32), lam_im.astype(f32)
    mag = jnp.exp(lr * dt)
    ab_re, ab_im = mag * jnp.cos(li * dt), mag * jnp.sin(li * dt)
    nr, ni = ab_re - 1.0, ab_im
    den = lr * lr + li * li
    gr = (nr * lr + ni * li) / den
    gi = (ni * lr - nr * li) / den
    br, bi = b_re.astype(f32), b_im.astype(f32)
    bb_re = gr[..., None] * br - gi[..., None] * bi
    bb_im = gr[..., None] * bi + gi[..., None] * br
    uf = u.astype(f32)
    bu_re = jnp.einsum('btgc,gpc->btgp', uf, bb_re)
    bu_im = jnp.einsum('btgc,gpc->btgp', uf, bb_im)
    x0r, x0i = x0_re.astype(f32), x0_im.astype(f32)
    bu_re = bu_re.at[:, 0].add(ab_re * x0r - ab_im * x0i)
    bu_im = bu_im.at[:, 0].add(ab_re * x0i + ab_im * x0r)
    a_re = jnp.broadcast_to(ab_re, bu_re.shape)
    a_im = jnp.broadcast_to(ab_im, bu_im.shape)
    _, _, xr, xi = lax.associative_scan(_complex_affine_combine, (a_re, a_im, bu_re, bu_im), axis=1)
    y = (jnp.einsum('btgp,gcp->btgc', xr, c_re.astype(f32))
         - jnp.einsum('btgp,gcp->btgc', xi, c_im.astype(f32))
         + d.astype(f32).reshape(N_SSM_GROUPS, SSM_GROUP) * uf)
    y = jax.nn.gelu(y.reshape(u.shape[:2] + (D_SSM,)))
    out = y * jax.nn.sigmoid(y @ w_glu.astype(f32) + b_glu.astype(f32))
    return out.astype(u.dtype), xr[:, -1], xi[:, -1]

def pool_mix(p, buf, pos0, w_pool, s_pool):
    B, T = p.shape[0], p.shape[1]
    full = jnp.concatenate([buf.astype(p.dtype), p], axis=1)
    ff = full.astype(jnp.float32)
    cs = jnp.concatenate([jnp.zeros((B, 1, D_POOL), jnp.float32), jnp.cumsum(ff, axis=1)], axis=1)
    pos = pos0 + jnp.arange(T)
    outs = []
    for gi, w in enumerate(POOL_WINDOWS):
        sl = slice(gi * POOL_GROUP, (gi + 1) * POOL_GROUP)
        hi = cs[:, POOL_BUF + 1:POOL_BUF + 1 + T, sl]
        lo = cs[:, POOL_BUF + 1 - w:POOL_BUF + 1 - w + T, sl]
        cnt = jnp.minimum(w, pos + 1).astype(jnp.float32)[None, :, None]
        outs.append((hi - lo) / cnt - ff[:, POOL_BUF:, sl])
    m = jnp.stack(outs, axis=2)
    y = jnp.einsum('btgc,gcd->btgd', m, w_pool.astype(jnp.float32)).reshape(B, T, D_POOL)
    y = y * s_pool.astype(jnp.float32)
    return y.astype(p.dtype), full[:, -POOL_BUF:]

def moe(h, w_router, b_router, w_gate, w_up, w_down):
    f32 = jnp.float32
    n = h.shape[0]
    aff = jax.nn.sigmoid(h.astype(f32) @ w_router.astype(f32))
    biased = aff + b_router.astype(f32)
    gscore = lax.top_k(biased.reshape(n, N_EXPERT_GROUPS, EXPERTS_PER_GROUP), 2)[0].sum(-1)
    gsel = jnp.argmax(gscore, axis=-1)
    in_group = (jnp.arange(N_EXPERTS) // EXPERTS_PER_GROUP)[None, :] == gsel[:, None]
    _, idx = lax.top_k(jnp.where(in_group, biased, NEG_INF), TOP_K)
    w_sel = jnp.take_along_axis(aff, idx, axis=-1)
    w_sel = w_sel / w_sel.sum(-1, keepdims=True)
    gates = jnp.einsum('nk,nke->ne', w_sel, jax.nn.one_hot(idx, N_EXPERTS, dtype=f32))
    a = jnp.einsum('nd,edf->nef', h, w_gate)
    b = jnp.einsum('nd,edf->nef', h, w_up)
    hid = jax.nn.silu(a) * b * gates[..., None].astype(h.dtype)
    return jnp.einsum('nef,efd->nd', hid, w_down)

def post_norm_block(x, mix, w_out, ln1_g, ln1_b, w_router, b_router, w_gate, w_up, w_down, ln2_g, ln2_b):
    h = layer_norm(ALPHA * x + mix @ w_out, ln1_g, ln1_b)
    f = moe(h.reshape(-1, D_MODEL), w_router, b_router, w_gate, w_up, w_down).reshape(h.shape)
    return layer_norm(ALPHA * h + f, ln2_g, ln2_b)

def setup_inputs(seed: int = 0) -> dict:
    key = jax.random.key(seed)
    ks = iter(jax.random.split(key, 48))
    f32 = jnp.float32

    def nrm(shape, scale=1.0, mean=0.0):
        return mean + scale * jax.random.normal(next(ks), shape, f32)

    n_pages = PAST_LEN // PAGE_SIZE
    n_used = DEC_BATCH * n_pages
    n_pool = n_used + (n_used + 3) // 4
    page_table = jax.random.permutation(next(ks), n_pool)[:n_used].reshape(DEC_BATCH, n_pages).astype(jnp.int32)
    n_idx = jnp.arange(SSM_STATE, dtype=f32)
    return {
        'x_prompt': nrm((BATCH, SEQ, D_MODEL)),
        'x_sample': nrm((DEC_BATCH, DEC_SEQ, D_MODEL)),
        'cache_k': nrm((n_pool, DEPTH, PAGE_SIZE, N_HEADS, HEAD_DIM)),
        'cache_v': nrm((n_pool, DEPTH, PAGE_SIZE, N_HEADS, HEAD_DIM)),
        'cache_logf': jax.nn.log_sigmoid(nrm((n_pool, DEPTH, PAGE_SIZE, N_HEADS), 1.0, 2.0)),
        'page_table': page_table,
        'state_ssm_re': nrm((DEC_BATCH, DEPTH, N_SSM_GROUPS, SSM_STATE), 0.3),
        'state_ssm_im': nrm((DEC_BATCH, DEPTH, N_SSM_GROUPS, SSM_STATE), 0.3),
        'state_pool': nrm((DEC_BATCH, DEPTH, POOL_BUF, D_POOL)),
        'meta_tokens': nrm((N_META, D_MODEL)),
        'ln0_g': nrm((D_MODEL,), 0.02, 1.0),
        'ln0_b': nrm((D_MODEL,), 0.02),
        'w_in': nrm((DEPTH, D_MODEL, D_IN), D_MODEL ** -0.5),
        'b_forget': nrm((DEPTH, N_HEADS), 0.5, 2.0),
        'ssm_lam_re': nrm((DEPTH, N_SSM_GROUPS, SSM_STATE), 0.01, -0.5),
        'ssm_lam_im': math.pi * n_idx + nrm((DEPTH, N_SSM_GROUPS, SSM_STATE), 0.01),
        'ssm_log_dt': jax.random.uniform(next(ks), (DEPTH, N_SSM_GROUPS), f32, math.log(DT_MIN), math.log(DT_MAX)),
        'ssm_b_re': nrm((DEPTH, N_SSM_GROUPS, SSM_STATE, SSM_GROUP), (2 * SSM_GROUP) ** -0.5),
        'ssm_b_im': nrm((DEPTH, N_SSM_GROUPS, SSM_STATE, SSM_GROUP), (2 * SSM_GROUP) ** -0.5),
        'ssm_c_re': nrm((DEPTH, N_SSM_GROUPS, SSM_GROUP, SSM_STATE), SSM_STATE ** -0.5),
        'ssm_c_im': nrm((DEPTH, N_SSM_GROUPS, SSM_GROUP, SSM_STATE), SSM_STATE ** -0.5),
        'ssm_d': nrm((DEPTH, D_SSM)),
        'w_glu': nrm((DEPTH, D_SSM, D_SSM), D_SSM ** -0.5),
        'b_glu': nrm((DEPTH, D_SSM), 0.02),
        'w_pool': nrm((DEPTH, len(POOL_WINDOWS), POOL_GROUP, POOL_GROUP), POOL_GROUP ** -0.5),
        's_pool': nrm((DEPTH, D_POOL), 0.02, 1.0),
        'w_out': nrm((DEPTH, D_MODEL, D_MODEL), BETA * D_MODEL ** -0.5),
        'ln1_g': nrm((DEPTH, D_MODEL), 0.02, 1.0),
        'ln1_b': nrm((DEPTH, D_MODEL), 0.02),
        'w_router': nrm((D_MODEL, N_EXPERTS), D_MODEL ** -0.5),
        'b_router': nrm((N_EXPERTS,), 0.01),
        'w_gate': nrm((DEPTH, N_EXPERTS, D_MODEL, D_EXPERT), D_MODEL ** -0.5),
        'w_up': nrm((DEPTH, N_EXPERTS, D_MODEL, D_EXPERT), D_MODEL ** -0.5),
        'w_down': nrm((DEPTH, N_EXPERTS, D_EXPERT, D_MODEL), BETA * D_EXPERT ** -0.5),
        'ln2_g': nrm((DEPTH, D_MODEL), 0.02, 1.0),
        'ln2_b': nrm((DEPTH, D_MODEL), 0.02),
    }

def reference(x_prompt, x_sample, cache_k, cache_v, cache_logf, page_table,
              state_ssm_re, state_ssm_im, state_pool,
              meta_tokens, ln0_g, ln0_b, w_in, b_forget,
              ssm_lam_re, ssm_lam_im, ssm_log_dt, ssm_b_re, ssm_b_im, ssm_c_re, ssm_c_im, ssm_d,
              w_glu, b_glu, w_pool, s_pool, w_out, ln1_g, ln1_b,
              w_router, b_router, w_gate, w_up, w_down, ln2_g, ln2_b):
    f32 = jnp.float32
    bp, bs = x_prompt.shape[0], x_sample.shape[0]
    n_prompt = N_META + x_prompt.shape[1]
    n_new = x_sample.shape[1]
    past_len = page_table.shape[1] * cache_k.shape[2]
    meta = jnp.broadcast_to(meta_tokens.astype(x_prompt.dtype)[None], (bp, N_META, D_MODEL))
    xp = layer_norm(jnp.concatenate([meta, x_prompt], axis=1), ln0_g, ln0_b)
    xs = layer_norm(x_sample, ln0_g, ln0_b)
    zero_state = jnp.zeros((bp, N_SSM_GROUPS, SSM_STATE), f32)
    zero_buf = jnp.zeros((bp, POOL_BUF, D_POOL), xp.dtype)
    kp_l, vp_l, lfp_l, srp_l, sip_l, pbp_l = [], [], [], [], [], []
    kq_l, vq_l, lfq_l, srq_l, siq_l, pbq_l = [], [], [], [], [], []
    for l in range(DEPTH):
        ssm_w = (ssm_lam_re[l], ssm_lam_im[l], ssm_log_dt[l], ssm_b_re[l], ssm_b_im[l],
                 ssm_c_re[l], ssm_c_im[l], ssm_d[l], w_glu[l], b_glu[l])
        blk_w = (w_out[l], ln1_g[l], ln1_b[l], w_router, b_router,
                 w_gate[l], w_up[l], w_down[l], ln2_g[l], ln2_b[l])
        q, k, v, lf, u, p = project(xp, w_in[l], b_forget[l])
        att = fox_prompt(q, k, v, lf).reshape(bp, n_prompt, D_ATT)
        ys, sr, si = s5_mix(u, zero_state, zero_state, *ssm_w)
        yq, pb = pool_mix(p, zero_buf, 0, w_pool[l], s_pool[l])
        xp = post_norm_block(xp, jnp.concatenate([att, ys, yq], axis=-1), *blk_w)
        kp_l.append(k); vp_l.append(v); lfp_l.append(lf)
        srp_l.append(sr); sip_l.append(si); pbp_l.append(pb)
        q, k, v, lf, u, p = project(xs, w_in[l], b_forget[l])
        k_past = cache_k[page_table, l].reshape(bs, past_len, N_HEADS, HEAD_DIM)
        v_past = cache_v[page_table, l].reshape(bs, past_len, N_HEADS, HEAD_DIM)
        lf_past = cache_logf[page_table, l].reshape(bs, past_len, N_HEADS)
        att = fox_sample(q, k, v, lf, k_past, v_past, lf_past).reshape(bs, n_new, D_ATT)
        ys, sr, si = s5_mix(u, state_ssm_re[:, l], state_ssm_im[:, l], *ssm_w)
        yq, pb = pool_mix(p, state_pool[:, l], past_len, w_pool[l], s_pool[l])
        xs = post_norm_block(xs, jnp.concatenate([att, ys, yq], axis=-1), *blk_w)
        kq_l.append(k); vq_l.append(v); lfq_l.append(lf)
        srq_l.append(sr); siq_l.append(si); pbq_l.append(pb)
    y_prompt = xp[:, N_META:]
    y_sample = xs
    return (y_prompt, y_sample,
            jnp.stack(kp_l, axis=1), jnp.stack(vp_l, axis=1), jnp.stack(lfp_l, axis=1),
            jnp.stack(srp_l, axis=1), jnp.stack(sip_l, axis=1), jnp.stack(pbp_l, axis=1),
            jnp.stack(kq_l, axis=1), jnp.stack(vq_l, axis=1), jnp.stack(lfq_l, axis=1),
            jnp.stack(srq_l, axis=1), jnp.stack(siq_l, axis=1), jnp.stack(pbq_l, axis=1))


_drawn_inputs = setup_inputs


def setup_inputs(seed=0):
    import zlib

    import numpy as np

    out = dict(_drawn_inputs(seed))
    spreads = {}
    factors = {'ssm_lam_re': 14.071, 'b_glu': 26.62, 's_pool': 5.179, 'ln2_g': 8.126, 'ln2_b': 8.376}
    for name, (base, spread) in spreads.items():
        noise = np.random.default_rng([zlib.crc32(name.encode()), seed]).standard_normal(out[name].shape)
        drawn = base * np.exp(spread * noise) if base else spread * noise
        out[name] = jnp.asarray(drawn.astype(out[name].dtype))
    for name, factor in factors.items():
        out[name] = (out[name] * factor).astype(out[name].dtype)
    return out
```

```python
import math
from contextlib import ExitStack, contextmanager

import concourse.bass as bass
from concourse import mybir

F32 = mybir.dt.float32
I32 = mybir.dt.int32
ALU = mybir.AluOpType
ACT = mybir.ActivationFunctionType
AX = mybir.AxisListType.X

P = 128
D = 1024
KD = D // P
SEQ, META = 1024, 16
NPR = META + SEQ
BS, TS = 8, 8
NSA = BS * TS
TOK = NPR + NSA
NT = (TOK + P - 1) // P
TP = NT * P
H, HD = 8, 64
DA = H * HD
DS = DPL = D // 4
O_F, O_U = 3 * DA, 3 * DA + H
O_P = O_U + DS
DIN = O_P + DPL
PAGE, NPAGE, NPOOL = 128, 2, 20
PAST = PAGE * NPAGE
NPAIR = 8
L = 4
CH = TOK // L
CHP = NPR // L
CHS = CH - CHP
CHT = TP // L
PBUF = 15
E, EG, DE = 16, 4, 256
SLOTT = 2 * TOK // P + E
ALPHA = 2 ** 0.25
EPS = 1e-5
SCALE = HD ** -0.5
NEG = -1e30
CHUNKS = [(0, 384), (384, 384), (768, 384)]
CHUNKS_T = [(0, 384), (384, 384), (768, TOK - 768)]


class Link:

    def __init__(self, eng, sem):
        self.eng, self.sem, self.n = eng, sem, 0

    def __call__(self, ins):
        self.n += 1
        ins.then_inc(self.sem, 1)
        self.eng.wait_ge(self.sem, self.n)


def bcast_rows(ap, n):
    return ap.rearrange("(a w) -> a w", a=1).to_broadcast([n, ap.shape[0]])


SSMN = 64
AR = 21120
(LRE, LIM, LDT, DT, LRDT, LRDT4, MAG, MAG4, COS0, SIN0, KT, KT2, ANG, ANG2, COS, SIN,
 T0, T1, NR, DEN, GR, GI) = range(22)
ROUND = 1.5 * 2 ** 23
TURN_HI = 6.28125
TURN_LO = 2 * math.pi - TURN_HI
PI_IN = 3.1415925
ROUNDS = (SLOTT + 2) // 3
TT = 3 * ROUNDS + 3
LEAST = (2 * TOK + P - 1) // P + (-((2 * TOK + P - 1) // P)) % 3


def hybrid_step(nc, A, O):
    ctx = ExitStack()
    with ctx:
        def sb(name, shape, dt=F32):
            return ctx.enter_context(nc.sbuf_tensor(name, shape, dt))

        made = []

        def sem(name):
            made.append(nc.alloc_semaphore(name=name))
            return made[-1]

        @contextmanager
        def phase():
            made.clear()
            with ExitStack() as mem:
                with nc.Block() as block:
                    yield mem, block
            nc.clear_and_free_semaphores(list(made))
            nc.all_engine_barrier()

        duo = [ctx.enter_context(nc.psum_tensor(f"banks{2 * i}_{2 * i + 1}", [P, 1024], F32)) for i in range(4)]
        bank = [duo[i // 2][:, 512 * (i % 2):512 * (i % 2) + 512] for i in range(8)]
        score_slot = duo[0:2]

        ctx.enter_context(nc.allow_non_contiguous_dma(reason="small parameter vectors"))

        ident = sb("ident", [P, P])
        causal = sb("causal", [P, P])
        xT = sb("xT", [P, KD, TP])
        mixT = sb("mixT", [P, KD, TP])
        v_tok = sb("v_tok", [P, NT, DA])
        gb = sb("gb", [P, 2, D])
        cum = sb("cum", [H, TP])
        ncum = sb("ncum", [H, TP])
        qs_T = sb("qs_T", [P, H // 2, NSA])
        ks_T = sb("ks_T", [P, H // 2, NSA])
        ones_col = sb("ones_col", [P, 1])
        arena = sb("arena", [P, AR])

        x_park = nc.dram_tensor("x_park", (NT, P, D), F32).ap()
        h_park = nc.dram_tensor("h_park", (TP, D), F32).ap()
        gate_sums = nc.dram_tensor("gate_sums", (2, H, TP), F32).ap()
        slot_tok = nc.dram_tensor("slot_tok", (SLOTT * P, 1), I32).ap()
        y_park = nc.dram_tensor("y_park", (SLOTT * P, D), F32).ap()

        with phase() as (mem, block):
            xin = [mem.enter_context(nc.sbuf_tensor(f"xin{s}", [P, D], F32)) for s in range(3)]
            st = [mem.enter_context(nc.sbuf_tensor(f"ln0_st{s}", [P, 20], F32)) for s in range(3)]
            s_ids = sem("n_ident_steps")
            s_gain = sem("n_gain_loaded")
            s_shift = sem("n_shift_loaded")
            s_xa = [sem(f"n_rows_low{s}") for s in range(3)]
            s_xb = [sem(f"n_rows_high{s}") for s in range(3)]
            s_std = sem("n_std_ready")
            s_scaled = sem("n_centred")
            s_gained = sem("n_gained")
            s_normed = sem("n_normed")
            s_copied = sem("n_xT_copied")
            s_stored = [sem(f"n_x_parked{s}") for s in range(3)]
            s_pc = sem("n_pool_chain")
            s_nb = sem("n_bias_ready")
            s_turned_half = sem("n_turned_half")
            s_sq = sem("n_var_ready")

            @block.sync
            def _(sp):
                sp.dma_start(gb[:, 0, :], bcast_rows(A["ln0_g"], P)).then_inc(s_gain, 16)
                sp.dma_start(gb[:, 1, :], bcast_rows(A["ln0_b"], P)).then_inc(s_shift, 16)

                def load(t):
                    s, xp = t % 3, A["x_prompt"][0]
                    if t >= 3:
                        sp.wait_ge(s_stored[s], 16 * (t // 3))
                        sp.wait_ge(s_turned_half, 2 * (t - 2))
                    if t == 0:
                        sp.dma_start(xin[s][0:META, :], A["meta_tokens"]).then_inc(s_xa[s], 16)
                    else:
                        sp.dma_start(xin[s][0:META, :], xp[t * P - META:t * P, :]).then_inc(s_xa[s], 16)
                    if t < NT - 1:
                        sp.dma_start(xin[s][META:P, :], xp[t * P:(t + 1) * P - META, :]).then_inc(s_xb[s], 16)
                    else:
                        sp.dma_start(xin[s][META:META + NSA, :],
                                     A["x_sample"].rearrange("b t d -> (b t) d")).then_inc(s_xb[s], 16)

                def park(t):
                    sp.wait_ge(s_normed, t + 1)
                    sp.dma_start(x_park[t], xin[t % 3][:, :]).then_inc(s_stored[t % 3], 16)

                for t in range(3):
                    load(t)
                for t in range(NT):
                    park(t)
                    if t + 3 < NT:
                        load(t + 3)
                for s in range(3):
                    sp.wait_ge(s_stored[s], 16 * (NT // 3))

            @block.gpsimd
            def _(pool):
                chain = Link(pool, s_pc)
                chain(nc.gpsimd.memset(ident[:, :], 0.0))
                nc.gpsimd.affine_select(out=ident[:, :], in_=ident[:, :], compare_op=ALU.not_equal, fill=1.0,
                                        base=0, pattern=[[-1, P]], channel_multiplier=1).then_inc(s_ids, 1)
                chain(nc.gpsimd.memset(causal[:, :], 0.0))
                chain(nc.gpsimd.affine_select(out=causal[:, :], in_=causal[:, :], compare_op=ALU.is_ge, fill=NEG,
                                              base=0, pattern=[[-1, P]], channel_multiplier=1))
                nc.gpsimd.memset(ones_col[:, :], 1.0)
                pool.wait_ge(s_shift, 16)
                with pool.Fori(0, NT // 3) as i:
                    for s in range(3):
                        pool.wait_ge(s_gained, i * 3 + (s + 1))
                        nc.gpsimd.tensor_tensor(xin[s][:, :], xin[s][:, :], gb[:, 1, :],
                                                ALU.add).then_inc(s_normed, 1)

            @block.vector
            def _(dve):
                def stats(i, s):
                    dve.wait_ge(s_xa[s], i * 16 + 16)
                    dve.wait_ge(s_xb[s], i * 16 + 16)
                    nc.vector.bn_stats(st[s][:, 0:6], xin[s][:, 0:512]).then_inc(s_sq, 1)
                    nc.vector.bn_stats(st[s][:, 6:12], xin[s][:, 512:1024]).then_inc(s_sq, 1)
                    dve.wait_ge(s_sq, i * 12 + (4 * s + 2))
                    nc.vector.tensor_copy(st[s][:, 18:19], st[s][:, 0:1])
                    nc.vector.bn_aggr(st[s][:, 12:14], st[s][:, 0:12]).then_inc(s_sq, 1)
                    dve.wait_ge(s_sq, i * 12 + (4 * s + 3))
                    nc.vector.tensor_scalar_add(st[s][:, 14:15], st[s][:, 13:14], EPS).then_inc(s_sq, 1)

                def centre(i, s):
                    dve.wait_ge(s_std, i * 3 + (s + 1))
                    nc.vector.reciprocal(st[s][:, 16:17], st[s][:, 15:16]).then_inc(s_nb, 1)
                    dve.wait_ge(s_nb, i * 6 + (2 * s + 1))
                    nc.vector.tensor_scalar(st[s][:, 17:18], st[s][:, 12:13], st[s][:, 16:17], -1.0,
                                            ALU.mult, ALU.mult).then_inc(s_nb, 1)

                def gain(i, s):
                    dve.wait_ge(s_scaled, i * 3 + (s + 1))
                    nc.vector.tensor_tensor(xin[s][:, :], xin[s][:, :], gb[:, 0, :],
                                            ALU.mult).then_inc(s_gained, 1)

                dve.wait_ge(s_gain, 16)
                with dve.Fori(0, NT // 3) as i:
                    for s in range(3):
                        stats(i, s)
                        centre(i, s)
                        gain(i, s)

            @block.scalar
            def _(act):
                def copy_out(i, s, half):
                    n = 2 * s + half
                    act.wait_ge(s_turned_half, i * 6 + (n + 1))
                    nc.scalar.copy(xT[:, 4 * half:4 * half + 4, bass.ds(i * (3 * P) + s * P, P)],
                                   bank[n][:, :].rearrange("p (k t) -> p k t", k=4)).then_inc(s_copied, 1)

                with act.Fori(0, NT // 3) as i:
                    for s in range(3):
                        act.wait_ge(s_sq, i * 12 + (4 * s + 4))
                        nc.scalar.activation(st[s][:, 15:16], st[s][:, 14:15], ACT.Sqrt).then_inc(s_std, 1)
                        act.wait_ge(s_nb, i * 6 + (2 * s + 2))
                        nc.scalar.activation(xin[s][:, :], xin[s][:, :], ACT.Identity,
                                             bias=st[s][:, 17:18], scale=st[s][:, 16:17]).then_inc(s_scaled, 1)
                        if s > 0:
                            for half in range(2):
                                copy_out(i, s - 1, half)
                    for half in range(2):
                        copy_out(i, 2, half)

            @block.tensor
            def _(pe):
                pe.wait_ge(s_ids, 1)
                pe.sem_inc(s_copied, 6)
                with pe.Fori(0, NT // 3) as i:
                    for s in range(3):
                        pe.wait_ge(s_normed, i * 3 + (s + 1))
                        for half in range(2):
                            n = 2 * s + half
                            pe.wait_ge(s_copied, i * 6 + (n + 1))
                            for k in range(4):
                                kk = 4 * half + k
                                last = nc.tensor.transpose(bank[n][:, k * P:(k + 1) * P],
                                                           xin[s][:, kk * P:(kk + 1) * P], ident[:, :])
                            last.then_inc(s_turned_half, 1)

        LINE = PBUF + NPR + BS * (PBUF + TS)

        def carve(at, *shape, names=""):
            n = math.prod(shape)
            return arena[:, at:at + n], at + n

        o = 0
        a_, o = carve(o, 2, TP)
        uT = a_.rearrange("p (m t) -> p m t", m=2)
        a_, o = carve(o, NPAIR, CH)
        U4 = a_.rearrange("p (q c) -> p q c", q=NPAIR)
        a_, o = carve(o, 2, LINE)
        line = a_.rearrange("p (m n) -> p m n", m=2)
        a_, o = carve(o, 2, NPAIR, CHP)
        Etab = a_.rearrange("p (r q c) -> p r q c", r=2, q=NPAIR)
        at_XS = o
        a_, o = carve(o, 2, NPAIR, CHP + 4)
        XS = a_.rearrange("p (r q c) -> p r q c", r=2, q=NPAIR)
        at_CA = o
        a_, o = carve(o, 2, NPAIR, (L + 1) * 32)
        CA = a_.rearrange("p (r q n) -> p r q n", r=2, q=NPAIR)
        a_, o = carve(o, NPAIR, 2, P)
        WT = a_.rearrange("p (q r n) -> p q r n", q=NPAIR, r=2)
        a_, o = carve(o, NPAIR, P)
        Tm = a_.rearrange("p (q n) -> p q n", q=NPAIR)
        assert o <= AR
        Wbd = arena[:, at_XS:at_XS + 2 * NPAIR * L * 32].rearrange("p (r q n) -> p r q n", r=2, q=NPAIR)
        prod = [arena[:, at_XS + 2048 + 640 * n:at_XS + 2048 + 640 * (n + 1)] for n in range(2)]
        vflat = v_tok[:, :, :].rearrange("p t n -> p (t n)")
        w_u = vflat[:, 0:KD * DS].rearrange("p (k n) -> p k n", k=KD)
        w_p = vflat[:, KD * DS:2 * KD * DS].rearrange("p (k n) -> p k n", k=KD)
        Sin = vflat[:, 0:2 * NPAIR * CH].rearrange("p (r q c) -> p r q c", r=2, q=NPAIR)
        mflat = mixT[:, 4:8, :].rearrange("p k t -> p (k t)")
        w_v = mixT[:, 0:4, :].rearrange("p k t -> p (k t)")[:, 0:KD * DA].rearrange("p (k n) -> p k n", k=KD)
        Zs = mflat[:, 0:2 * NPAIR * CHP].rearrange("p (r q c) -> p r q c", r=2, q=NPAIR)

        par = sb("par", [P, 40, NPAIR])
        pw = sb("pw", [P, 2, L + 1, NPAIR])
        wback = sb("wback", [P, 2, L, NPAIR])
        x0 = sb("x0", [P, 2, BS, NPAIR])
        finals = sb("finals", [P, 2, BS + 1, NPAIR])
        en = sb("en", [P, 6, NPAIR])
        Braw = sb("Braw", [P, 2, NPAIR, 16])
        Bbar = sb("Bbar", [P, 2, NPAIR, 16])
        Craw = sb("Craw", [P, 2, NPAIR, 16])
        dcol = sb("dcol", [P, NPAIR])

        with phase() as (mem, block):
            def tmp(name, shape):
                return mem.enter_context(nc.sbuf_tensor(name, shape, F32))
            w_f = tmp("w_f", [P, KD, H])
            bf = tmp("bf", [H, 1])
            lf = tmp("lf", [H, TP])
            stack1 = tmp("stack1", [16, P])
            ldt = tmp("ldt", [NPAIR, 2])
            ldtx = tmp("ldtx", [NPAIR, P])
            stack2 = tmp("stack2", [P, P])
            cstage = tmp("cstage", [P, 2, 2, SSMN])
            hist = tmp("hist", [BS * PBUF, DPL])
            lfT = tmp("lfT", [P, NT, H])

            s_ld = {n: sem("m_loaded_" + n) for n in
                    ("wf", "wu", "wp", "bf", "lre", "lim", "ldt", "xre", "xim", "bre", "bim", "cre", "cim",
                     "d0", "d1", "d2", "d3", "hist")}
            s_mm = sem("m_chunk_projected")
            s_tr = sem("m_param_turned")
            s_free = sem("m_bank_emptied")
            s_v = sem("m_vector_chain")
            s_a = sem("m_scalar_chain")
            s_par = sem("m_params_copied")
            s_x = sem("m_for_scalar")
            s_uT = sem("m_uT_rows")
            s_z = sem("m_forget_logits")
            s_lf = sem("m_log_gates")
            s_lft = sem("m_log_gates_turned")
            s_lfc = sem("m_log_gates_copied")
            s_o1 = sem("m_out_logf_a")
            s_o2 = sem("m_out_logf_b")
            s_o3 = sem("m_out_logf_c")
            s_o4 = sem("m_sums_parked")
            s_o5 = sem("m_negated_sums_parked")
            s_pm = sem("m_pool_cleared")
            s_cum = sem("m_cum_ready")

            w_in = A["w_in"][0].rearrange("(k p) n -> p k n", p=P)

            @block.sync
            def _(sp):
                def ld(key, dst, src):
                    sp.dma_start(dst, src).then_inc(s_ld[key], 16)
                ld("wf", w_f[:, :, :], w_in[:, :, O_F:O_F + H])
                ld("lre", stack1[0:8, :], A["ssm_lam_re"][0].rearrange("(q g) p -> q (g p)", g=2))
                ld("lim", stack1[8:16, :], A["ssm_lam_im"][0].rearrange("(q g) p -> q (g p)", g=2))
                ld("ldt", ldt[:, :], A["ssm_log_dt"][0].rearrange("(q g) -> q g", g=2))
                ld("xre", stack2[0:64, :], A["state_ssm_re"].rearrange("b l (q g) p -> (b l q) (g p)", g=2))
                ld("xim", stack2[64:128, :], A["state_ssm_im"].rearrange("b l (q g) p -> (b l q) (g p)", g=2))
                ld("bre", Braw[:, 0, :, :], A["ssm_b_re"][0].rearrange("(q g) p c -> (g p) q c", g=2))
                ld("bim", Braw[:, 1, :, :], A["ssm_b_im"][0].rearrange("(q g) p c -> (g p) q c", g=2))
                ld("cre", cstage[:, :, 0, :], A["ssm_c_re"][0].rearrange("(h g) c p -> (g c) h p", h=2))
                ld("cim", cstage[:, :, 1, :], A["ssm_c_im"][0].rearrange("(h g) c p -> (g c) h p", h=2))
                ld("wu", w_u, w_in[:, :, O_U:O_U + DS])
                ld("bf", bf[:, :], A["b_forget"][0].rearrange("(h a) -> h a", a=1))
                for j in range(L):
                    ld(f"d{j}", dcol[32 * j:32 * j + 32, :], A["ssm_d"][0].rearrange("(q r) -> r q", r=32))
                ld("hist", hist[:, :], A["state_pool"].rearrange("b l r c -> (b l r) c"))
                ld("wp", w_p, w_in[:, :, O_P:O_P + DPL])
                sp.wait_ge(s_lfc, 1)
                sp.dma_start(O["logf_prompt"][0, 0, 0:8 * P, :].rearrange("(t p) h -> p t h", p=P),
                             lfT[:, 0:8, :]).then_inc(s_o1, 16)
                sp.dma_start(O["logf_prompt"][0, 0, 8 * P:NPR, :], lfT[0:META, 8, :]).then_inc(s_o2, 16)
                sp.dma_start(O["logf_sample"].rearrange("b l t h -> (b l t) h"),
                             lfT[META:META + NSA, 8, :]).then_inc(s_o3, 16)
                sp.dma_start(gate_sums[0], cum[:, :]).then_inc(s_o4, 16)
                sp.dma_start(gate_sums[1], ncum[:, :]).then_inc(s_o5, 16)
                for s in (s_o1, s_o2, s_o3, s_o4, s_o5):
                    sp.wait_ge(s, 16)

            @block.tensor
            def _(pe):
                for k in ("lre", "lim"):
                    pe.wait_ge(s_ld[k], 16)
                nc.tensor.transpose(bank[4][:, 0:16], stack1[:, :], ident[0:16, 0:16])
                pe.wait_ge(s_v, 1)
                nc.tensor.transpose(bank[4][:, 16:24], ldtx[:, :], ident[0:8, 0:8]).then_inc(s_tr, 1)
                for k in ("xre", "xim"):
                    pe.wait_ge(s_ld[k], 16)
                nc.tensor.transpose(bank[6][:, 0:P], stack2[:, :], ident[:, :]).then_inc(s_tr, 1)
                for k in ("cre", "cim"):
                    pe.wait_ge(s_ld[k], 16)
                for n in range(4):
                    last = nc.tensor.transpose(bank[5][0:SSMN, n * P:(n + 1) * P], cstage[:, n // 2, n % 2, :],
                                               ident[:, :])
                last.then_inc(s_tr, 1)
                n = 0
                for key, w, m, cols in ([("wf", w_f, None, H)] + [("wu", w_u, m, P) for m in range(2)]
                                        + [("wp", w_p, m, P) for m in range(2)]):
                    pe.wait_ge(s_ld[key], 16)
                    for c0, cn in CHUNKS:
                        if 4 <= n < 7:
                            pe.wait_ge(s_z, n - 3)
                        elif n >= 7:
                            pe.wait_ge(s_free, n - 6)
                        for k in range(KD):
                            lhs = w[:, k, :] if m is None else w[:, k, m * P:(m + 1) * P]
                            last = nc.tensor.matmul(bank[n % 4][0:cols, 0:cn], lhs, xT[:, k, c0:c0 + cn],
                                                    start=(k == 0), stop=(k == KD - 1))
                        last.then_inc(s_mm, 1)
                        n += 1
                    if key == "wu" and m == 0:
                        pe.wait_ge(s_ld["hist"], 16)
                        for m2 in range(2):
                            last = nc.tensor.transpose(bank[7][:, m2 * P:m2 * P + BS * PBUF],
                                                       hist[:, m2 * P:(m2 + 1) * P],
                                                       ident[0:BS * PBUF, 0:BS * PBUF])
                        last.then_inc(s_tr, 1)
                pe.wait_ge(s_lf, 1)
                for t in range(NT):
                    last = nc.tensor.transpose(bank[7][:, t * H:(t + 1) * H], lf[:, t * P:(t + 1) * P],
                                               ident[0:H, 0:H])
                last.then_inc(s_lft, 1)

            @block.scalar
            def _(act):
                chain = Link(act, s_a)
                act.wait_ge(s_x, 1)
                chain(nc.scalar.activation(par[:, DT, :], par[:, LDT, :], ACT.Exp))
                act.wait_ge(s_x, 2)
                chain(nc.scalar.activation(par[:, MAG:MAG + 2, :], par[:, LRDT:LRDT + 2, :], ACT.Exp))
                act.wait_ge(s_x, 3)
                chain(nc.scalar.activation(par[:, COS:COS + 2, :], par[:, ANG:ANG + 2, :], ACT.Sin))
                act.wait_ge(s_z, 3)
                chain(nc.scalar.activation(ncum[:, :], lf[:, :], ACT.Abs))
                chain(nc.scalar.activation(ncum[:, :], ncum[:, :], ACT.Exp, scale=-1.0))
                chain(nc.scalar.activation(ncum[:, :], ncum[:, :], ACT.Ln, bias=1.0))
                for n in range(3, 15):
                    act.wait_ge(s_mm, n + 1)
                    m, (c0, cn) = (n - 3) // 3 % 2, CHUNKS[n % 3]
                    src = bank[n % 4]
                    if n < 9:
                        nc.scalar.copy(uT[:, m, c0:c0 + cn], src[:, 0:cn]).then_inc(s_free, 1)
                        continue
                    pn = min(cn, NPR - c0)
                    ins = nc.scalar.copy(line[:, m, PBUF + c0:PBUF + c0 + pn], src[:, 0:pn])
                    if c0 + cn > NPR:
                        ins = nc.scalar.copy(
                            line[:, m, PBUF + NPR:LINE].rearrange("p (b r) -> p b r", b=BS)[:, :, PBUF:PBUF + TS],
                            src[:, pn:pn + NSA].rearrange("p (b r) -> p b r", b=BS))
                    ins.then_inc(s_free, 1)

            @block.gpsimd
            def _(pool):
                nc.gpsimd.memset(Wbd, 0.0)
                nc.gpsimd.memset(CA, 0.0)
                nc.gpsimd.memset(Tm, 0.0)
                nc.gpsimd.memset(line[:, :, 0:PBUF], 0.0).then_inc(s_pm, 1)
                for m in range(2):
                    pool.wait_ge(s_free, 3 * (m + 1))
                    for q in range(4):
                        for j in range(L):
                            nc.gpsimd.tensor_copy(
                                U4[32 * j:32 * j + 32, 4 * m + q, :],
                                uT[32 * q:32 * q + 32, m, 0:TOK].rearrange("p (c j) -> p c j", j=L)[:, :, j])

            @block.vector
            def _(dve):
                V = nc.vector
                chain = Link(dve, s_v)

                def mul(o_, a, b, last=None):
                    chain(V.tensor_tensor(o_, a, b, ALU.mult))

                def p_(i, n=1):
                    return par[:, i, :] if n == 1 else par[:, i:i + n, :]

                def cmul(outr, outi, ar, ai, br, bi, t0, t1):
                    V.tensor_tensor(t0, ar, br, ALU.mult)
                    chain(V.tensor_tensor(t1, ai, bi, ALU.mult))
                    chain(V.tensor_tensor(outr, t0, t1, ALU.subtract))
                    V.tensor_tensor(t0, ar, bi, ALU.mult)
                    chain(V.tensor_tensor(t1, ai, br, ALU.mult))
                    chain(V.tensor_tensor(outi, t0, t1, ALU.add))

                dve.wait_ge(s_ld["ldt"], 16)
                chain(V.tensor_copy(ldtx[:, :].rearrange("q (g p) -> q g p", g=2),
                                    ldt[:, :].unsqueeze(2).to_broadcast([NPAIR, 2, SSMN])))
                dve.wait_ge(s_tr, 1)
                V.tensor_copy(par[:, LRE:LRE + 3, :], bank[4][:, 0:24].rearrange("p (a q) -> p a q", a=3)).then_inc(s_x, 1)
                dve.wait_ge(s_tr, 2)
                V.tensor_copy(x0[:, :, :, :].rearrange("p r b q -> p (r b q)"), bank[6][:, 0:P]).then_inc(s_par, 1)
                dve.wait_ge(s_tr, 3)
                for h in range(2):
                    for r in range(2):
                        n = 2 * h + r
                        for g in range(2):
                            ins = V.tensor_copy(
                                Craw[64 * g:64 * g + 64, r, 4 * h:4 * h + 4, :],
                                bank[5][0:SSMN, n * P:(n + 1) * P].rearrange("p (q g c) -> p q g c", q=4, g=2)[:, :, g, :])
                chain(ins)
                dve.wait_ge(s_a, 1)
                mul(p_(LRDT), p_(LRE), p_(DT))
                V.tensor_scalar(p_(LRDT4), p_(LRDT), float(L), None, ALU.mult).then_inc(s_x, 1)
                mul(p_(SIN0), p_(LIM), p_(DT))
                chain(V.tensor_scalar(p_(COS0), p_(SIN0), math.pi / 2, None, ALU.add))
                V.tensor_scalar(p_(KT, 2), p_(COS0, 2), 1.0 / (2 * math.pi), ROUND, ALU.mult, ALU.add)
                chain(V.tensor_copy(p_(ANG, 2), p_(COS0, 2)))
                chain(V.tensor_scalar(p_(KT, 2), p_(KT, 2), ROUND, None, ALU.subtract))
                chain(V.scalar_tensor_tensor(p_(ANG, 2), p_(KT, 2), -TURN_HI, p_(ANG, 2), ALU.mult, ALU.add))
                chain(V.scalar_tensor_tensor(p_(ANG, 2), p_(KT, 2), -TURN_LO, p_(ANG, 2), ALU.mult, ALU.add))
                V.tensor_scalar(p_(ANG, 2), p_(ANG, 2), PI_IN, -PI_IN, ALU.min, ALU.max).then_inc(s_x, 1)
                V.memset(pw[:, 0, 0, :], 1.0)
                V.memset(Etab[:, 0, :, 0:1], 1.0)
                V.memset(Etab[:, 1, :, 0:1], 0.0)
                chain(V.memset(pw[:, 1, 0, :], 0.0))
                dve.wait_ge(s_a, 3)
                V.tensor_tensor(pw[:, 0, 1, :], p_(MAG), p_(COS), ALU.mult)
                mul(pw[:, 1, 1, :], p_(MAG), p_(SIN))
                for k in range(2, L + 1):
                    cmul(pw[:, 0, k, :], pw[:, 1, k, :], pw[:, 0, k - 1, :], pw[:, 1, k - 1, :],
                         pw[:, 0, 1, :], pw[:, 1, 1, :], p_(T0), p_(T1))
                for j in range(L):
                    ins = V.tensor_copy(wback[:, :, j, :], pw[:, :, L - 1 - j, :])
                chain(ins)
                V.tensor_scalar(p_(NR), pw[:, 0, 1, :], -1.0, None, ALU.add)
                V.tensor_tensor(p_(T0), p_(LRE), p_(LRE), ALU.mult)
                mul(p_(T1), p_(LIM), p_(LIM))
                chain(V.tensor_tensor(p_(T0), p_(T0), p_(T1), ALU.add))
                chain(V.reciprocal(p_(DEN), p_(T0)))
                V.tensor_tensor(p_(T0), p_(NR), p_(LRE), ALU.mult)
                mul(p_(T1), pw[:, 1, 1, :], p_(LIM))
                chain(V.tensor_tensor(p_(GR), p_(T0), p_(T1), ALU.add))
                V.tensor_tensor(p_(T0), pw[:, 1, 1, :], p_(LRE), ALU.mult)
                mul(p_(T1), p_(NR), p_(LIM))
                chain(V.tensor_tensor(p_(GI), p_(T0), p_(T1), ALU.subtract))
                V.tensor_tensor(p_(GR), p_(GR), p_(DEN), ALU.mult)
                mul(p_(GI), p_(GI), p_(DEN))
                for k in ("bre", "bim"):
                    dve.wait_ge(s_ld[k], 16)

                def over_c(x, *shape):
                    return x.unsqueeze(2).to_broadcast([P, NPAIR, 16])

                pr = [t[:, 0:NPAIR * 16].rearrange("p (q c) -> p q c", q=NPAIR) for t in prod]
                cmul(Bbar[:, 0, :, :], Bbar[:, 1, :, :], over_c(p_(GR)), over_c(p_(GI)),
                     Braw[:, 0, :, :], Braw[:, 1, :, :], pr[0], pr[1])
                dve.wait_ge(s_pm, 1)
                for (powers, nk, base, dst, sign_im) in ((wback, L, Bbar, Wbd, 1), (pw, L + 1, Craw, CA, -1)):
                    pr = [t[:, 0:NPAIR * nk * 16].rearrange("p (q k c) -> p q k c", q=NPAIR, k=nk) for t in prod]

                    def power(r):
                        x = powers[:, r, :, :].rearrange("p k q -> p q k")
                        return x.unsqueeze(3).to_broadcast([P, NPAIR, nk, 16])

                    def per_c(r):
                        return base[:, r, :, :].unsqueeze(2).to_broadcast([P, NPAIR, nk, 16])

                    for r in range(2):
                        V.tensor_tensor(pr[0], power(0), per_c(r), ALU.mult)
                        chain(V.tensor_tensor(pr[1], power(1), per_c(1 - r), ALU.mult))
                        if r == 1 and sign_im < 0:
                            chain(V.tensor_scalar(pr[0], pr[0], -1.0, None, ALU.mult))
                        for g in range(2):
                            sl = slice(64 * g, 64 * g + 64)
                            out = dst[:, r, :, :].rearrange("p q (k n) -> p q k n", k=nk)
                            ins = V.tensor_tensor(out[sl, :, :, 16 * g:16 * g + 16], pr[0][sl], pr[1][sl],
                                                  ALU.add if r == 1 and sign_im > 0 else ALU.subtract)
                        chain(ins)
                dve.wait_ge(s_ld["bf"], 16)
                for n, (c0, cn) in enumerate(CHUNKS):
                    dve.wait_ge(s_mm, n + 1)
                    V.tensor_scalar(lf[:, c0:c0 + cn], bank[n][0:H, 0:cn], bf[:, 0:1], None, ALU.add).then_inc(s_z, 1)
                cmul(en[:, 0, :], en[:, 1, :], p_(COS), p_(SIN), p_(COS), p_(SIN), en[:, 4, :], en[:, 5, :])
                cmul(en[:, 2, :], en[:, 3, :], en[:, 0, :], en[:, 1, :], en[:, 0, :], en[:, 1, :],
                     en[:, 4, :], en[:, 5, :])
                n, cur = 1, 2
                while n < CHP:
                    m = min(n, CHP - n)
                    cr = en[:, cur, :].unsqueeze(2).to_broadcast([P, NPAIR, m])
                    ci = en[:, cur + 1, :].unsqueeze(2).to_broadcast([P, NPAIR, m])
                    sc = [Zs[:, r, :, 0:m] for r in range(2)]
                    cmul(Etab[:, 0, :, n:n + m], Etab[:, 1, :, n:n + m], Etab[:, 0, :, 0:m], Etab[:, 1, :, 0:m],
                         cr, ci, sc[0], sc[1])
                    nxt = 2 - cur
                    cmul(en[:, nxt, :], en[:, nxt + 1, :], en[:, cur, :], en[:, cur + 1, :],
                         en[:, cur, :], en[:, cur + 1, :], en[:, 4, :], en[:, 5, :])
                    n, cur = n + m, nxt
                dve.wait_ge(s_tr, 4)
                for m in range(2):
                    ins = V.tensor_copy(
                        line[:, m, PBUF + NPR:LINE].rearrange("p (b r) -> p b r", b=BS)[:, :, 0:PBUF],
                        bank[7][:, m * P:m * P + BS * PBUF].rearrange("p (b r) -> p b r", b=BS))
                dve.wait_ge(s_a, 6)
                V.scalar_tensor_tensor(lf[:, :], lf[:, :], 0.0, ncum[:, :], ALU.min, ALU.subtract).then_inc(s_lf, 1)
                dve.wait_ge(s_lf, 1)
                V.tensor_copy(cum[:, NPR:TP], lf[:, NPR:TP])
                V.tensor_tensor_scan(cum[:, 0:NPR], ones_col[0:H, :].to_broadcast([H, NPR]), lf[:, 0:NPR],
                                     0.0, ALU.mult, ALU.add).then_inc(s_cum, 1)
                dve.wait_ge(s_cum, 1)
                V.tensor_scalar(ncum[:, 0:NPR], cum[:, 0:NPR], -1.0, None, ALU.mult)
                dve.wait_ge(s_lft, 1)
                V.tensor_copy(lfT[:, :, :], bank[7][:, 0:NT * H].rearrange("p (t h) -> p t h", t=NT)).then_inc(s_lfc, 1)

        XI = sb("XI", [P, 2, NPAIR, CHS])

        with phase() as (mem, block):
            fin_t = mem.enter_context(nc.sbuf_tensor("fin_t", [(BS + 1) * NPAIR, 2, P], F32))
            s_wv = sem("s_values_weights")
            s_wt = sem("s_W_turned")
            s_wc = sem("s_W_copied")
            s_tb = sem("s_T_built")
            s_tc = sem("s_T_ready")
            s_in = sem("s_inputs_summed")
            s_ic = sem("s_inputs_copied")
            s_v = sem("s_vector_chain")
            s_xs = sem("s_states_ready")
            s_fi = sem("s_finals_ready")
            s_y = sem("s_outputs_summed")
            s_ge = sem("s_gelu_done")
            s_ft = sem("s_finals_turned")
            s_fc = sem("s_finals_copied")
            s_o = [sem(f"s_out_state{n}") for n in range(4)]

            @block.sync
            def _(sp):
                sp.dma_start(w_v, A["w_in"][0].rearrange("(k p) n -> p k n", p=P)[:, :, 2 * DA:3 * DA]).then_inc(s_wv, 16)
                sp.wait_ge(s_fc, 1)
                for r, nm in enumerate(("re", "im")):
                    sp.dma_start(O[f"ssm_{nm}_prompt"][0, 0].rearrange("(q g) p -> q (g p)", g=2),
                                 fin_t[0:NPAIR, r, :]).then_inc(s_o[r], 16)
                    sp.dma_start(O[f"ssm_{nm}_sample"].rearrange("b l (q g) p -> (b l q) (g p)", g=2),
                                 fin_t[NPAIR:(BS + 1) * NPAIR, r, :]).then_inc(s_o[2 + r], 16)
                for s in s_o:
                    sp.wait_ge(s, 16)
                sp.wait_ge(s_wv, 16)

            @block.tensor
            def _(pe):
                for q in range(NPAIR):
                    for r in range(2):
                        last = nc.tensor.transpose(bank[q // 2][:, (2 * (q % 2) + r) * P:(2 * (q % 2) + r + 1) * P],
                                                   Wbd[:, r, q, :], ident[:, :])
                    if q % 2:
                        last.then_inc(s_wt, 1)
                for q in range(NPAIR):
                    for j in range(L):
                        for r in range(2):
                            last = nc.tensor.matmul(
                                bank[4 + q // 4][32 * j:32 * j + 32, (q % 4) * P + 32 * j:(q % 4 + 1) * P],
                                Wbd[:, r, q, 32 * (L - 1):32 * L], CA[:, r, q, 0:32 * (L - j)],
                                start=(r == 0), stop=(r == 1))
                last.then_inc(s_tb, 1)
                for n in range(2 * NPAIR):
                    q, r = n // 2, n % 2
                    pe.wait_ge(s_wc, q // 2 + 1)
                    if n < 4:
                        pe.wait_ge(s_wc, n + 1)
                    if n >= 4:
                        pe.wait_ge(s_ic, n - 3)
                    nc.tensor.matmul(bank[n % 4][:, 0:CH], WT[:, q, r, :], U4[:, q, :],
                                     start=True, stop=True).then_inc(s_in, 1)
                pe.wait_ge(s_tc, 1)
                for q in range(NPAIR):
                    b = bank[4 + q % 4]
                    if q >= 4:
                        pe.wait_ge(s_ge, q - 3)
                    nc.tensor.matmul(b[:, 0:CH], Tm[:, q, :], U4[:, q, :], start=True, stop=False)
                    if q == 0:
                        pe.wait_ge(s_xs, 1)
                    for r in range(2):
                        lhs = CA[:, r, q, 32:32 * (L + 1)]
                        nc.tensor.matmul(b[:, 0:CHP], lhs, XS[:, r, q, 0:CHP], start=False, stop=False)
                        last = nc.tensor.matmul(b[:, CHP:CH], lhs, XI[:, r, q, :], start=False, stop=(r == 1))
                    last.then_inc(s_y, 1)
                pe.wait_ge(s_ic, 2 * NPAIR)
                pe.wait_ge(s_fi, 1)
                for r in range(2):
                    last = nc.tensor.transpose(bank[0][0:(BS + 1) * NPAIR, r * P:(r + 1) * P],
                                               finals[:, r, :, :].rearrange("p b q -> p (b q)"), ident[:, :])
                last.then_inc(s_ft, 1)

            @block.scalar
            def _(act):
                for b in range(4):
                    act.wait_ge(s_wt, b + 1)
                    nc.scalar.copy(WT[:, 2 * b:2 * b + 2, :, :].rearrange("p q r n -> p (q r n)"),
                                   bank[b][:, :]).then_inc(s_wc, 1)
                for n in range(2 * NPAIR):
                    act.wait_ge(s_in, n + 1)
                    nc.scalar.copy(Sin[:, n % 2, n // 2, :], bank[n % 4][:, 0:CH]).then_inc(s_ic, 1)
                for q in range(NPAIR):
                    act.wait_ge(s_y, q + 1)
                    for i in range(L):
                        rows = uT[32 * (q % 4):32 * (q % 4) + 32, q // 4, 0:TOK].rearrange("p (c j) -> p c j", j=L)
                        last = nc.scalar.activation(rows[:, :, i], bank[4 + q % 4][32 * i:32 * i + 32, 0:CH],
                                                    ACT.Gelu_apprx_tanh)
                    last.then_inc(s_ge, 1)

            @block.vector
            def _(dve):
                V = nc.vector
                chain = Link(dve, s_v)
                dve.wait_ge(s_tb, 1)
                for h in range(2):
                    for j in range(L):
                        sl = slice(32 * j, 32 * j + 32)
                        last = V.tensor_copy(Tm[sl, 4 * h:4 * h + 4, 32 * j:P],
                                             bank[4 + h][sl, :].rearrange("p (q n) -> p q n", q=4)[:, :, 32 * j:P])
                chain(last)
                for q in range(NPAIR):
                    last = V.scalar_tensor_tensor(Tm[:, q, :], ident[:, :], dcol[:, q:q + 1], Tm[:, q, :],
                                                  ALU.mult, ALU.add)
                last.then_inc(s_tc, 1)
                dve.wait_ge(s_ic, 2 * NPAIR)
                c_, s_ = Etab[:, 0, :, :], Etab[:, 1, :, :]
                S_ = [Sin[:, r, :, 0:CHP] for r in range(2)]
                Z_ = [Zs[:, r, :, :] for r in range(2)]
                X_ = [XS[:, r, :, 0:CHP] for r in range(2)]
                Ss = [Sin[:, r, :, CHP:CH].rearrange("p q (b h) -> p q b h", h=2) for r in range(2)]
                Xi = [XI[:, r, :, :].rearrange("p q (b h) -> p q b h", h=2) for r in range(2)]
                xq = [x0[:, r, :, :].rearrange("p b q -> p q b") for r in range(2)]
                fq = [finals[:, r, 1:BS + 1, :].rearrange("p b q -> p q b") for r in range(2)]
                A4 = [pw[:, r, L, :].unsqueeze(2).to_broadcast([P, NPAIR, BS]) for r in range(2)]
                t_ = [par[:, 22 + 8 * r:30 + 8 * r, :] for r in range(2)]
                for r in range(2):
                    V.tensor_copy(Xi[r][:, :, :, 0], xq[r])
                for h, xin_, xout in ((0, xq, [Xi[r][:, :, :, 1] for r in range(2)]),
                                      (1, [Xi[r][:, :, :, 1] for r in range(2)], fq)):
                    for r in range(2):
                        V.tensor_tensor(t_[0], A4[0], xin_[r], ALU.mult)
                        chain(V.tensor_tensor(t_[1], A4[1], xin_[1 - r], ALU.mult))
                        chain(V.tensor_tensor(t_[0], t_[0], t_[1], ALU.subtract if r == 0 else ALU.add))
                        chain(V.tensor_tensor(xout[r], t_[0], Ss[r][:, :, :, h], ALU.add))
                V.tensor_tensor(Z_[0], c_, S_[0], ALU.mult)
                V.tensor_tensor(X_[0], s_, S_[1], ALU.mult)
                V.tensor_tensor(Z_[1], c_, S_[1], ALU.mult)
                chain(V.tensor_tensor(X_[1], s_, S_[0], ALU.mult))
                V.tensor_tensor(Z_[0], Z_[0], X_[0], ALU.add)
                chain(V.tensor_tensor(Z_[1], Z_[1], X_[1], ALU.subtract))
                for r in range(2):
                    for q in range(NPAIR):
                        last = V.tensor_tensor_scan(Sin[:, r, q, 0:CHP],
                                                    par[:, MAG4, q:q + 1].to_broadcast([P, CHP]),
                                                    Zs[:, r, q, :], 0.0, ALU.mult, ALU.add)
                chain(last)
                Xn = [XS[:, r, :, 1:CHP + 1] for r in range(2)]
                V.memset(XS[:, :, :, 0:1], 0.0)
                V.tensor_tensor(Xn[0], c_, S_[0], ALU.mult)
                V.tensor_tensor(Z_[0], s_, S_[1], ALU.mult)
                V.tensor_tensor(Xn[1], c_, S_[1], ALU.mult)
                chain(V.tensor_tensor(Z_[1], s_, S_[0], ALU.mult))
                V.tensor_tensor(Xn[0], Xn[0], Z_[0], ALU.subtract)
                V.tensor_tensor(Xn[1], Xn[1], Z_[1], ALU.add).then_inc(s_xs, 1)
                dve.wait_ge(s_xs, 1)
                for r in range(2):
                    last = V.tensor_copy(finals[:, r, 0, :], XS[:, r, :, CHP])
                last.then_inc(s_fi, 1)
                dve.wait_ge(s_ft, 1)
                V.tensor_copy(fin_t[:, :, :].rearrange("p r n -> p (r n)"),
                              bank[0][0:(BS + 1) * NPAIR, 0:2 * P]).then_inc(s_fc, 1)

        with phase() as (mem, block):
            def tmp(name, shape):
                return mem.enter_context(nc.sbuf_tensor(name, shape, F32))
            la = arena[:, at_CA:at_CA + LINE]
            lb = arena[:, at_XS:at_XS + LINE]
            pooled = Etab.rearrange("p r q c -> p (r q c)")[:, 0:2 * TOK].rearrange("p (m t) -> p m t", m=2)
            at_w = at_CA + 2 * NPAIR * (L + 1) * 32 + P
            w_g = arena[:, at_w:at_w + 2 * DS].rearrange("p (m n) -> p m n", m=2)
            bg = tmp("bg", [P, 2])
            w_pl = tmp("w_pl", [P, 2, P])
            spc = tmp("spc", [P, 2])
            gate = [tmp(f"gate{n}", [P, 384]) for n in range(2)]
            fix = tmp("fix", [P, 2, PBUF])
            prow = tmp("prow", [NSA, 2, P])
            prowp = tmp("prowp", [PBUF, 2, P])

            s_ld = {n: sem("r_loaded_" + n) for n in ("wg", "bg", "p0", "p1", "p2", "p3", "sp")}
            at_WT = at_CA + 2 * NPAIR * (L + 1) * 32
            plast = arena[:, at_WT:at_WT + 2 * NSA].rearrange("p (m n) -> p m n", m=2)
            s_pl = sem("r_sample_rows_packed")
            s_pz = sem("r_pool_weights_cleared")
            s_vm = sem("r_values_projected")
            s_vc = sem("r_values_copied")
            s_vo = [sem(f"r_out_values{n}") for n in range(2)]
            s_gm = sem("r_gate_projected")
            s_gs = sem("r_gate_ready")
            s_gd = sem("r_gate_used")
            s_v = sem("r_vector_chain")
            s_g = sem("r_pool_chain")
            s_pd = sem("r_pooled_ready")
            s_pm = sem("r_pool_projected")
            s_pc = sem("r_pool_copied")
            s_pt = sem("r_pool_rows_turned")
            s_pr = sem("r_pool_rows_copied")
            s_o = [sem(f"r_out_pool{n}") for n in range(3)]

            @block.sync
            def _(sp):
                sp.dma_start(w_g, A["w_glu"][0].rearrange("(k p) n -> p k n", p=P)).then_inc(s_ld["wg"], 16)
                sp.dma_start(bg[:, :], A["b_glu"][0].rearrange("(m p) -> p m", p=P)).then_inc(s_ld["bg"], 16)
                sp.dma_start(spc[:, :], A["s_pool"][0].rearrange("(m p) -> p m", p=P)).then_inc(s_ld["sp"], 16)
                sp.wait_ge(s_pz, 1)
                for g in range(4):
                    h = 64 * (g % 2)
                    sp.dma_start(w_pl[h:h + 64, g // 2, h:h + 64], A["w_pool"][0, g]).then_inc(s_ld[f"p{g}"], 16)
                sp.dma_start(O["pool_sample"][:, 0, 0:PBUF - TS, :], A["state_pool"][:, 0, TS:PBUF, :]).then_inc(s_o[0], 16)
                sp.wait_ge(s_pr, 1)
                sp.dma_start(O["pool_prompt"][0, 0], prowp[:, :, :].rearrange("t m c -> t (m c)")).then_inc(s_o[1], 16)
                sp.dma_start(O["pool_sample"][:, 0, PBUF - TS:PBUF, :],
                             prow[:, :, :].rearrange("t m c -> t (m c)")).then_inc(s_o[2], 16)
                sp.wait_ge(s_vc, 2 * NT)
                sp.dma_start(O["v_prompt"][0, 0, 0:8 * P].rearrange("(t p) h d -> p t (h d)", p=P),
                             v_tok[:, 0:8, :]).then_inc(s_vo[0], 16)
                sp.dma_start(O["v_prompt"][0, 0, 8 * P:NPR].rearrange("t h d -> t (h d)"),
                             v_tok[0:META, 8, :]).then_inc(s_o[1], 16)
                sp.dma_start(O["v_sample"].rearrange("b l t h d -> (b l t) (h d)"),
                             v_tok[META:META + NSA, 8, :]).then_inc(s_vo[1], 16)
                sp.wait_ge(s_o[0], 16)
                sp.wait_ge(s_o[1], 32)
                sp.wait_ge(s_o[2], 16)
                for s in s_vo:
                    sp.wait_ge(s, 16)

            @block.tensor
            def _(pe):
                def values(t):
                    if t >= 4:
                        pe.wait_ge(s_vc, 2 * (t - 3))
                    for k in range(KD):
                        last = nc.tensor.matmul(bank[t % 4][:, :], xT[:, k, t * P:(t + 1) * P], w_v[:, k, :],
                                                start=(k == 0), stop=(k == KD - 1))
                    last.then_inc(s_vm, 1)

                pe.wait_ge(s_pl, 1)
                for m in range(2):
                    nc.tensor.transpose(bank[6][0:PBUF, m * P:(m + 1) * P], line[:, m, NPR:NPR + PBUF], ident[:, :])
                    last = nc.tensor.transpose(
                        bank[7][0:NSA, m * P:(m + 1) * P], plast[:, m, :], ident[:, :])
                last.then_inc(s_pt, 1)
                for t in range(3):
                    values(t)
                pe.wait_ge(s_ld["wg"], 16)
                n = 0
                for m in range(2):
                    for c0, cn in CHUNKS_T:
                        if n >= 2:
                            pe.wait_ge(s_gs, n - 1)
                        for k in range(2):
                            last = nc.tensor.matmul(bank[4 + n % 2][:, 0:cn], w_g[:, k, m * P:(m + 1) * P],
                                                    uT[:, k, c0:c0 + cn], start=(k == 0), stop=(k == 1))
                        last.then_inc(s_gm, 1)
                        n += 1
                    values(3 + m)
                for t in range(5, NT):
                    values(t)
                for g in range(4):
                    pe.wait_ge(s_ld[f"p{g}"], 16)
                pe.wait_ge(s_pd, 1)
                pe.wait_ge(s_pr, 1)
                n = 0
                for m in range(2):
                    for c0, cn in CHUNKS_T:
                        if n >= 2:
                            pe.wait_ge(s_pc, n - 1)
                        nc.tensor.matmul(bank[6 + n % 2][:, 0:cn], w_pl[:, m, :], pooled[:, m, c0:c0 + cn],
                                         start=True, stop=True).then_inc(s_pm, 1)
                        n += 1

            @block.scalar
            def _(act):
                def values(t):
                    act.wait_ge(s_vm, t + 1)
                    nc.scalar.copy(v_tok[:, t, :], bank[t % 4][:, :]).then_inc(s_vc, 2)
                for t in range(3):
                    values(t)
                act.wait_ge(s_ld["bg"], 16)
                n = 0
                for m in range(2):
                    for c0, cn in CHUNKS_T:
                        act.wait_ge(s_gm, n + 1)
                        if n >= 2:
                            act.wait_ge(s_gd, n - 1)
                        nc.scalar.activation(gate[n % 2][:, 0:cn], bank[4 + n % 2][:, 0:cn], ACT.Sigmoid,
                                             bias=bg[:, m:m + 1]).then_inc(s_gs, 1)
                        n += 1
                    values(3 + m)
                for t in range(5, NT):
                    values(t)
                act.wait_ge(s_ld["sp"], 16)
                n = 0
                for m in range(2):
                    for c0, cn in CHUNKS_T:
                        act.wait_ge(s_pm, n + 1)
                        nc.scalar.activation(mixT[:, 6 + m, c0:c0 + cn], bank[6 + n % 2][:, 0:cn], ACT.Copy,
                                             scale=spc[:, m:m + 1]).then_inc(s_pc, 1)
                        n += 1

            @block.gpsimd
            def _(pool):
                G = nc.gpsimd
                chain = Link(pool, s_g)
                G.memset(w_pl[:, :, :], 0.0).then_inc(s_pz, 1)
                G.memset(mixT[:, 4:8, TOK:TP], 0.0)
                chain(G.iota(fix[:, :, :], [[0, 2], [1, PBUF]], base=1, channel_multiplier=0,
                             allow_small_or_imprecise_dtypes=True))
                for g, w in enumerate((2, 4, 8, 16)):
                    f = fix[64 * (g % 2):64 * (g % 2) + 64, g // 2, :]
                    last = G.tensor_scalar(f, f, float(w), None, ALU.min)
                chain(last)

            @block.vector
            def _(dve):
                V = nc.vector
                chain = Link(dve, s_v)
                for m in range(2):
                    last = V.tensor_copy(
                        plast[:, m, :].rearrange("p (b r) -> p b r", b=BS),
                        line[:, m, PBUF + NPR:LINE].rearrange("p (b r) -> p b r", b=BS)[:, :, PBUF:PBUF + TS])
                last.then_inc(s_pl, 1)
                dve.wait_ge(s_pt, 1)
                V.tensor_copy(prowp[:, :, :].rearrange("t m c -> t (m c)"), bank[6][0:PBUF, 0:2 * P])
                V.tensor_copy(prow[:, :, :].rearrange("t m c -> t (m c)"), bank[7][0:NSA, 0:2 * P]).then_inc(s_pr, 1)
                dve.wait_ge(s_g, 2)
                chain(V.reciprocal(fix[:, :, :], fix[:, :, :]))
                for g, w in enumerate((2, 4, 8, 16)):
                    f = fix[64 * (g % 2):64 * (g % 2) + 64, g // 2, :]
                    last = V.tensor_scalar(f, f, float(w), None, ALU.mult)
                chain(last)

                def shifted(o_, i_, s, rows=slice(0, P)):
                    V.tensor_copy(o_[rows, 0:s], i_[rows, 0:s])
                    chain(V.tensor_tensor(o_[rows, s:LINE], i_[rows, s:LINE], i_[rows, 0:LINE - s], ALU.add))

                def average(m, half, sums, w):
                    r = slice(64 * half, 64 * half + 64)
                    chain(V.tensor_tensor(sums[r, PBUF:2 * PBUF], sums[r, PBUF:2 * PBUF], fix[r, m, :], ALU.mult))
                    V.scalar_tensor_tensor(pooled[r, m, 0:NPR], sums[r, PBUF:PBUF + NPR], 1.0 / w,
                                           line[r, m, PBUF:PBUF + NPR], ALU.mult, ALU.subtract)

                    def new(x):
                        return x.rearrange("p (b r) -> p b r", b=BS)[:, :, PBUF:PBUF + TS]
                    return V.scalar_tensor_tensor(
                        pooled[r, m, NPR:TOK].rearrange("p (b r) -> p b r", b=BS), new(sums[r, PBUF + NPR:LINE]),
                        1.0 / w, new(line[r, m, PBUF + NPR:LINE]), ALU.mult, ALU.subtract)

                def gates(n):
                    m, (c0, cn) = n // 3, CHUNKS_T[n % 3]
                    dve.wait_ge(s_gs, n + 1)
                    V.tensor_tensor(mixT[:, 4 + m, c0:c0 + cn], gate[n % 2][:, 0:cn], uT[:, m, c0:c0 + cn],
                                    ALU.mult).then_inc(s_gd, 1)

                shifted(la, line[:, 0, :], 1)
                shifted(lb, la, 2)
                average(0, 0, la, 2)
                chain(average(0, 1, lb, 4))
                gates(0)
                gates(1)
                shifted(la, line[:, 1, :], 1)
                shifted(lb, la, 2)
                gates(2)
                gates(3)
                shifted(la, lb, 4)
                shifted(lb, la, 8, slice(64, P))
                average(1, 0, la, 8)
                average(1, 1, lb, 16).then_inc(s_pd, 1)
                gates(4)
                gates(5)

        W_O_AT = AR - KD * D
        w_o = arena[:, W_O_AT:AR].rearrange("p (k n) -> p k n", k=KD)
        with phase() as (mem, block):
            o = 0
            a_, o = carve(o, 2, TP)
            qb = a_.rearrange("p (h t) -> p h t", h=2)
            a_, o = carve(o, 2, TP)
            kb = a_.rearrange("p (h t) -> p h t", h=2)
            pbuf = []
            for _n in range(2):
                a_, o = carve(o, NPR)
                pbuf.append(a_)
            pt = []
            for _n in range(2):
                a_, o = carve(o, 4, P)
                pt.append(a_)
            a_, o = carve(o, KD, P)
            wk_s = a_.rearrange("p (k n) -> p k n", k=KD)
            a_, o = carve(o, KD, P)
            wq_s = a_.rearrange("p (k n) -> p k n", k=KD)
            a_, o = carve(o, NT, P)
            att = a_.rearrange("p (t n) -> p t n", t=NT)
            a_, o = carve(o, NT, P)
            k_tok = a_.rearrange("p (t n) -> p t n", t=NT)
            a_, o = carve(o, 4, 2 * NT)
            sm = a_.rearrange("p (r n) -> p r n", r=4)
            a_, o = carve(o, 2, 2)
            sm2 = a_.rearrange("p (r n) -> p r n", r=2)
            a_, o = carve(o, META)
            ptail = a_
            assert o <= W_O_AT

            NST, QT = 2 * NT, NT
            steps = [(h, i) for h in range(2) for i in range(QT)]
            groups = [(n, g) for n, (h, i) in enumerate(steps) for g in range(i // 4 + 1)]
            NG = len(groups)
            upto = [sum(1 for m, _ in groups if m <= n) for n in range(NST)]

            def nq(i):
                return min(P, NPR - i * P)

            def blocks(n, g):
                return range(4 * g, min(4 * g + 4, steps[n][1] + 1))

            s_w = {k: sem("a_weights_" + k) for k in "kq"}
            s_pj = sem("a_projected")
            s_kev = sem("a_k_rows_ready")
            s_qev = sem("a_q_rows_ready")
            s_rw = [sem(f"a_gate_rows{n}") for n in range(2)]
            s_zero = sem("a_zero_rows")
            s_one = sem("a_ones_rows")
            s_round = sem("a_keys_out")
            s_tail = sem("a_tail_cleared")
            s_fill = [sem(f"a_unused_rows_filled{n}") for n in range(2)]
            s_wo = [sem(f"a_out_weights{n}") for n in range(2)]
            s_hold = sem("a_waits_held")
            s_ktt = sem("a_k_turned")
            s_ktA = sem("a_k_tok_by_scalar")
            s_ktD = sem("a_k_tok_by_vector")
            s_ko = [sem(f"a_out_k{n}") for n in range(3)]
            s_S = sem("a_scores")
            s_mx = sem("a_maxima")
            s_mp = sem("a_max_parts")
            s_ex = sem("a_exponentials")
            s_T = sem("a_turned")
            s_E = [sem("a_turned_copied_by_vector"), sem("a_turned_copied_by_scalar")]
            s_PV = sem("a_weighted")
            s_rc = sem("a_inverse_sums")
            s_att = sem("a_outputs")
            s_at = sem("a_outputs_turned")
            s_aeA = sem("a_mix_by_scalar")
            s_aeD = sem("a_mix_by_vector")

            w_in = A["w_in"][0].rearrange("(k p) n -> p k n", p=P)
            score = [(0, 1), (2, 3)]

            def pieces(n):
                nk = min((steps[n][1] + 1) * P, NPR)
                out = [(score[n % 2][c], 512 * c, min(512, nk - 512 * c)) for c in range(2) if nk > 512 * c]
                return out + ([(6 + n % 2, 1024, NPR - 1024)] if nk > 1024 else [])

            @block.gpsimd
            def _(pool):
                G = nc.gpsimd
                G.memset(mixT[:, 0:4, TOK:TP], 0.0)
                G.memset(ptail, 0.0).then_inc(s_tail, 1)
                pool.dma_start(wk_s, w_in[:, :, DA:DA + P]).then_inc(s_w["k"], 16)
                pool.dma_start(wq_s, w_in[:, :, 0:P]).then_inc(s_w["q"], 16)
                with pool.Fori(0, 3) as i:
                    pool.wait_ge(s_pj, i * 6 + 6)
                    pool.dma_start(wk_s, w_in[:, :, bass.ds(i * P + (DA + P), P)]).then_inc(s_w["k"], 16)
                    pool.dma_start(wq_s, w_in[:, :, bass.ds(i * P + P, P)]).then_inc(s_w["q"], 16)

            @block.sync
            def _(sp):
                sp.wait_ge(s_pj, 1)
                fill = xT[:, :, :].rearrange("p k t -> p (k t)")[:, 0:8 * D].rearrange("p (s d) -> p s d", s=8)
                for n in range(2):
                    t0, t1 = LEAST + 8 * n, min(LEAST + 8 * n + 8, SLOTT)
                    sp.dma_start(y_park[t0 * P:t1 * P, :].rearrange("(s p) d -> p s d", p=P),
                                 fill[:, 0:t1 - t0, :]).then_inc(s_fill[n], 16)
                wo = A["w_out"][0].rearrange("(k p) n -> p k n", p=P)
                for n in range(2):
                    sp.dma_start(w_o[:, 4 * n:4 * n + 4, :], wo[:, 4 * n:4 * n + 4, :]).then_inc(s_wo[n], 16)
                sp.wait_ge(s_one, 1)
                kp = O["k_prompt"][0, 0].rearrange("t h d -> t (h d)")
                ks = O["k_sample"].rearrange("b l t h d -> (b l t) (h d)")
                with sp.Fori(0, 4) as i:
                    sp.wait_ge(s_pj, i * 6 + 6)
                    sp.sem_inc(s_round, 1)
                    sp.dma_start(qb[65:66, :, :], gate_sums[0:1, bass.ds(i * 2, 2), :]).then_inc(s_rw[0], 16)
                    sp.dma_start(kb[64:65, :, :], gate_sums[1:2, bass.ds(i * 2, 2), :]).then_inc(s_rw[1], 16)
                    sp.wait_ge(s_ktA, i + 1)
                    sp.sem_inc(s_round, 1)
                    sp.wait_ge(s_ktD, i * 2 + 2)
                    sp.sem_inc(s_round, 1)
                    cols = bass.ds(i * P, P)
                    sp.dma_start(kp[0:8 * P, cols].rearrange("(t p) n -> p t n", p=P), k_tok[:, 0:8, :]).then_inc(s_ko[0], 16)
                    sp.dma_start(kp[8 * P:NPR, cols], k_tok[0:META, 8, :]).then_inc(s_ko[1], 16)
                    sp.dma_start(ks[:, cols], k_tok[META:META + NSA, 8, :]).then_inc(s_ko[2], 16)
                    for s in s_ko:
                        sp.wait_ge(s, i * 16 + 16)
                        sp.sem_inc(s_round, 1)
                for n in range(2):
                    sp.wait_ge(s_fill[n], 16)
                    sp.wait_ge(s_wo[n], 16)

            @block.tensor
            def _(pe):
                T = nc.tensor

                def waited():
                    pe.sem_inc(s_hold, 1)

                def project(i):
                    n = 0
                    for key, w in (("k", wk_s), ("q", wq_s)):
                        pe.wait_ge(s_w[key], i * 16 + 16)
                        for c0, cn in CHUNKS_T:
                            if n >= 4:
                                pe.wait_ge(s_kev, i * 3 + (n - 3))
                            for k in range(KD):
                                last = T.matmul(bank[n % 4][:, 0:cn], w[:, k, :], xT[:, k, c0:c0 + cn],
                                                start=(k == 0), stop=(k == KD - 1))
                            last.then_inc(s_pj, 1)
                            n += 1

                def turn_k(i):
                    pe.wait_ge(s_kev, i * 3 + 3)
                    waited()
                    for t in range(NT):
                        w = min(P, TOK - t * P)
                        for h in range(2):
                            last = T.transpose(bank[4 + t // 4][0:w, (t % 4) * P + h * HD:(t % 4) * P + (h + 1) * HD],
                                               kb[0:HD, h, t * P:t * P + w], ident[0:HD, 0:HD])
                        if t % 4 == 3 or t == NT - 1:
                            last.then_inc(s_ktt, 1)

                def scores(i, n):
                    h, t = steps[n]
                    if n == 0:
                        pe.wait_ge(s_qev, i * 3 + 3)
                        for s in s_rw:
                            pe.wait_ge(s, i * 16 + 16)
                    if n >= 2:
                        pe.wait_ge(s_ex, i * NST + (n - 1))
                    if t == QT - 1:
                        pe.wait_ge(s_att, i * NST + (n - 1))
                    for b, k0, kn in pieces(n):
                        diag = k0 + kn > t * P
                        T.matmul(bank[b][0:nq(t), 0:kn], qb[:, h, t * P:t * P + nq(t)],
                                 kb[:, h, k0:k0 + kn], start=True, stop=not diag)
                    o0, w = t * P - k0, min(P, NPR - t * P)
                    T.matmul(bank[b][0:nq(t), o0:o0 + w], ident[:, 0:nq(t)], causal[:, 0:w],
                             start=False, stop=True).then_inc(s_S, 1)

                def turn(i, k):
                    n, g = groups[k]
                    t = steps[n][1]
                    pe.wait_ge(s_ex, i * NST + (n + 1))
                    if k < 2:
                        pe.wait_ge((s_ktA, s_ktD)[k], i * (1 + k) + 1)
                    else:
                        pe.wait_ge(s_E[k % 2], i * (NG // 2) + k // 2)
                    waited()
                    for j, b in enumerate(blocks(n, g)):
                        w = min(P, NPR - b * P)
                        last = T.transpose(bank[4 + k % 2][0:w, j * P:j * P + nq(t)],
                                           pbuf[n % 2][0:nq(t), b * P:b * P + w], ident[0:nq(t), 0:nq(t)])
                    last.then_inc(s_T, 1)

                def weigh(i, k):
                    n, g = groups[k]
                    h, t = steps[n]
                    pe.wait_ge(s_E[k % 2], i * (NG // 2) + (k // 2 + 1))
                    if g == 0 and n >= 2:
                        pe.wait_ge(s_att, i * NST + (n - 1))
                    if g == 0 and n == 0:
                        pe.wait_ge(s_ktD, i * 2 + 2)
                    waited()
                    for j, b in enumerate(blocks(n, g)):
                        lhs = pt[k % 2][:, j * P:j * P + nq(t)] if b < NT - 1 else ptail
                        last = T.matmul(bank[6 + n % 2][0:nq(t), 0:HD], lhs, v_tok[:, b,bass.ds(i * P + h * HD, HD)],
                                        start=(b == 0), stop=(b == t))
                    last.then_inc(s_PV, 1)

                pe.wait_ge(s_one, 1)
                with pe.Fori(0, 4) as i:
                    project(i)
                    turn_k(i)
                    scores(i, 0)
                    k = 0
                    weighed = 0
                    for n in range(NST):
                        if n + 1 < NST:
                            if steps[n + 1][1] == QT - 1:
                                weigh(i, k - 1)
                                weighed = k
                            scores(i, n + 1)
                        for _ in range(steps[n][1] // 4 + 1):
                            turn(i, k)
                            if k > weighed:
                                weigh(i, k - 1)
                                weighed = k
                            k += 1
                    weigh(i, NG - 1)
                    pe.wait_ge(s_att, i * NST + NST)
                    waited()
                    for t in range(QT):
                        b = (4, 5, 7)[t // 4]
                        last = T.transpose(bank[b][:, (t % 4) * P:(t % 4) * P + nq(t)], att[0:nq(t), t, :],
                                           ident[0:nq(t), 0:nq(t)])
                        if t % 4 == 3 or t == QT - 1:
                            last.then_inc(s_at, 1)
                    pe.wait_ge(s_aeA, i + 1)
                    pe.wait_ge(s_aeD, i * 2 + 2)

            def copy_turned(eng, copy, i, k):
                n, g = groups[k]
                t, bl = steps[n][1], blocks(n, g)
                eng.wait_ge(s_T, i * NG + (k + 1))
                full = [b for b in bl if NPR - b * P >= P]
                if nq(t) == P:
                    last = copy(pt[k % 2][:, 0:len(bl) * P], bank[4 + k % 2][:, 0:len(bl) * P])
                elif full:
                    last = copy(pt[k % 2].rearrange("p (j n) -> p j n", j=4)[:, 0:len(full), 0:nq(t)],
                                bank[4 + k % 2][:, :].rearrange("p (j n) -> p j n", j=4)[:, 0:len(full), 0:nq(t)])
                else:
                    w = NPR - bl[0] * P
                    last = copy(ptail[0:w, :], bank[4 + k % 2][0:w, 0:nq(t)])
                last.then_inc(s_E[k % 2], 1)

            @block.scalar
            def _(act):
                S = nc.scalar

                def exps(i, n):
                    h, t = steps[n]
                    q = nq(t)
                    act.wait_ge(s_mx, i * NST + (n + 1))
                    if n >= 2:
                        act.wait_ge(s_T, i * NG + upto[n - 2])
                    nk = min((t + 1) * P, 1024)
                    src = score_slot[n % 2][0:q, 0:nk]
                    if nk < (t + 1) * P:
                        last = S.activation(pbuf[n % 2][0:q, 1024:NPR], bank[6 + n % 2][0:q, 0:NPR - 1024], ACT.Exp,
                                            bias=sm[0:q, 0, n:n + 1], accum_out=sm2[0:q, 1, h:h + 1])
                    last = S.activation(pbuf[n % 2][0:q, 0:nk], src, ACT.Exp, bias=sm[0:q, 0, n:n + 1],
                                        accum_out=sm[0:q, 1, n:n + 1])
                    last.then_inc(s_ex, 1)

                act.wait_ge(s_tail, 1)
                with act.Fori(0, 4) as i:
                    for c, (c0, cn) in enumerate(CHUNKS_T):
                        n = 3 + c
                        act.wait_ge(s_pj, i * 6 + (n + 1))
                        pn = min(cn, NPR - c0)
                        if pn < cn:
                            S.mul(qs_T[:, bass.ds(i, 1), :], bank[n % 4][:, pn:cn].unsqueeze(1), SCALE)
                        for h in range(2):
                            last = S.mul(qb[0:HD, h, c0:c0 + pn], bank[n % 4][HD * h:HD * h + HD, 0:pn], SCALE)
                        last.then_inc(s_qev, 1)
                    act.wait_ge(s_rw[0], i * 16 + 16)
                    act.wait_ge(s_ktt, i * 3 + 1)
                    S.copy(k_tok[:, 0:4, :], bank[4][:, :].rearrange("p (t n) -> p t n", t=4)).then_inc(s_ktA, 1)
                    exps(i, 0)
                    for n in range(NST):
                        for k, (m, g) in enumerate(groups):
                            if m == n and k % 2:
                                copy_turned(act, S.copy, i, k)
                        if n + 1 < NST:
                            exps(i, n + 1)
                    act.wait_ge(s_at, i * 3 + 1)
                    S.copy(mixT[:, bass.ds(i, 1), 0:512], bank[4][:, :].unsqueeze(1)).then_inc(s_aeA, 1)

            @block.vector
            def _(dve):
                V = nc.vector
                V.memset(qb[64:P, :, :], 0.0)
                V.memset(kb[64:P, :, :], 0.0).then_inc(s_zero, 1)
                dve.wait_ge(s_zero, 1)
                V.memset(qb[64:66, :, :], 1.0)
                V.memset(kb[64:66, :, :], 1.0).then_inc(s_one, 1)
                dve.wait_ge(s_tail, 1)

                def maxima(i, n):
                    h, t = steps[n]
                    q = nq(t)
                    dve.wait_ge(s_S, i * NST + (n + 1))
                    nk = min((t + 1) * P, 1024)
                    src = score_slot[n % 2][0:q, 0:nk]
                    if nk == (t + 1) * P:
                        V.tensor_reduce(sm[0:q, 0, n:n + 1], src, AX, ALU.max, negate=True).then_inc(s_mx, 1)
                        return
                    V.tensor_reduce(sm[0:q, 3, 0:1], src, AX, ALU.max).then_inc(s_mp, 1)
                    V.tensor_reduce(sm[0:q, 3, 1:2], bank[pieces(n)[-1][0]][0:q, 0:NPR - t * P], AX,
                                    ALU.max).then_inc(s_mp, 1)
                    dve.wait_ge(s_mp, i * 4 + (2 * h + 2))
                    V.tensor_reduce(sm[0:q, 0, n:n + 1], sm[0:q, 3, 0:2], AX, ALU.max, negate=True).then_inc(s_mx, 1)

                def outputs(i, n):
                    h, t = steps[n]
                    q = nq(t)
                    dve.wait_ge(s_PV, i * NG + upto[n])
                    base = i * (NST + 2) + n + h
                    if t == QT - 1:
                        V.tensor_tensor(sm[0:q, 1, n:n + 1], sm[0:q, 1, n:n + 1], sm2[0:q, 1, h:h + 1],
                                        ALU.add).then_inc(s_rc, 1)
                        dve.wait_ge(s_rc, base + 1)
                        base = base + 1
                    V.reciprocal(sm[0:q, 2, n:n + 1], sm[0:q, 1, n:n + 1]).then_inc(s_rc, 1)
                    dve.wait_ge(s_rc, base + 1)
                    V.tensor_scalar(att[0:q, t, h * HD:(h + 1) * HD], bank[6 + n % 2][0:q, 0:HD],
                                    sm[0:q, 2, n:n + 1], None, ALU.mult).then_inc(s_att, 1)

                with dve.Fori(0, 4) as i:
                    for c, (c0, cn) in enumerate(CHUNKS_T):
                        dve.wait_ge(s_pj, i * 6 + (c + 1))
                        pn = min(cn, NPR - c0)
                        if pn < cn:
                            V.tensor_copy(ks_T[:, bass.ds(i, 1), :], bank[c][:, pn:cn].unsqueeze(1))
                        for h in range(2):
                            last = V.tensor_copy(kb[0:HD, h, c0:c0 + cn], bank[c][HD * h:HD * h + HD, 0:cn])
                        last.then_inc(s_kev, 1)
                    dve.wait_ge(s_rw[0], i * 16 + 16)
                    dve.wait_ge(s_ktt, i * 3 + 2)
                    V.tensor_copy(k_tok[:, 4:8, :], bank[5][:, :].rearrange("p (t n) -> p t n", t=4)).then_inc(s_ktD, 1)
                    dve.wait_ge(s_ktt, i * 3 + 3)
                    w = META + NSA
                    V.tensor_copy(k_tok[0:w, 8, :], bank[6][0:w, 0:P]).then_inc(s_ktD, 1)
                    maxima(i, 0)
                    for n in range(NST):
                        early = n + 1 < NST and steps[n + 1][1] == QT - 1
                        if early:
                            outputs(i, n - 1)
                        if n + 1 < NST:
                            maxima(i, n + 1)
                        for k, (m, g) in enumerate(groups):
                            if m == n and k % 2 == 0:
                                copy_turned(dve, V.tensor_copy, i, k)
                        if n and not early:
                            outputs(i, n - 1)
                    outputs(i, NST - 1)
                    for j, (c0, b, w) in enumerate(((512, 5, 512), (1024, 7, META))):
                        dve.wait_ge(s_at, i * 3 + (j + 2))
                        V.tensor_copy(mixT[:, bass.ds(i, 1), c0:c0 + w], bank[b][:, 0:w].unsqueeze(1)).then_inc(s_aeD, 1)

        logits = sb("logits", [P, NT, E])
        wsel = sb("wsel", [P, NT, 2])
        slot_i = sb("slot_i", [P, NT, 2], I32)
        tab_i = sb("tab_i", [1, 3, TT], I32)
        rounds_i = sb("rounds_i", [1, 1], I32)

        with phase() as (mem, block):
            o = 0
            NK = PAST + TS
            kc, vc, lc, vn = [], [], [], []
            for _s in range(2):
                a_, o = carve(o, NPAGE, DA)
                kc.append(a_.rearrange("p (j n) -> p j n", j=NPAGE))
                a_, o = carve(o, NPAGE, DA)
                vc.append(a_.rearrange("p (j n) -> p j n", j=NPAGE))
                a_, o = carve(o, NPAGE, H)
                lc.append(a_.rearrange("p (j n) -> p j n", j=NPAGE))
                a_, o = carve(o, DA)
                vn.append(a_)
            a_, o = carve(o, 4, NK)
            kT = a_.rearrange("p (a n) -> p a n", a=4)
            a_, o = carve(o, 320)
            qbd = a_
            qdiag = a_.rearrange("p (a n) -> p a n", n=80)
            a_, o = carve(o, NK)
            gates = a_
            a_, o = carve(o, NK)
            sums = a_
            a_, o = carve(o, NK)
            nsums = a_
            a_, o = carve(o, 64)
            qsum = a_
            a_, o = carve(o, 64)
            by_head = a_
            a_, o = carve(o, 64)
            by_query = a_
            a_, o = carve(o, NK)
            ones8 = a_
            a_, o = carve(o, NK)
            pr_ = a_
            a_, o = carve(o, 3, 64)
            pT = a_
            a_, o = carve(o, 3, 2)
            st = a_.rearrange("p (r s) -> p r s", r=3)
            xs_ = []
            for _s in range(3):
                a_, o = carve(o, D)
                xs_.append(a_)
            assert o <= W_O_AT
            ptab = mem.enter_context(nc.sbuf_tensor("ptab", [1, BS * NPAGE], I32))
            w_r = mem.enter_context(nc.sbuf_tensor("w_r", [P, KD, E], F32))
            zero_i = mem.enter_context(nc.sbuf_tensor("zero_i", [P, SLOTT], I32))
            ln = [mem.enter_context(nc.sbuf_tensor(f"ln1_st{s}", [P, 20], F32)) for s in range(3)]
            B_HT, B_LG, B_SC, B_K, B_PT, B_OUT = 2, 4, 5, (6, 7), 6, 7

            kinds = ("k0", "k1", "v0", "v1", "l0", "l1", "vn")
            s_ld = [{k: sem(f"d_loaded_{k}_{s}") for k in kinds} for s in range(2)]
            s_tab = sem("d_page_table")
            s_cst = sem("d_constants")
            s_lt = sem("d_gates_turned")
            s_kt = sem("d_keys_turned")
            s_kc = sem("d_keys_copied")
            s_q = sem("d_queries_placed")
            s_gc = sem("d_gates_copied")
            s_dc = sem("d_sums_made")
            s_cq = sem("d_sums_ready")
            s_sc = sem("d_scores")
            s_mx = sem("d_maxima")
            s_ex = sem("d_exponentials")
            s_rc = sem("d_inverse_sums")
            s_ps = sem("d_probabilities")
            s_tt = sem("d_turned")
            s_tc = sem("d_turned_copied")
            s_pv = sem("d_weighted")
            s_uc = sem("d_outputs")
            s_gz = sem("d_queries_cleared")
            s_wr = sem("c_router_weights")
            s_gb = [sem(f"c_gain_shift{n}") for n in range(2)]
            s_zi = sem("c_zeros_ready")
            s_zo = sem("c_slots_zeroed")
            s_x = [sem(f"c_stream{s}") for s in range(3)]
            s_mm = sem("c_projected")
            s_res = sem("c_residual_added")
            s_v = sem("c_vector_chain")
            s_var = sem("c_variance")
            s_std = sem("c_std")
            s_nb = sem("c_bias")
            s_cen = sem("c_centred")
            s_gn = sem("c_gained")
            s_h = sem("c_h_ready")
            s_ht = sem("c_h_turned")
            s_hc = sem("c_hT_copied")
            s_ho = [sem(f"c_h_parked{s}") for s in range(3)]
            s_lg = sem("c_logits")
            s_lc = sem("c_logits_copied")

            @block.sync
            def _(sp):
                sp.dma_start(ptab[:, :], A["page_table"].rearrange("(a b) j -> a (b j)", a=1)).then_inc(s_tab, 16)

                def load_x(t):
                    if t >= 3:
                        sp.wait_ge(s_ht, 2 * (t - 2))
                        sp.wait_ge(s_ho[t % 3], 16 * (t // 3))
                    sp.dma_start(xs_[t % 3], x_park[t]).then_inc(s_x[t % 3], 16)

                def load_past(b):
                    s = b % 2
                    ck = A["cache_k"].rearrange("n l p h d -> n (l p) (h d)")
                    cv = A["cache_v"].rearrange("n l p h d -> n (l p) (h d)")
                    cl = A["cache_logf"].rearrange("n l p h -> n (l p) h")
                    if b >= 2:
                        sp.wait_ge(s_pv, b - 1)
                    for j in range(NPAGE):
                        page = sp.value_load(ptab[0:1, b * NPAGE + j:b * NPAGE + j + 1], min_val=0, max_val=NPOOL - 1)
                        for key, src, dst in (("l", cl, lc), ("k", ck, kc), ("v", cv, vc)):
                            sp.dma_start(dst[s][:, j, :], src[bass.ds(page, 1), :, :].rearrange("a p n -> p (a n)")
                                         ).then_inc(s_ld[s][f"{key}{j}"], 16)
                    sp.dma_start(vn[s][0:TS, :], O["v_sample"][b, 0].rearrange("t h d -> t (h d)")
                                 ).then_inc(s_ld[s]["vn"], 16)

                sp.wait_ge(s_tab, 16)
                load_past(0)
                load_x(0)
                sp.dma_start(gb[:, 0, :], bcast_rows(A["ln1_g"][0], P)).then_inc(s_gb[0], 16)
                sp.dma_start(gb[:, 1, :], bcast_rows(A["ln1_b"][0], P)).then_inc(s_gb[1], 16)
                sp.dma_start(w_r[:, :, :], A["w_router"].rearrange("(k p) n -> p k n", p=P)).then_inc(s_wr, 16)
                load_past(1)
                load_x(1)
                load_x(2)
                sp.wait_ge(s_zi, 1)
                sp.dma_start(slot_tok.rearrange("(p n) a -> p (n a)", p=P), zero_i[:, :]).then_inc(s_zo, 16)
                for t in range(NT):
                    if t + 2 < BS:
                        load_past(t + 2)
                    sp.wait_ge(s_h, t + 1)
                    sp.dma_start(h_park[t * P:(t + 1) * P, :], xs_[t % 3]).then_inc(s_ho[t % 3], 16)
                    if t + 3 < NT:
                        load_x(t + 3)
                for s in range(3):
                    sp.wait_ge(s_ho[s], 16 * (NT // 3))
                sp.wait_ge(s_zo, 16)

            @block.tensor
            def _(pe):
                T = nc.tensor

                def project(t, quarter):
                    if quarter == 0:
                        if t >= 1:
                            pe.wait_ge(s_res, t)
                        if t == NT - 1:
                            pe.wait_ge(s_uc, BS)
                    half = quarter // 2
                    for k in range(4 * (quarter % 2), 4 * (quarter % 2) + 4):
                        last = T.matmul(bank[half], mixT[:, k, t * P:(t + 1) * P],
                                        w_o[:, k, 512 * half:512 * half + 512], start=(k == 0), stop=(k == KD - 1))
                    if quarter == 3:
                        last.then_inc(s_mm, 1)

                def turn(t):
                    pe.wait_ge(s_h, t + 1)
                    for half in range(2):
                        if t >= 1:
                            pe.wait_ge(s_hc, 2 * t - 1 + half)
                        for k in range(4):
                            kk = 4 * half + k
                            last = T.transpose(bank[B_HT + half][:, k * P:(k + 1) * P],
                                               xs_[t % 3][:, kk * P:(kk + 1) * P], ident[:, :])
                        last.then_inc(s_ht, 1)

                def route(t):
                    pe.wait_ge(s_hc, 2 * t + 2)
                    if t >= 1:
                        pe.wait_ge(s_lc, t)
                    for k in range(KD):
                        last = T.matmul(bank[B_LG][:, 0:E], xT[:, k, t * P:(t + 1) * P], w_r[:, k, :],
                                        start=(k == 0), stop=(k == KD - 1))
                    last.then_inc(s_lg, 1)

                def turn_past(b):
                    s, use = b % 2, b // 2 + 1
                    for j in range(NPAGE):
                        pe.wait_ge(s_ld[s][f"l{j}"], use * 16)
                    if b >= 1:
                        pe.wait_ge(s_ex, b)
                        pe.wait_ge(s_tc, b)
                    for j in range(NPAGE):
                        last = T.transpose(bank[B_SC][0:H, j * P:(j + 1) * P], lc[s][:, j, :], ident[:, :])
                    last.then_inc(s_lt, 1)
                    for j in range(NPAGE):
                        pe.wait_ge(s_ld[s][f"k{j}"], use * 16)
                    for a in range(4):
                        if a == 2 and b >= 1:
                            pe.wait_ge(s_uc, b)
                        for j in range(NPAGE):
                            last = T.transpose(bank[B_K[a // 2]][:, ((a % 2) * 2 + j) * P:((a % 2) * 2 + j + 1) * P],
                                               kc[s][:, j, a * P:(a + 1) * P], ident[:, :])
                        if a % 2:
                            last.then_inc(s_kt, 1)

                def scores(b):
                    pe.wait_ge(s_q, b + 1)
                    pe.wait_ge(s_kc, b * 2 + 2)
                    pe.wait_ge(s_cq, b + 1)
                    z = bank[B_SC]
                    for a in range(4):
                        T.matmul(z[0:64, 0:NK], qbd[:, 64 * a:64 * a + 64], kT[:, a, :], start=(a == 0), stop=False)
                    T.matmul(z[0:64, 0:NK], by_head[0:H, :], nsums[0:H, :], start=False, stop=False)
                    T.matmul(z[0:64, 0:NK], qsum[0:H, :], ones8[0:H, :], start=False, stop=False)
                    T.matmul(z[0:64, PAST:NK], by_query[0:TS, :], causal[0:TS, 0:TS],
                             start=False, stop=True).then_inc(s_sc, 1)

                def turn_probabilities(b):
                    pe.wait_ge(s_ps, b + 1)
                    for j in range(3):
                        w = min(P, NK - j * P)
                        last = T.transpose(bank[B_PT][0:w, j * 64:(j + 1) * 64], pr_[0:64, j * P:j * P + w],
                                           ident[0:64, 0:64])
                    last.then_inc(s_tt, 1)

                def weigh(b):
                    s, use = b % 2, b // 2 + 1
                    for k in ("v0", "v1", "vn"):
                        pe.wait_ge(s_ld[s][k], use * 16)
                    pe.wait_ge(s_tc, b + 1)
                    for a in range(4):
                        for j in range(3):
                            w = min(P, NK - j * P)
                            lhs = vc[s][:, j, a * P:(a + 1) * P] if j < 2 else vn[s][0:TS, a * P:(a + 1) * P]
                            last = T.matmul(bank[B_OUT][:, a * 16:a * 16 + 16], lhs,
                                            pT[0:w, 64 * j + 16 * a:64 * j + 16 * a + 16],
                                            start=(j == 0), stop=(j == 2))
                    last.then_inc(s_pv, 1)

                pe.wait_ge(s_cst, 1)
                for t in range(NT):
                    project(t, 0)
                    if t < BS:
                        turn_past(t)
                    project(t, 1)
                    if t < BS:
                        scores(t)
                    project(t, 2)
                    if t >= 1:
                        turn(t - 1)
                    if t < BS:
                        turn_probabilities(t)
                    project(t, 3)
                    if t == 1:
                        pe.wait_ge(s_wr, 16)
                    if t >= 1:
                        route(t - 1)
                    if t < BS:
                        weigh(t)
                turn(NT - 1)
                route(NT - 1)

            @block.scalar
            def _(act):
                S = nc.scalar

                def centre(t):
                    s = t % 3
                    act.wait_ge(s_var, t + 1)
                    S.activation(ln[s][:, 15:16], ln[s][:, 14:15], ACT.Sqrt).then_inc(s_std, 1)
                    act.wait_ge(s_nb, t + 1)
                    S.activation(xs_[s], xs_[s], ACT.Identity, bias=ln[s][:, 17:18],
                                 scale=ln[s][:, 16:17]).then_inc(s_cen, 1)

                def h_turned(t):
                    for half in range(2):
                        act.wait_ge(s_ht, 2 * t + half + 1)
                        S.copy(xT[:, 4 * half:4 * half + 4, t * P:(t + 1) * P],
                               bank[B_HT + half].rearrange("p (k n) -> p k n", k=4)).then_inc(s_hc, 1)

                def keys(b):
                    if b >= 1:
                        act.wait_ge(s_sc, b)
                    for c in range(2):
                        act.wait_ge(s_kt, b * 2 + (c + 1))
                        S.copy(kT[:, 2 * c:2 * c + 2, 0:PAST],
                               bank[B_K[c]][:, :].rearrange("p (a n) -> p a n", a=2)).then_inc(s_kc, 1)

                for t in range(NT + 1):
                    if t >= 1:
                        centre(t - 1)
                    if t < BS:
                        keys(t)
                        act.wait_ge(s_mx, t + 1)
                        S.activation(pr_[0:64, :], bank[B_SC][0:64, 0:NK], ACT.Exp, bias=st[0:64, 0, 0:1],
                                     accum_out=st[0:64, 1, 0:1]).then_inc(s_ex, 1)
                    if t >= 1:
                        h_turned(t - 1)
                    if t < BS:
                        act.wait_ge(s_tt, t + 1)
                        S.copy(pT[:, 0:128], bank[B_PT][:, 0:128])
                        S.copy(pT[0:TS, 128:192], bank[B_PT][0:TS, 128:192]).then_inc(s_tc, 1)

            @block.gpsimd
            def _(pool):
                G = nc.gpsimd
                G.memset(qbd, 0.0).then_inc(s_gz, 1)
                G.memset(zero_i[:, :], 0).then_inc(s_zi, 1)
                pool.wait_ge(s_gb[1], 16)
                for t in range(NT):
                    pool.wait_ge(s_gn, t + 1)
                    G.tensor_tensor(xs_[t % 3], xs_[t % 3], gb[:, 1, :], ALU.add).then_inc(s_h, 1)

            @block.vector
            def _(dve):
                V = nc.vector
                chain = Link(dve, s_v)

                def normalise(t):
                    s = t % 3
                    dve.wait_ge(s_x[s], 16 * (t // 3 + 1))
                    dve.wait_ge(s_mm, t + 1)
                    V.scalar_tensor_tensor(xs_[s], xs_[s], ALPHA, duo[0][:, :], ALU.mult, ALU.add).then_inc(s_res, 1)
                    dve.wait_ge(s_res, t + 1)
                    V.bn_stats(ln[s][:, 0:6], xs_[s][:, 0:512])
                    chain(V.bn_stats(ln[s][:, 6:12], xs_[s][:, 512:1024]))
                    chain(V.bn_aggr(ln[s][:, 12:14], ln[s][:, 0:12]))
                    V.tensor_scalar_add(ln[s][:, 14:15], ln[s][:, 13:14], EPS).then_inc(s_var, 1)
                    dve.wait_ge(s_std, t + 1)
                    chain(V.reciprocal(ln[s][:, 16:17], ln[s][:, 15:16]))
                    V.tensor_scalar(ln[s][:, 17:18], ln[s][:, 12:13], ln[s][:, 16:17], -1.0,
                                    ALU.mult, ALU.mult).then_inc(s_nb, 1)
                    dve.wait_ge(s_cen, t + 1)
                    V.tensor_tensor(xs_[s], xs_[s], gb[:, 0, :], ALU.mult).then_inc(s_gn, 1)

                def take_logits(t):
                    dve.wait_ge(s_lg, t + 1)
                    V.tensor_copy(logits[:, t, :], bank[B_LG][:, 0:E]).then_inc(s_lc, 1)

                def sequence(b):
                    if b >= 1:
                        dve.wait_ge(s_sc, b)
                    new = slice(b * TS, b * TS + TS)
                    newc = slice(b * TS + NPR, b * TS + NPR + TS)
                    V.tensor_copy(qdiag[0:64, :, 0:TS], qs_T[0:64, :, new])
                    V.tensor_copy(qdiag[64:P, :, TS:2 * TS], qs_T[64:P, :, new])
                    V.tensor_copy(kT[:, :, PAST:NK], ks_T[:, :, new]).then_inc(s_q, 1)
                    V.tensor_copy(gates[0:H, PAST:NK], cum[:, newc])
                    dve.wait_ge(s_lt, b + 1)
                    V.tensor_copy(gates[0:H, 0:PAST], bank[B_SC][0:H, 0:PAST]).then_inc(s_gc, 1)
                    dve.wait_ge(s_gc, b + 1)
                    V.tensor_tensor_scan(sums[0:H, :], ones8[0:H, :], gates[0:H, :], 0.0, ALU.mult, ALU.add).then_inc(s_dc, 1)
                    dve.wait_ge(s_dc, b + 1)
                    V.tensor_scalar(nsums[0:H, :], sums[0:H, :], -1.0, None, ALU.mult)
                    V.tensor_tensor(qsum[0:H, :].rearrange("h (g q) -> h g q", g=H),
                                    by_head[0:H, :].rearrange("h (g q) -> h g q", g=H),
                                    sums[0:H, PAST:NK].unsqueeze(1).to_broadcast([H, H, TS]),
                                    ALU.mult).then_inc(s_cq, 1)
                    dve.wait_ge(s_sc, b + 1)
                    V.tensor_reduce(st[0:64, 0, 0:1], bank[B_SC][0:64, 0:NK], AX, ALU.max,
                                    negate=True).then_inc(s_mx, 1)
                    dve.wait_ge(s_ex, b + 1)
                    V.reciprocal(st[0:64, 2, 0:1], st[0:64, 1, 0:1]).then_inc(s_rc, 1)
                    dve.wait_ge(s_rc, b + 1)
                    V.tensor_scalar(pr_[0:64, :], pr_[0:64, :], st[0:64, 2, 0:1], None,
                                    ALU.mult).then_inc(s_ps, 1)

                def outputs(b):
                    dve.wait_ge(s_pv, b + 1)
                    newc = slice(b * TS + NPR, b * TS + NPR + TS)
                    u = bank[B_OUT][:, 0:64].rearrange("p (a n) -> p a n", a=4)
                    V.tensor_copy(mixT[0:64, 0:4, newc], u[0:64, :, 0:TS])
                    V.tensor_copy(mixT[64:P, 0:4, newc], u[64:P, :, TS:2 * TS]).then_inc(s_uc, 1)

                V.memset(ones8[0:H, :], 1.0)
                V.tensor_copy(by_head[0:H, :].rearrange("h (g q) -> h g q", g=H),
                              ident[0:H, 0:H].unsqueeze(2).to_broadcast([H, H, TS]))
                V.tensor_copy(by_query[0:TS, :].rearrange("h (g q) -> h g q", g=H),
                              ident[0:TS, 0:TS].unsqueeze(1).to_broadcast([TS, H, TS])).then_inc(s_cst, 1)
                dve.wait_ge(s_cst, 1)
                dve.wait_ge(s_gz, 1)
                dve.wait_ge(s_gb[0], 16)
                for t in range(NT + 1):
                    if t >= 1:
                        normalise(t - 1)
                    if t < BS:
                        sequence(t)
                    if t >= 1:
                        take_logits(t - 1)
                    if t < BS:
                        outputs(t)

        with phase() as (mem, block):
            o = 0

            def small(*shape):
                at = cursor[0]
                n = math.prod(shape)
                cursor[0] += n
                ap = arena[:, at:at + n]
                if len(shape) == 1:
                    return ap
                if len(shape) == 2:
                    return ap.rearrange("p (a b) -> p a b", b=shape[1])
                return ap.rearrange("p (a b c) -> p a b c", b=shape[1], c=shape[2])

            cursor = [0]
            NG4 = E // EG
            before = small(P)
            all1 = small(P)
            valid = small(NT)
            aff, biased, masked, sel1, sel2, both = (small(NT, E) for _ in range(6))
            pairs = small(NT * NG4, 6)
            gscore = small(NT, NG4)
            best = small(NT)
            key4 = small(NT, NG4)
            pref4 = small(NG4)
            pref16 = small(E)
            scr = small(NT, E)
            rank, prior = small(NT, E), small(NT + 1, E)
            over = small(E, NT)
            thr = small(NT)
            tiles, upto_, base = small(E), small(E), small(E)
            slotf = small(NT, 2)
            tau = small(TT)
            cmp = small(TT, E)
            ef, chg, run = small(TT), small(TT + 1), small(TT)
            th3 = small(5)
            cmp3 = small(TT, 5)
            r3 = small(TT)
            th11 = small(ROUNDS)
            c11 = small(ROUNDS)
            nr = small(1)
            wsum = small(NT)
            br = mem.enter_context(nc.sbuf_tensor("br", [P, E], F32))
            tok_i = mem.enter_context(nc.sbuf_tensor("tok_i", [P, NT], I32))
            s_br = sem("t_router_bias")
            s_p = sem("t_pool_chain")
            s_v = sem("t_vector_chain")
            s_sg = sem("t_sigmoids")
            s_both = sem("t_choices")
            s_rk = sem("t_ranks")
            s_sl = sem("t_slots")
            s_sc = sem("t_scattered")

            @block.sync
            def _(sp):
                sp.dma_start(br[:, :], bcast_rows(A["b_router"], P)).then_inc(s_br, 16)
                sp.wait_ge(s_br, 16)

            @block.scalar
            def _(act):
                nc.scalar.activation(aff, logits[:, :, :], ACT.Sigmoid).then_inc(s_sg, 1)

            @block.tensor
            def _(pe):
                pe.wait_ge(s_p, 9)
                pe.wait_ge(s_both, 1)
                flat = both.rearrange("p t e -> p (t e)")
                nc.tensor.matmul(bank[0][:, 0:NT * E], before, flat, start=True, stop=True)
                nc.tensor.matmul(bank[1][:, 0:NT * E], all1, flat, start=True, stop=True).then_inc(s_rk, 1)

            @block.gpsimd
            def _(pool):
                G = nc.gpsimd
                chain = Link(pool, s_p)
                imp = dict(allow_small_or_imprecise_dtypes=True)
                chain(G.memset(all1, 1.0))
                chain(G.affine_select(out=before, in_=all1, compare_op=ALU.is_gt, fill=0.0, base=0,
                                      pattern=[[1, P]], channel_multiplier=-1))
                chain(G.affine_select(out=valid, in_=all1[:, 0:NT], compare_op=ALU.is_gt, fill=0.0, base=TOK,
                                      pattern=[[-P, NT]], channel_multiplier=-1))
                chain(G.iota(pref4, [[-1, NG4]], base=NG4, channel_multiplier=0, **imp))
                chain(G.iota(pref16, [[-1, E]], base=E, channel_multiplier=0, **imp))
                chain(G.iota(thr, [[P, NT]], base=0, channel_multiplier=0, **imp))
                chain(G.iota(tau, [[1, TT]], base=0, channel_multiplier=0, **imp))
                chain(G.iota(th3, [[3, 5]], base=3, channel_multiplier=0, **imp))
                chain(G.iota(th11, [[3, ROUNDS]], base=0, channel_multiplier=0, **imp))
                chain(G.iota(tok_i[:, :], [[P, NT]], base=0, channel_multiplier=1))
                pool.wait_ge(s_sl, 1)
                n = 0
                for t in range(NT):
                    rows = min(P, TOK - t * P)
                    for c in range(2):
                        G.indirect_dma_start(
                            out=slot_tok, out_offset=bass.IndirectOffsetOnAxis(ap=slot_i[0:rows, t, c:c + 1], axis=0),
                            in_=tok_i[0:rows, t:t + 1], in_offset=None).then_inc(s_sc, 16)
                        n += 1
                pool.wait_ge(s_sc, 16 * n)

            @block.vector
            def _(dve):
                V = nc.vector
                link = Link(dve, s_v)

                def tt(o_, a, b, op):
                    link(V.tensor_tensor(o_, a, b, op))

                def mx(o_, a):
                    link(V.tensor_reduce(o_, a, AX, ALU.max))

                def sm_(o_, a):
                    link(V.tensor_reduce(o_, a, AX, ALU.add))

                def inner(x, n):
                    return x.unsqueeze(len(x.shape)).to_broadcast(list(x.shape) + [n])

                def outer(x, n):
                    return x.unsqueeze(1).to_broadcast([P, n, x.shape[1]])

                dve.wait_ge(s_p, 10)
                dve.wait_ge(s_br, 16)
                dve.wait_ge(s_sg, 1)
                tt(biased, aff, outer(br[:, :], NT), ALU.add)
                b4 = biased.rearrange("p t (g e) -> p (t g) e", e=EG)
                V.tensor_tensor(pairs[:, :, 0:3], b4[:, :, 0:3], b4[:, :, 1:4], ALU.add)
                V.tensor_tensor(pairs[:, :, 3:5], b4[:, :, 0:2], b4[:, :, 2:4], ALU.add)
                tt(pairs[:, :, 5:6], b4[:, :, 0:1], b4[:, :, 3:4], ALU.add)
                mx(gscore.rearrange("p t g -> p (t g)"), pairs)
                mx(best, gscore)
                tt(key4, gscore, inner(best, NG4), ALU.is_ge)
                tt(key4, key4, outer(pref4, NT), ALU.mult)
                mx(best, key4)
                tt(key4, key4, inner(best, NG4), ALU.is_equal)
                g4 = key4.rearrange("p t g -> p (t g)")
                m4 = masked.rearrange("p t (g e) -> p (t g) e", e=EG)
                s4 = scr.rearrange("p t (g e) -> p (t g) e", e=EG)
                V.tensor_tensor(m4, b4, inner(g4, EG), ALU.mult)
                link(V.tensor_scalar(s4, inner(g4, EG), -NEG, NEG, ALU.mult, ALU.add))
                tt(masked, masked, scr, ALU.add)
                for sel in (sel1, sel2):
                    mx(best, masked)
                    tt(sel, masked, inner(best, E), ALU.is_ge)
                    tt(sel, sel, outer(pref16, NT), ALU.mult)
                    mx(best, sel)
                    tt(sel, sel, inner(best, E), ALU.is_equal)
                    link(V.scalar_tensor_tensor(masked, sel, 3 * NEG, masked, ALU.mult, ALU.add))
                for c, sel in enumerate((sel1, sel2)):
                    tt(scr, sel, aff, ALU.mult)
                    sm_(wsel[:, :, c], scr)
                tt(wsum, wsel[:, :, 0], wsel[:, :, 1], ALU.add)
                link(V.reciprocal(wsum, wsum))
                tt(wsel[:, :, :], wsel[:, :, :], inner(wsum, 2), ALU.mult)
                tt(both, sel1, sel2, ALU.add)
                V.tensor_tensor(both, both, inner(valid, E), ALU.mult).then_inc(s_both, 1)
                dve.wait_ge(s_rk, 1)
                V.tensor_copy(rank.rearrange("p t e -> p (t e)"), bank[0][:, 0:NT * E])
                link(V.memset(prior[:, 0, :], 0.0))
                for t in range(NT):
                    tt(prior[:, t + 1, :], prior[:, t, :], bank[1][:, t * E:(t + 1) * E], ALU.add)
                tt(over, inner(prior[:, NT, :], NT), outer(thr, E), ALU.is_gt)
                sm_(tiles, over)
                link(V.tensor_tensor_scan(upto_, all1[:, 0:E], tiles, 0.0, ALU.mult, ALU.add))
                tt(base, upto_, tiles, ALU.subtract)
                link(V.tensor_scalar(base, base, float(P), None, ALU.mult))
                tt(rank, rank, prior[:, 0:NT, :], ALU.add)
                tt(rank, rank, outer(base, NT), ALU.add)
                for c, sel in enumerate((sel1, sel2)):
                    tt(scr, sel, rank, ALU.mult)
                    sm_(slotf[:, :, c], scr)
                V.tensor_copy(slot_i[:, :, :], slotf).then_inc(s_sl, 1)
                tt(cmp, outer(upto_, TT), inner(tau, E), ALU.is_le)
                sm_(ef, cmp)
                link(V.tensor_scalar(ef, ef, float(E - 1), None, ALU.min))
                link(V.memset(chg[:, 0:1], 1.0))
                tt(chg[:, 1:TT], ef[:, 1:TT], ef[:, 0:TT - 1], ALU.not_equal)
                link(V.tensor_tensor_scan(run, all1[:, 0:TT], chg[:, 0:TT], -1.0, ALU.mult, ALU.add))
                tt(cmp3, inner(run, 5), outer(th3, TT), ALU.is_ge)
                sm_(r3, cmp3)
                link(V.scalar_tensor_tensor(r3, r3, -3.0, run, ALU.mult, ALU.add))
                tt(c11, upto_[:, E - 1:E].to_broadcast([P, ROUNDS]), th11, ALU.is_gt)
                sm_(nr, c11)
                V.tensor_copy(tab_i[:, 0, :], ef[0:1, :])
                V.tensor_copy(tab_i[:, 1, :], r3[0:1, :])
                V.tensor_copy(tab_i[:, 2, :], chg[0:1, 0:TT])
                link(V.tensor_copy(rounds_i[:, :], nr[0:1, :]))

        with phase() as (mem, block):
            o = 0
            DW = KD * DE
            weights = []
            for _n in range(3):
                a_, o = carve(o, 3, DW)
                weights.append(a_.rearrange("p (s n) -> p s n", s=3))
            w_gs, w_us, w_ds = weights
            assert o <= AR
            xg = [vflat[:, D * s:D * (s + 1)] for s in range(3)]
            mall = mixT[:, :, :].rearrange("p k t -> p (k t)")
            xgT = [mall[:, D * s:D * (s + 1)] for s in range(3)]
            ysl = [mall[:, D * (3 + s):D * (4 + s)] for s in range(3)]
            rest = mall[:, 6 * D:]
            sil = [rest[:, DE * s:DE * (s + 1)] for s in range(3)]
            hid = [rest[:, DE * (3 + s):DE * (4 + s)] for s in range(3)]
            hidT = [rest[:, DE * (6 + s):DE * (7 + s)] for s in range(3)]
            idx_all = mem.enter_context(nc.sbuf_tensor("idx_all", [P, TT], I32))
            idx = [mem.enter_context(nc.sbuf_tensor(f"idx{s}", [P, 1], I32)) for s in range(3)]
            s_ix = sem("e_slot_tokens")
            s_pad = sem("e_padding_zeroed")
            s_ic = [sem(f"e_index_copied{s}") for s in range(3)]
            s_g = [sem(f"e_gathered{s}") for s in range(3)]
            s_w = [[sem(f"e_{k}_weights{s}") for s in range(3)] for k in ("gate", "up", "down")]
            s_xt = sem("e_rows_turned")
            s_xc = sem("e_rows_copied")
            s_gu = sem("e_gate_up")
            s_si = sem("e_silu")
            s_hid = sem("e_hidden")
            s_ht = sem("e_hidden_turned")
            s_he = sem("e_hidden_copied")
            s_dn = sem("e_down")
            s_yA = sem("e_output_low")
            s_yD = sem("e_output_high")
            s_yo = [sem(f"e_output_stored{s}") for s in range(3)]
            s_hold = sem("e_waits_held_by_sync")
            s_holdp = sem("e_waits_held_by_tensor")
            s_holdg = sem("e_waits_held_by_pool")

            def rounds(eng, prologue, body, epilogue):
                n = eng.value_load(rounds_i[0:1, 0:1], min_val=1, max_val=ROUNDS)
                prologue()
                for s in range(3):
                    body(s, 0, s, True)
                with eng.Fori(1, ROUNDS) as i:
                    with eng.If(i < n):
                        for s in range(3):
                            body(i * 3 + s, i, s, False)
                epilogue(n)

            @block.sync
            def _(sp):
                sp.dma_start(idx_all[:, 0:SLOTT], slot_tok.rearrange("(t p) a -> p (t a)", p=P)).then_inc(s_ix, 16)
                srcs = (A["w_gate"][0].rearrange("e (p k) f -> e p (k f)", p=P),
                        A["w_up"][0].rearrange("e (p k) f -> e p (k f)", p=P),
                        A["w_down"][0].rearrange("e (p j) d -> e p (j d)", p=P))

                def load(tau, s):
                    e, slot, new = (sp.value_load(tab_i[0:1, r, bass.ds(tau, 1)], min_val=0, max_val=m)
                                    for r, m in enumerate((E - 1, 2, 1)))
                    for k in range(3):
                        sp.dma_start(weights[k][:, bass.ds(slot, 1), :],
                                     srcs[k][bass.ds(e, 1), :, :].rearrange("a p n -> p a n"),
                                     cond=new > 0).then_inc(s_w[k][s], 16)

                def store(tau, s):
                    sp.wait_ge(s_yA, tau + 2)
                    sp.sem_inc(s_hold, 1)
                    sp.wait_ge(s_yD, tau + 2)
                    sp.sem_inc(s_hold, 1)
                    rows = slice(tau * P, tau * P + P) if isinstance(tau, int) else bass.ds(tau * P, P)
                    sp.dma_start(y_park[rows, :], ysl[s]).then_inc(s_yo[s], 16)

                def prologue():
                    for s in range(3):
                        sp.sem_inc(s_yo[s], 16)
                        load(s, s)

                def body(tau, i, s, first):
                    sp.wait_ge(s_dn, tau + 1)
                    sp.sem_inc(s_hold, 1)
                    load(tau + 3, s)
                    store(tau, s)

                def epilogue(n):
                    for s in range(3):
                        sp.wait_ge(s_yo[s], n * 16 + 16)
                        sp.sem_inc(s_hold, 1)
                        for k in range(3):
                            sp.wait_ge(s_w[k][s], n * 16 + 16)
                            sp.sem_inc(s_hold, 1)
                rounds(sp, prologue, body, epilogue)

            @block.gpsimd
            def _(pool):
                G = nc.gpsimd

                def gather(tau, i, s):
                    src = idx_all[:, tau:tau + 1] if isinstance(tau, int) else idx_all[:, bass.ds(tau, 1)]
                    G.tensor_copy(idx[s][:, :], src).then_inc(s_ic[s], 1)
                    pool.wait_ge(s_ic[s], i + 1)
                    pool.sem_inc(s_holdg, 1)
                    G.indirect_dma_start(out=xg[s], out_offset=None, in_=h_park,
                                         in_offset=bass.IndirectOffsetOnAxis(ap=idx[s][:, 0:1], axis=0)
                                         ).then_inc(s_g[s], 16)

                def prologue():
                    G.memset(idx_all[:, SLOTT:TT], 0).then_inc(s_pad, 1)
                    pool.wait_ge(s_pad, 1)
                    pool.wait_ge(s_ix, 16)
                    for s in range(3):
                        gather(s, 0, s)

                def body(tau, i, s, first):
                    pool.wait_ge(s_xt, tau * 2 + 2)
                    pool.sem_inc(s_holdg, 1)
                    pool.wait_ge(s_g[s], i * 16 + 16)
                    pool.sem_inc(s_holdg, 1)
                    gather(tau + 3, i + 1, s)

                def epilogue(n):
                    for s in range(3):
                        pool.wait_ge(s_g[s], n * 16 + 16)
                        pool.sem_inc(s_holdg, 1)
                rounds(pool, prologue, body, epilogue)

            @block.tensor
            def _(pe):
                T = nc.tensor

                def waited():
                    pe.sem_inc(s_holdp, 1)

                def turn_x(tau, i, s):
                    pe.wait_ge(s_g[s], i * 16 + 16)
                    for half in range(2):
                        if not (isinstance(tau, int) and tau == 0):
                            pe.wait_ge(s_xc, tau * 2 - 1 + half)
                        waited()
                        for k in range(4):
                            last = T.transpose(bank[half][:, k * P:(k + 1) * P],
                                               xg[s][:, 4 * half + k::KD], ident[:, :])
                        last.then_inc(s_xt, 1)

                def half_gu(tau, i, s, which, slot):
                    if which == 0:
                        pe.wait_ge(s_xc, tau * 2 + 2)
                    pe.wait_ge(s_w[which][s], i * 16 + 16)
                    waited()
                    for k in range(KD):
                        last = T.matmul(bank[2 + s][:, DE * which:DE * (which + 1)], xgT[s][:, k * P:(k + 1) * P],
                                        weights[which][:, bass.ds(slot, 1), k * DE:(k + 1) * DE],
                                        start=(k == 0), stop=(k == KD - 1))
                    if which == 1:
                        last.then_inc(s_gu, 1)

                def turn_hidden(tau, s):
                    pe.wait_ge(s_hid, tau + 1)
                    pe.wait_ge(s_he, tau + 1)
                    waited()
                    for j in range(2):
                        last = T.transpose(bank[5][:, j * P:(j + 1) * P], hid[s][:, j::2], ident[:, :])
                    last.then_inc(s_ht, 1)

                def down(tau, i, off, s, slot):
                    pe.wait_ge(s_he, tau + 2)
                    pe.wait_ge(s_w[2][s], i * 16 + (16 * off + 16))
                    pe.wait_ge(s_yA, tau + 1)
                    pe.wait_ge(s_yD, tau + 1)
                    waited()
                    for half in range(2):
                        for j in range(2):
                            last = T.matmul(bank[6 + half], hidT[s][:, j * P:(j + 1) * P],
                                            w_ds[:, bass.ds(slot, 1), j * D + 512 * half:j * D + 512 * half + 512],
                                            start=(j == 0), stop=(j == 1))
                    last.then_inc(s_dn, 1)

                def slot_of(tau):
                    return pe.value_load(tab_i[0:1, 1, bass.ds(tau, 1)], min_val=0, max_val=2)

                def prologue():
                    turn_x(0, 0, 0)

                def body(tau, i, s, first):
                    back = not (first and s == 0)
                    slot = slot_of(tau)
                    half_gu(tau, i, s, 0, slot)
                    if back:
                        turn_hidden(tau - 1, (s - 1) % 3)
                    half_gu(tau, i, s, 1, slot)
                    turn_x(tau + 1, i + (1 if s == 2 else 0), (s + 1) % 3)
                    if back:
                        down(tau - 1, i, 0 if s else -1, (s - 1) % 3, slot_of(tau - 1))

                def epilogue(n):
                    turn_hidden(n * 3 - 1, 2)
                    down(n * 3 - 1, n, -1, 2, slot_of(n * 3 - 1))
                rounds(pe, prologue, body, epilogue)

            @block.scalar
            def _(act):
                S = nc.scalar

                def copy_x(tau, s):
                    for half in range(2):
                        act.wait_ge(s_xt, tau * 2 + (half + 1))
                        S.copy(xgT[s][:, 512 * half:512 * half + 512], bank[half]).then_inc(s_xc, 1)

                def low(tau, i, off, s):
                    act.wait_ge(s_dn, tau + 1)
                    act.wait_ge(s_yo[s], i * 16 + (16 * off + 16))
                    S.copy(ysl[s][:, 0:512], bank[6]).then_inc(s_yA, 1)

                def prologue():
                    act.sem_inc(s_yA, 1)
                    copy_x(0, 0)

                def body(tau, i, s, first):
                    act.wait_ge(s_gu, tau + 1)
                    S.activation(sil[s], bank[2 + s][:, 0:DE], ACT.Silu).then_inc(s_si, 1)
                    copy_x(tau + 1, (s + 1) % 3)
                    if not (first and s == 0):
                        low(tau - 1, i, 0 if s else -1, (s - 1) % 3)

                def epilogue(n):
                    low(n * 3 - 1, n, -1, 2)
                rounds(act, prologue, body, epilogue)

            @block.vector
            def _(dve):
                V = nc.vector

                def copy_hidden(tau, s):
                    dve.wait_ge(s_ht, tau + 1)
                    V.tensor_copy(hidT[s], bank[5][:, 0:DE]).then_inc(s_he, 1)

                def high(tau, i, off, s):
                    dve.wait_ge(s_dn, tau + 1)
                    dve.wait_ge(s_yo[s], i * 16 + (16 * off + 16))
                    V.tensor_copy(ysl[s][:, 512:D], bank[7]).then_inc(s_yD, 1)

                def body(tau, i, s, first):
                    back = not (first and s == 0)
                    if back:
                        copy_hidden(tau - 1, (s - 1) % 3)
                    dve.wait_ge(s_si, tau + 1)
                    V.tensor_tensor(hid[s], sil[s], bank[2 + s][:, DE:2 * DE], ALU.mult).then_inc(s_hid, 1)
                    if back:
                        high(tau - 1, i, 0 if s else -1, (s - 1) % 3)

                def epilogue(n):
                    copy_hidden(n * 3 - 1, 2)
                    high(n * 3 - 1, n, -1, 2)
                def prologue():
                    dve.sem_inc(s_he, 1)
                    dve.sem_inc(s_yD, 1)
                rounds(dve, prologue, body, epilogue)

        with phase() as (mem, block):
            o = 0
            ya, yb, hh = [], [], []
            for lst in (ya, yb, hh):
                for _s in range(3):
                    a_, o = carve(o, D)
                    lst.append(a_)
            st = [mem.enter_context(nc.sbuf_tensor(f"ln2_st{s}", [P, 20], F32)) for s in range(3)]
            s_gb = [sem(f"f_gain_shift{n}") for n in range(2)]
            s_h = [sem(f"f_h{s}") for s in range(3)]
            s_ya = [sem(f"f_first_rows{s}") for s in range(3)]
            s_yb = [sem(f"f_second_rows{s}") for s in range(3)]
            s_w1 = sem("f_first_weighted")
            s_sum = sem("f_summed")
            s_v = sem("f_vector_chain")
            s_var = sem("f_variance")
            s_std = sem("f_std")
            s_nb = sem("f_bias")
            s_cen = sem("f_centred")
            s_gn = sem("f_gained")
            s_y = sem("f_output_ready")
            s_o = [sem(f"f_output_stored{s}") for s in range(3)]

            @block.sync
            def _(sp):
                sp.dma_start(gb[:, 0, :], bcast_rows(A["ln2_g"][0], P)).then_inc(s_gb[0], 16)
                sp.dma_start(gb[:, 1, :], bcast_rows(A["ln2_b"][0], P)).then_inc(s_gb[1], 16)

                def load(t):
                    if t >= 3:
                        sp.wait_ge(s_o[t % 3], 16 * (t // 3))
                    sp.dma_start(hh[t % 3], h_park[t * P:(t + 1) * P, :]).then_inc(s_h[t % 3], 16)
                for t in range(3):
                    load(t)
                yp = O["y_prompt"][0]
                for t in range(NT):
                    s = t % 3
                    sp.wait_ge(s_y, t + 1)
                    if t == 0:
                        sp.dma_start(yp[0:P - META, :], hh[s][META:P, :]).then_inc(s_o[s], 16)
                    elif t < NT - 1:
                        sp.dma_start(yp[t * P - META:(t + 1) * P - META, :], hh[s]).then_inc(s_o[s], 16)
                    else:
                        sp.dma_start(yp[t * P - META:SEQ, :], hh[s][0:META, :]).then_inc(s_o[s], 16)
                        sp.dma_start(O["y_sample"].rearrange("b t d -> (b t) d"),
                                     hh[s][META:META + NSA, :]).then_inc(s_o[s], 16)
                    if t + 3 < NT:
                        load(t + 3)
                for s in range(3):
                    sp.wait_ge(s_o[s], 16 * (NT // 3) + (16 if s == (NT - 1) % 3 else 0))

            @block.gpsimd
            def _(pool):
                G = nc.gpsimd

                def gather(t):
                    s = t % 3
                    rows = min(P, TOK - t * P)
                    if t >= 3:
                        pool.wait_ge(s_sum, 2 * (t - 2))
                    for c, (dst, sm_) in enumerate(((ya, s_ya), (yb, s_yb))):
                        G.indirect_dma_start(out=dst[s][0:rows, :], out_offset=None, in_=y_park,
                                             in_offset=bass.IndirectOffsetOnAxis(ap=slot_i[0:rows, t, c:c + 1], axis=0)
                                             ).then_inc(sm_[s], 16)
                for t in range(3):
                    gather(t)
                pool.wait_ge(s_gb[1], 16)
                for t in range(NT):
                    rows = min(P, TOK - t * P)
                    pool.wait_ge(s_gn, t + 1)
                    G.tensor_tensor(hh[t % 3][0:rows, :], hh[t % 3][0:rows, :], gb[0:rows, 1, :], ALU.add).then_inc(s_y, 1)
                    if t + 3 < NT:
                        gather(t + 3)

            @block.scalar
            def _(act):
                S = nc.scalar
                for t in range(NT + 1):
                    if t < NT:
                        s = t % 3
                        rows = slice(0, min(P, TOK - t * P))
                        act.wait_ge(s_ya[s], 16 * (t // 3 + 1))
                        S.activation(ya[s][rows, :], ya[s][rows, :], ACT.Copy, scale=wsel[rows, t, 0:1]).then_inc(s_w1, 1)
                    if t:
                        u, s = t - 1, (t - 1) % 3
                        rows = slice(0, min(P, TOK - u * P))
                        act.wait_ge(s_var, u + 1)
                        S.activation(st[s][rows, 15:16], st[s][rows, 14:15], ACT.Sqrt).then_inc(s_std, 1)
                        act.wait_ge(s_nb, u + 1)
                        S.activation(hh[s][rows, :], hh[s][rows, :], ACT.Identity, bias=st[s][rows, 17:18],
                                     scale=st[s][rows, 16:17]).then_inc(s_cen, 1)

            @block.vector
            def _(dve):
                V = nc.vector
                chain = Link(dve, s_v)
                dve.wait_ge(s_gb[0], 16)

                def gain(t):
                    s = t % 3
                    rows = slice(0, min(P, TOK - t * P))
                    dve.wait_ge(s_cen, t + 1)
                    V.tensor_tensor(hh[s][rows, :], hh[s][rows, :], gb[rows, 0, :], ALU.mult).then_inc(s_gn, 1)

                for t in range(NT):
                    s = t % 3
                    rows = slice(0, min(P, TOK - t * P))
                    dve.wait_ge(s_yb[s], 16 * (t // 3 + 1))
                    dve.wait_ge(s_w1, t + 1)
                    V.scalar_tensor_tensor(yb[s][rows, :], yb[s][rows, :], wsel[rows, t, 1:2], ya[s][rows, :],
                                           ALU.mult, ALU.add).then_inc(s_sum, 1)
                    dve.wait_ge(s_sum, 2 * t + 1)
                    dve.wait_ge(s_h[s], 16 * (t // 3 + 1))
                    V.scalar_tensor_tensor(hh[s][rows, :], hh[s][rows, :], ALPHA, yb[s][rows, :],
                                           ALU.mult, ALU.add).then_inc(s_sum, 1)
                    dve.wait_ge(s_sum, 2 * t + 2)
                    V.bn_stats(st[s][rows, 0:6], hh[s][rows, 0:512])
                    chain(V.bn_stats(st[s][rows, 6:12], hh[s][rows, 512:1024]))
                    chain(V.bn_aggr(st[s][rows, 12:14], st[s][rows, 0:12]))
                    V.tensor_scalar_add(st[s][rows, 14:15], st[s][rows, 13:14], EPS).then_inc(s_var, 1)
                    if t:
                        gain(t - 1)
                    dve.wait_ge(s_std, t + 1)
                    chain(V.reciprocal(st[s][rows, 16:17], st[s][rows, 15:16]))
                    V.tensor_scalar(st[s][rows, 17:18], st[s][rows, 12:13], st[s][rows, 16:17], -1.0,
                                    ALU.mult, ALU.mult).then_inc(s_nb, 1)
                gain(NT - 1)


_INS = ["x_prompt", "x_sample", "cache_k", "cache_v", "cache_logf", "page_table", "state_ssm_re", "state_ssm_im",
        "state_pool", "meta_tokens", "ln0_g", "ln0_b", "w_in", "b_forget", "ssm_lam_re", "ssm_lam_im",
        "ssm_log_dt", "ssm_b_re", "ssm_b_im", "ssm_c_re", "ssm_c_im", "ssm_d", "w_glu", "b_glu", "w_pool",
        "s_pool", "w_out", "ln1_g", "ln1_b", "w_router", "b_router", "w_gate", "w_up", "w_down", "ln2_g", "ln2_b"]
_OUTS = [("y_prompt", (1, SEQ, D)), ("y_sample", (BS, TS, D)),
         ("k_prompt", (1, 1, NPR, H, HD)), ("v_prompt", (1, 1, NPR, H, HD)), ("logf_prompt", (1, 1, NPR, H)),
         ("ssm_re_prompt", (1, 1, 16, 64)), ("ssm_im_prompt", (1, 1, 16, 64)), ("pool_prompt", (1, 1, PBUF, DPL)),
         ("k_sample", (BS, 1, TS, H, HD)), ("v_sample", (BS, 1, TS, H, HD)), ("logf_sample", (BS, 1, TS, H)),
         ("ssm_re_sample", (BS, 1, 16, 64)), ("ssm_im_sample", (BS, 1, 16, 64)), ("pool_sample", (BS, 1, PBUF, DPL))]


def kernel(**inputs):
    import numpy as _np
    import concourse.bacc as _bacc
    from concourse.bass_utils import run_bass_kernel_spmd as _run

    nc = _bacc.Bacc("TRN2", target_bir_lowering=False, num_devices=1)
    arrays, ins, outs = {}, {}, {}
    for name in _INS:
        a = _np.ascontiguousarray(inputs[name])
        arrays[f"in_{name}"] = a
        ins[name] = nc.dram_tensor(f"in_{name}", a.shape, mybir.dt.from_np(a.dtype), kind="ExternalInput").ap()
    for name, shape in _OUTS:
        outs[name] = nc.dram_tensor(f"out_{name}", shape, F32, kind="ExternalOutput").ap()
    hybrid_step(nc, ins, outs)
    r = _run(nc, [arrays], core_ids=[0])
    return tuple(r.results[0][f"out_{name}"] for name, _ in _OUTS)
```

```python
import math
from contextlib import ExitStack, contextmanager

import concourse.bass as bass
from concourse import mybir

F32 = mybir.dt.float32
I32 = mybir.dt.int32
ALU = mybir.AluOpType
ACT = mybir.ActivationFunctionType
AX = mybir.AxisListType.X

P = 128
D = 1024
KD = D // P
SEQ, META = 1024, 16
NPR = META + SEQ
BS, TS = 8, 8
NSA = BS * TS
TOK = NPR + NSA
NT = (TOK + P - 1) // P
TP = NT * P
H, HD = 8, 64
DA = H * HD
DS = DPL = D // 4
O_F, O_U = 3 * DA, 3 * DA + H
O_P = O_U + DS
DIN = O_P + DPL
PAGE, NPAGE, NPOOL = 128, 2, 20
PAST = PAGE * NPAGE
NPAIR = 8
L = 4
CH = TOK // L
CHP = NPR // L
CHS = CH - CHP
CHT = TP // L
PBUF = 15
E, EG, DE = 16, 4, 256
SLOTT = 2 * TOK // P + E
ALPHA = 2 ** 0.25
EPS = 1e-5
SCALE = HD ** -0.5
NEG = -1e30
CHUNKS = [(0, 384), (384, 384), (768, 384)]
CHUNKS_T = [(0, 384), (384, 384), (768, TOK - 768)]


class Link:

    def __init__(self, eng, sem):
        self.eng, self.sem, self.n = eng, sem, 0

    def __call__(self, ins):
        self.n += 1
        ins.then_inc(self.sem, 1)
        self.eng.wait_ge(self.sem, self.n)


def bcast_rows(ap, n):
    return ap.rearrange("(a w) -> a w", a=1).to_broadcast([n, ap.shape[0]])


SSMN = 64
AR = 21120
(LRE, LIM, LDT, DT, LRDT, LRDT4, MAG, MAG4, COS0, SIN0, KT, KT2, ANG, ANG2, COS, SIN,
 T0, T1, NR, DEN, GR, GI) = range(22)
ROUND = 1.5 * 2 ** 23
TURN_HI = 6.28125
TURN_LO = 2 * math.pi - TURN_HI
PI_IN = 3.1415925
ROUNDS = (SLOTT + 2) // 3
TT = 3 * ROUNDS + 3
LEAST = (2 * TOK + P - 1) // P + (-((2 * TOK + P - 1) // P)) % 3


def hybrid_step(nc, A, O):
    ctx = ExitStack()
    with ctx:
        def sb(name, shape, dt=F32):
            return ctx.enter_context(nc.sbuf_tensor(name, shape, dt))

        made = []

        def sem(name):
            made.append(nc.alloc_semaphore(name=name))
            return made[-1]

        @contextmanager
        def phase():
            made.clear()
            with ExitStack() as mem:
                with nc.Block() as block:
                    yield mem, block
            nc.clear_and_free_semaphores(list(made))
            nc.all_engine_barrier()

        duo = [ctx.enter_context(nc.psum_tensor(f"banks{2 * i}_{2 * i + 1}", [P, 1024], F32)) for i in range(4)]
        bank = [duo[i // 2][:, 512 * (i % 2):512 * (i % 2) + 512] for i in range(8)]
        score_slot = duo[0:2]

        ctx.enter_context(nc.allow_non_contiguous_dma(reason="small parameter vectors"))

        ident = sb("ident", [P, P])
        causal = sb("causal", [P, P])
        xT = sb("xT", [P, KD, TP])
        mixT = sb("mixT", [P, KD, TP])
        v_tok = sb("v_tok", [P, NT, DA])
        gb = sb("gb", [P, 2, D])
        cum = sb("cum", [H, TP])
        ncum = sb("ncum", [H, TP])
        qs_T = sb("qs_T", [P, H // 2, NSA])
        ks_T = sb("ks_T", [P, H // 2, NSA])
        ones_col = sb("ones_col", [P, 1])
        arena = sb("arena", [P, AR])

        x_park = nc.dram_tensor("x_park", (NT, P, D), F32).ap()
        h_park = nc.dram_tensor("h_park", (TP, D), F32).ap()
        gate_sums = nc.dram_tensor("gate_sums", (2, H, TP), F32).ap()
        slot_tok = nc.dram_tensor("slot_tok", (SLOTT * P, 1), I32).ap()
        y_park = nc.dram_tensor("y_park", (SLOTT * P, D), F32).ap()

        LINE = PBUF + NPR + BS * (PBUF + TS)

        def carve(at, *shape, names=""):
            n = math.prod(shape)
            return arena[:, at:at + n], at + n

        o = 0
        a_, o = carve(o, 2, TP)
        uT = a_.rearrange("p (m t) -> p m t", m=2)
        a_, o = carve(o, NPAIR, CH)
        U4_flat = a_
        U4 = a_.rearrange("p (q c) -> p q c", q=NPAIR)
        a_, o = carve(o, 2, LINE)
        line = a_.rearrange("p (m n) -> p m n", m=2)
        a_, o = carve(o, 2, NPAIR, CHP)
        Etab = a_.rearrange("p (r q c) -> p r q c", r=2, q=NPAIR)
        at_XS = o
        a_, o = carve(o, 2, NPAIR, CHP + 4)
        XS = a_.rearrange("p (r q c) -> p r q c", r=2, q=NPAIR)
        at_CA = o
        a_, o = carve(o, 2, NPAIR, (L + 1) * 32)
        CA = a_.rearrange("p (r q n) -> p r q n", r=2, q=NPAIR)
        a_, o = carve(o, NPAIR, 2, P)
        WT = a_.rearrange("p (q r n) -> p q r n", q=NPAIR, r=2)
        a_, o = carve(o, NPAIR, P)
        Tm = a_.rearrange("p (q n) -> p q n", q=NPAIR)
        assert o <= AR
        Wbd = arena[:, at_XS:at_XS + 2 * NPAIR * L * 32].rearrange("p (r q n) -> p r q n", r=2, q=NPAIR)
        prod = [arena[:, at_XS + 2048 + 640 * n:at_XS + 2048 + 640 * (n + 1)] for n in range(2)]
        vflat = v_tok[:, :, :].rearrange("p t n -> p (t n)")
        w_u = vflat[:, 0:KD * DS].rearrange("p (k n) -> p k n", k=KD)
        w_p = vflat[:, KD * DS:2 * KD * DS].rearrange("p (k n) -> p k n", k=KD)
        mflat = mixT[:, 4:8, :].rearrange("p k t -> p (k t)")
        w_v = mixT[:, 0:4, :].rearrange("p k t -> p (k t)")[:, 0:KD * DA].rearrange("p (k n) -> p k n", k=KD)
        Sin = mflat[:, 0:2 * NPAIR * CH].rearrange("p (r q c) -> p r q c", r=2, q=NPAIR)
        Zs = mflat[:, 0:2 * NPAIR * CHP].rearrange("p (r q c) -> p r q c", r=2, q=NPAIR)

        par = sb("par", [P, 40, NPAIR])
        pw = sb("pw", [P, 2, L + 1, NPAIR])
        wback = sb("wback", [P, 2, L, NPAIR])
        x0 = sb("x0", [P, 2, BS, NPAIR])
        finals = sb("finals", [P, 2, BS + 1, NPAIR])
        en = sb("en", [P, 6, NPAIR])
        Braw = sb("Braw", [P, 2, NPAIR, 16])
        Bbar = sb("Bbar", [P, 2, NPAIR, 16])
        Craw = sb("Craw", [P, 2, NPAIR, 16])
        dcol = sb("dcol", [P, NPAIR])

        with phase() as (mem, block):
            def tmp(name, shape):
                return mem.enter_context(nc.sbuf_tensor(name, shape, F32))
            XSL = 6
            xin = ([mixT[:, :, :].rearrange("p k t -> p (k t)")[:, D * s:D * (s + 1)] for s in range(4)]
                   + [U4_flat[:, D * s:D * (s + 1)] for s in range(2)])
            st = [tmp(f"ln0_st{s}", [P, 20]) for s in range(XSL)]
            w_f = tmp("w_f", [P, KD, H])
            bf = tmp("bf", [P, H])
            lf = mflat[0:H, 0:TP]
            stack1 = tmp("stack1", [16, P])
            ldt = tmp("ldt", [NPAIR, 2])
            ldtx = tmp("ldtx", [NPAIR, P])
            stack2 = tmp("stack2", [P, P])
            cstage = tmp("cstage", [P, 2, 2, SSMN])
            hist = tmp("hist", [BS * PBUF, DPL])
            lfT = tmp("lfT", [P, NT, H])
            soft = tmp("soft", [P, NT, H])

            s_ids = sem("n_ident_steps")
            s_gain = sem("n_gain_loaded")
            s_shift = sem("n_shift_loaded")
            s_xa = [sem(f"n_rows_low{s}") for s in range(XSL)]
            s_xb = [sem(f"n_rows_high{s}") for s in range(XSL)]
            s_st = sem("n_vector_chain")
            s_var = sem("n_var_ready")
            s_std = sem("n_std_ready")
            s_nb = sem("n_bias_ready")
            s_cen = sem("n_centred")
            s_gained = sem("n_gained")
            s_normed = sem("n_normed")
            s_turned = sem("n_turned_half")
            s_copied = sem("n_xT_copied")
            s_stored = [sem(f"n_x_parked{s}") for s in range(XSL)]
            s_pc = sem("n_pool_chain")
            s_ld = {n: sem("m_loaded_" + n) for n in
                    ("wf", "wu", "wp", "bf", "lre", "lim", "ldt", "xre", "xim", "bre", "bim", "cre", "cim",
                     "d0", "d1", "d2", "d3", "hist")}
            s_mm = sem("m_chunk_projected")
            s_free = sem("m_bank_emptied")
            s_tr = sem("m_param_turned")
            s_v = sem("m_param_chain")
            s_a = sem("m_scalar_chain")
            s_par = sem("m_params_copied")
            s_x = sem("m_for_scalar")
            s_f = sem("m_forget_projected")
            s_z = sem("m_forget_logits")
            s_sp = sem("m_softplus")
            s_lf = sem("m_log_gates")
            s_lft = sem("m_log_gates_turned")
            s_lfc = sem("m_log_gates_copied")
            s_o1 = sem("m_out_logf_a")
            s_o2 = sem("m_out_logf_b")
            s_o3 = sem("m_out_logf_c")
            s_o4 = sem("m_sums_parked")
            s_o5 = sem("m_negated_sums_parked")
            s_pm = sem("m_pool_cleared")
            s_cum = sem("m_cum_ready")

            w_in = A["w_in"][0].rearrange("(k p) n -> p k n", p=P)
            UNITS = [("wu", w_u, 0), ("wu", w_u, 1), ("wp", w_p, 0), ("wp", w_p, 1)]

            @block.sync
            def _(sp):
                def ld(key, dst, src):
                    sp.dma_start(dst, src).then_inc(s_ld[key], 16)

                def load(t):
                    s, xp = t % XSL, A["x_prompt"][0]
                    if t >= XSL:
                        sp.wait_ge(s_stored[s], 16 * (t // XSL))
                        sp.wait_ge(s_turned, 2 * (t - XSL + 1))
                    if t == 0:
                        sp.dma_start(xin[s][0:META, :], A["meta_tokens"]).then_inc(s_xa[s], 16)
                    else:
                        sp.dma_start(xin[s][0:META, :], xp[t * P - META:t * P, :]).then_inc(s_xa[s], 16)
                    if t < NT - 1:
                        sp.dma_start(xin[s][META:P, :], xp[t * P:(t + 1) * P - META, :]).then_inc(s_xb[s], 16)
                    else:
                        sp.dma_start(xin[s][META:META + NSA, :],
                                     A["x_sample"].rearrange("b t d -> (b t) d")).then_inc(s_xb[s], 16)

                load(0)
                sp.dma_start(gb[:, 0, :], bcast_rows(A["ln0_g"], P)).then_inc(s_gain, 16)
                sp.dma_start(gb[:, 1, :], bcast_rows(A["ln0_b"], P)).then_inc(s_shift, 16)
                ld("ldt", ldt[:, :], A["ssm_log_dt"][0].rearrange("(q g) -> q g", g=2))
                ld("lre", stack1[0:8, :], A["ssm_lam_re"][0].rearrange("(q g) p -> q (g p)", g=2))
                ld("lim", stack1[8:16, :], A["ssm_lam_im"][0].rearrange("(q g) p -> q (g p)", g=2))
                load(1)
                ld("xre", stack2[0:64, :], A["state_ssm_re"].rearrange("b l (q g) p -> (b l q) (g p)", g=2))
                ld("xim", stack2[64:128, :], A["state_ssm_im"].rearrange("b l (q g) p -> (b l q) (g p)", g=2))
                ld("cre", cstage[:, :, 0, :], A["ssm_c_re"][0].rearrange("(h g) c p -> (g c) h p", h=2))
                ld("cim", cstage[:, :, 1, :], A["ssm_c_im"][0].rearrange("(h g) c p -> (g c) h p", h=2))
                load(2)
                load(3)
                ld("wf", w_f[:, :, :], w_in[:, :, O_F:O_F + H])
                ld("wu", w_u, w_in[:, :, O_U:O_U + DS])
                ld("bf", bf[:, :], bcast_rows(A["b_forget"][0], P))
                ld("hist", hist[:, :], A["state_pool"].rearrange("b l r c -> (b l r) c"))
                ld("wp", w_p, w_in[:, :, O_P:O_P + DPL])
                ld("bre", Braw[:, 0, :, :], A["ssm_b_re"][0].rearrange("(q g) p c -> (g p) q c", g=2))
                ld("bim", Braw[:, 1, :, :], A["ssm_b_im"][0].rearrange("(q g) p c -> (g p) q c", g=2))
                load(4)
                load(5)
                for j in range(L):
                    ld(f"d{j}", dcol[32 * j:32 * j + 32, :], A["ssm_d"][0].rearrange("(q r) -> r q", r=32))
                for t in range(NT):
                    sp.wait_ge(s_normed, t + 1)
                    sp.dma_start(x_park[t], xin[t % XSL]).then_inc(s_stored[t % XSL], 16)
                    if t + XSL < NT:
                        load(t + XSL)
                sp.wait_ge(s_lf, 1)
                sp.dma_start(O["logf_prompt"][0, 0, 0:8 * P, :].rearrange("(t p) h -> p t h", p=P),
                             lfT[:, 0:8, :]).then_inc(s_o1, 16)
                sp.dma_start(O["logf_prompt"][0, 0, 8 * P:NPR, :], lfT[0:META, 8, :]).then_inc(s_o2, 16)
                sp.dma_start(O["logf_sample"].rearrange("b l t h -> (b l t) h"),
                             lfT[META:META + NSA, 8, :]).then_inc(s_o3, 16)
                sp.wait_ge(s_cum, 2)
                sp.dma_start(gate_sums[0], cum[:, :]).then_inc(s_o4, 16)
                sp.dma_start(gate_sums[1], ncum[:, :]).then_inc(s_o5, 16)
                for s in range(XSL):
                    sp.wait_ge(s_stored[s], 16 * len(range(s, NT, XSL)))
                for s in (s_o1, s_o2, s_o3, s_o4, s_o5):
                    sp.wait_ge(s, 16)

            def by_chunk(engine, m):
                for q in range(4):
                    for j in range(L):
                        engine.tensor_copy(
                            U4[32 * j:32 * j + 32, 4 * m + q, :],
                            uT[32 * q:32 * q + 32, m, 0:TOK].rearrange("p (c j) -> p c j", j=L)[:, :, j])

            @block.gpsimd
            def _(pool):
                G = nc.gpsimd
                chain = Link(pool, s_pc)
                chain(G.memset(ident[:, :], 0.0))
                chain(G.affine_select(out=ident[:, :], in_=ident[:, :], compare_op=ALU.not_equal, fill=1.0,
                                      base=0, pattern=[[-1, P]], channel_multiplier=1))
                pool.sem_inc(s_ids, 1)
                chain(G.memset(causal[:, :], 0.0))
                chain(G.affine_select(out=causal[:, :], in_=causal[:, :], compare_op=ALU.is_ge, fill=NEG,
                                      base=0, pattern=[[-1, P]], channel_multiplier=1))
                G.memset(ones_col[:, :], 1.0)
                pool.wait_ge(s_shift, 16)

                for t in range(NT):
                    pool.wait_ge(s_gained, t + 1)
                    G.tensor_tensor(xin[t % XSL], xin[t % XSL], gb[:, 1, :], ALU.add).then_inc(s_normed, 1)
                    if t < 4:
                        G.memset((Wbd, CA, Tm, line[:, :, 0:PBUF])[t], 0.0).then_inc(s_pm, 1)
                pool.wait_ge(s_free, 4 * 2 + 1)
                for s in (4, 5):
                    pool.wait_ge(s_stored[s], 16)
                by_chunk(G, 0)

            @block.tensor
            def _(pe):
                T = nc.tensor

                def turn_x(t):
                    pe.wait_ge(s_normed, t + 1)
                    for half in range(2):
                        if t >= 1:
                            pe.wait_ge(s_copied, 2 * t - 1 + half)
                        for k in range(4):
                            kk = 4 * half + k
                            last = T.transpose(bank[half][:, k * P:(k + 1) * P],
                                               xin[t % XSL][:, kk * P:(kk + 1) * P], ident[:, :])
                        last.then_inc(s_turned, 1)

                def project(c, u):
                    key, w, m = UNITS[u]
                    n = 4 * c + u
                    c0, cn = CHUNKS[c]
                    if c == 0:
                        pe.wait_ge(s_ld[key], 16)
                    if u == 0:
                        pe.wait_ge(s_copied, 6 * c + 6)
                    if n >= 2:
                        pe.wait_ge(s_free, n - 1)
                    for k in range(KD):
                        last = T.matmul(bank[2 + n % 2][:, 0:cn], w[:, k, m * P:(m + 1) * P],
                                        xT[:, k, c0:c0 + cn], start=(k == 0), stop=(k == KD - 1))
                    last.then_inc(s_mm, 1)

                def forget(c):
                    if c == 0:
                        pe.wait_ge(s_ld["wf"], 16)
                        pe.wait_ge(s_x, 1)
                    for t in range(3 * c, 3 * c + 3):
                        for k in range(KD):
                            last = T.matmul(bank[4][:, t * H:(t + 1) * H], xT[:, k, t * P:(t + 1) * P], w_f[:, k, :],
                                            start=(k == 0), stop=(k == KD - 1))
                    last.then_inc(s_f, 1)

                pe.wait_ge(s_ids, 1)
                for k in ("lre", "lim"):
                    pe.wait_ge(s_ld[k], 16)
                T.transpose(bank[4][:, 0:16], stack1[:, :], ident[0:16, 0:16])
                pe.wait_ge(s_v, 1)
                T.transpose(bank[4][:, 16:24], ldtx[:, :], ident[0:8, 0:8]).then_inc(s_tr, 1)
                for k in ("xre", "xim"):
                    pe.wait_ge(s_ld[k], 16)
                T.transpose(bank[6][:, 0:P], stack2[:, :], ident[:, :]).then_inc(s_tr, 1)
                for k in ("cre", "cim"):
                    pe.wait_ge(s_ld[k], 16)
                for n in range(4):
                    last = T.transpose(bank[5][0:SSMN, n * P:(n + 1) * P], cstage[:, n // 2, n % 2, :], ident[:, :])
                last.then_inc(s_tr, 1)
                turn_x(0)
                turn_x(1)
                pe.wait_ge(s_ld["hist"], 16)
                for m2 in range(2):
                    last = T.transpose(bank[7][:, m2 * P:m2 * P + BS * PBUF], hist[:, m2 * P:(m2 + 1) * P],
                                       ident[0:BS * PBUF, 0:BS * PBUF])
                last.then_inc(s_tr, 1)
                turn_x(2)
                for c in range(1, 3):
                    turn_x(3 * c)
                    project(c - 1, 0)
                    forget(c - 1)
                    turn_x(3 * c + 1)
                    project(c - 1, 1)
                    turn_x(3 * c + 2)
                    project(c - 1, 2)
                    project(c - 1, 3)
                pe.wait_ge(s_copied, 2 * NT)
                forget(2)
                for u in range(3):
                    project(2, u)
                pe.wait_ge(s_lf, 1)
                for t in range(NT):
                    last = T.transpose(bank[(0, 1, 5)[t // 4]][0:H, (t % 4) * P:(t % 4 + 1) * P], lfT[:, t, :], ident[:, :])
                last.then_inc(s_lft, 1)
                project(2, 3)

            @block.scalar
            def _(act):
                S = nc.scalar
                chain = Link(act, s_a)

                def centre(t):
                    s = t % XSL
                    act.wait_ge(s_var, t + 1)
                    S.activation(st[s][:, 15:16], st[s][:, 14:15], ACT.Sqrt).then_inc(s_std, 1)
                    act.wait_ge(s_nb, t + 1)
                    S.activation(xin[s], xin[s], ACT.Identity, bias=st[s][:, 17:18],
                                 scale=st[s][:, 16:17]).then_inc(s_cen, 1)

                def copy_out(t):
                    for half in range(2):
                        act.wait_ge(s_turned, 2 * t + half + 1)
                        S.copy(xT[:, 4 * half:4 * half + 4, t * P:(t + 1) * P],
                               bank[half][:, :].rearrange("p (k t) -> p k t", k=4)).then_inc(s_copied, 1)

                def take(c, u):
                    n = 4 * c + u
                    act.wait_ge(s_mm, n + 1)
                    m, (c0, cn) = UNITS[u][2], CHUNKS[c]
                    src = bank[2 + n % 2]
                    if u < 2:
                        S.copy(uT[:, m, c0:c0 + cn], src[:, 0:cn]).then_inc(s_free, 1)
                        return
                    pn = min(cn, NPR - c0)
                    ins = S.copy(line[:, m, PBUF + c0:PBUF + c0 + pn], src[:, 0:pn])
                    if c0 + cn > NPR:
                        ins = S.copy(
                            line[:, m, PBUF + NPR:LINE].rearrange("p (b r) -> p b r", b=BS)[:, :, PBUF:PBUF + TS],
                            src[:, pn:pn + NSA].rearrange("p (b r) -> p b r", b=BS))
                    ins.then_inc(s_free, 1)

                for t in range(NT):
                    centre(t)
                    if t == 1:
                        act.wait_ge(s_x, 1)
                        chain(S.activation(par[:, DT, :], par[:, LDT, :], ACT.Exp))
                    if t == 3:
                        act.wait_ge(s_x, 3)
                        chain(S.activation(par[:, MAG:MAG + 2, :], par[:, LRDT:LRDT + 2, :], ACT.Exp))
                        chain(S.activation(par[:, COS:COS + 2, :], par[:, ANG:ANG + 2, :], ACT.Sin))
                    if t >= 1:
                        copy_out(t - 1)
                    if t >= 4:
                        c, u = (t - 4) // 3, (t - 4) % 3
                        take(c, u)
                        if u == 2:
                            take(c, 3)
                copy_out(NT - 1)
                take(1, 2)
                take(1, 3)
                take(2, 0)
                take(2, 1)
                act.wait_ge(s_z, 1)
                chain(S.activation(soft[:, :, :], lfT[:, :, :], ACT.Abs))
                chain(S.activation(soft[:, :, :], soft[:, :, :], ACT.Exp, scale=-1.0))
                chain(S.activation(soft[:, :, :], soft[:, :, :], ACT.Ln, bias=1.0))
                take(2, 2)
                take(2, 3)

            @block.vector
            def _(dve):
                V = nc.vector
                chain = Link(dve, s_v)
                link = Link(dve, s_st)

                def stats(t):
                    s = t % XSL
                    dve.wait_ge(s_xa[s], 16 * (t // XSL) + 16)
                    dve.wait_ge(s_xb[s], 16 * (t // XSL) + 16)
                    V.bn_stats(st[s][:, 0:6], xin[s][:, 0:512])
                    link(V.bn_stats(st[s][:, 6:12], xin[s][:, 512:1024]))
                    link(V.bn_aggr(st[s][:, 12:14], st[s][:, 0:12]))
                    V.tensor_scalar_add(st[s][:, 14:15], st[s][:, 13:14], EPS).then_inc(s_var, 1)

                def centre(t):
                    s = t % XSL
                    dve.wait_ge(s_std, t + 1)
                    link(V.reciprocal(st[s][:, 16:17], st[s][:, 15:16]))
                    V.tensor_scalar(st[s][:, 17:18], st[s][:, 12:13], st[s][:, 16:17], -1.0,
                                    ALU.mult, ALU.mult).then_inc(s_nb, 1)

                def gain(t):
                    s = t % XSL
                    dve.wait_ge(s_cen, t + 1)
                    V.tensor_tensor(xin[s], xin[s], gb[:, 0, :], ALU.mult).then_inc(s_gained, 1)

                def mul(o_, a, b, last=None):
                    chain(V.tensor_tensor(o_, a, b, ALU.mult))

                def p_(i, n=1):
                    return par[:, i, :] if n == 1 else par[:, i:i + n, :]

                def cmul(outr, outi, ar, ai, br, bi, t0, t1):
                    V.tensor_tensor(t0, ar, br, ALU.mult)
                    chain(V.tensor_tensor(t1, ai, bi, ALU.mult))
                    chain(V.tensor_tensor(outr, t0, t1, ALU.subtract))
                    V.tensor_tensor(t0, ar, bi, ALU.mult)
                    chain(V.tensor_tensor(t1, ai, br, ALU.mult))
                    chain(V.tensor_tensor(outi, t0, t1, ALU.add))

                def parameters():
                    dve.wait_ge(s_ld["ldt"], 16)
                    chain(V.tensor_copy(ldtx[:, :].rearrange("q (g p) -> q g p", g=2),
                                        ldt[:, :].unsqueeze(2).to_broadcast([NPAIR, 2, SSMN])))
                    dve.wait_ge(s_tr, 1)
                    V.tensor_copy(par[:, LRE:LRE + 3, :], bank[4][:, 0:24].rearrange("p (a q) -> p a q", a=3)).then_inc(s_x, 1)
                    dve.wait_ge(s_tr, 2)
                    V.tensor_copy(x0[:, :, :, :].rearrange("p r b q -> p (r b q)"), bank[6][:, 0:P]).then_inc(s_par, 1)
                    dve.wait_ge(s_tr, 3)
                    for h in range(2):
                        for r in range(2):
                            n = 2 * h + r
                            for g in range(2):
                                ins = V.tensor_copy(
                                    Craw[64 * g:64 * g + 64, r, 4 * h:4 * h + 4, :],
                                    bank[5][0:SSMN, n * P:(n + 1) * P].rearrange("p (q g c) -> p q g c", q=4, g=2)[:, :, g, :])
                    chain(ins)

                def angles():
                    dve.wait_ge(s_a, 1)
                    mul(p_(LRDT), p_(LRE), p_(DT))
                    V.tensor_scalar(p_(LRDT4), p_(LRDT), float(L), None, ALU.mult).then_inc(s_x, 1)
                    mul(p_(SIN0), p_(LIM), p_(DT))
                    chain(V.tensor_scalar(p_(COS0), p_(SIN0), math.pi / 2, None, ALU.add))
                    V.tensor_scalar(p_(KT, 2), p_(COS0, 2), 1.0 / (2 * math.pi), ROUND, ALU.mult, ALU.add)
                    chain(V.tensor_copy(p_(ANG, 2), p_(COS0, 2)))
                    chain(V.tensor_scalar(p_(KT, 2), p_(KT, 2), ROUND, None, ALU.subtract))
                    chain(V.scalar_tensor_tensor(p_(ANG, 2), p_(KT, 2), -TURN_HI, p_(ANG, 2), ALU.mult, ALU.add))
                    chain(V.scalar_tensor_tensor(p_(ANG, 2), p_(KT, 2), -TURN_LO, p_(ANG, 2), ALU.mult, ALU.add))
                    V.tensor_scalar(p_(ANG, 2), p_(ANG, 2), PI_IN, -PI_IN, ALU.min, ALU.max).then_inc(s_x, 1)

                def powers():
                    V.memset(pw[:, 0, 0, :], 1.0)
                    V.memset(Etab[:, 0, :, 0:1], 1.0)
                    V.memset(Etab[:, 1, :, 0:1], 0.0)
                    chain(V.memset(pw[:, 1, 0, :], 0.0))
                    dve.wait_ge(s_a, 3)
                    V.tensor_tensor(pw[:, 0, 1, :], p_(MAG), p_(COS), ALU.mult)
                    mul(pw[:, 1, 1, :], p_(MAG), p_(SIN))
                    for k in range(2, L + 1):
                        cmul(pw[:, 0, k, :], pw[:, 1, k, :], pw[:, 0, k - 1, :], pw[:, 1, k - 1, :],
                             pw[:, 0, 1, :], pw[:, 1, 1, :], p_(T0), p_(T1))
                    for j in range(L):
                        ins = V.tensor_copy(wback[:, :, j, :], pw[:, :, L - 1 - j, :])
                    chain(ins)

                def input_gain():
                    V.tensor_scalar(p_(NR), pw[:, 0, 1, :], -1.0, None, ALU.add)
                    V.tensor_tensor(p_(T0), p_(LRE), p_(LRE), ALU.mult)
                    mul(p_(T1), p_(LIM), p_(LIM))
                    chain(V.tensor_tensor(p_(T0), p_(T0), p_(T1), ALU.add))
                    chain(V.reciprocal(p_(DEN), p_(T0)))
                    V.tensor_tensor(p_(T0), p_(NR), p_(LRE), ALU.mult)
                    mul(p_(T1), pw[:, 1, 1, :], p_(LIM))
                    chain(V.tensor_tensor(p_(GR), p_(T0), p_(T1), ALU.add))
                    V.tensor_tensor(p_(T0), pw[:, 1, 1, :], p_(LRE), ALU.mult)
                    mul(p_(T1), p_(NR), p_(LIM))
                    chain(V.tensor_tensor(p_(GI), p_(T0), p_(T1), ALU.subtract))
                    V.tensor_tensor(p_(GR), p_(GR), p_(DEN), ALU.mult)
                    mul(p_(GI), p_(GI), p_(DEN))

                def input_matrix():
                    for k in ("bre", "bim"):
                        dve.wait_ge(s_ld[k], 16)

                    def over_c(x, *shape):
                        return x.unsqueeze(2).to_broadcast([P, NPAIR, 16])

                    pr = [t[:, 0:NPAIR * 16].rearrange("p (q c) -> p q c", q=NPAIR) for t in prod]
                    cmul(Bbar[:, 0, :, :], Bbar[:, 1, :, :], over_c(p_(GR)), over_c(p_(GI)),
                         Braw[:, 0, :, :], Braw[:, 1, :, :], pr[0], pr[1])

                def block_matrices():
                    dve.wait_ge(s_pm, 4)
                    for (powers, nk, base, dst, sign_im) in ((wback, L, Bbar, Wbd, 1), (pw, L + 1, Craw, CA, -1)):
                        pr = [t[:, 0:NPAIR * nk * 16].rearrange("p (q k c) -> p q k c", q=NPAIR, k=nk) for t in prod]

                        def power(r):
                            x = powers[:, r, :, :].rearrange("p k q -> p q k")
                            return x.unsqueeze(3).to_broadcast([P, NPAIR, nk, 16])

                        def per_c(r):
                            return base[:, r, :, :].unsqueeze(2).to_broadcast([P, NPAIR, nk, 16])

                        for r in range(2):
                            V.tensor_tensor(pr[0], power(0), per_c(r), ALU.mult)
                            chain(V.tensor_tensor(pr[1], power(1), per_c(1 - r), ALU.mult))
                            if r == 1 and sign_im < 0:
                                chain(V.tensor_scalar(pr[0], pr[0], -1.0, None, ALU.mult))
                            for g in range(2):
                                sl = slice(64 * g, 64 * g + 64)
                                out = dst[:, r, :, :].rearrange("p q (k n) -> p q k n", k=nk)
                                ins = V.tensor_tensor(out[sl, :, :, 16 * g:16 * g + 16], pr[0][sl], pr[1][sl],
                                                      ALU.add if r == 1 and sign_im > 0 else ALU.subtract)
                            chain(ins)

                def turns():
                    cmul(en[:, 0, :], en[:, 1, :], p_(COS), p_(SIN), p_(COS), p_(SIN), en[:, 4, :], en[:, 5, :])
                    cmul(en[:, 2, :], en[:, 3, :], en[:, 0, :], en[:, 1, :], en[:, 0, :], en[:, 1, :],
                         en[:, 4, :], en[:, 5, :])
                    n, cur = 1, 2
                    while n < CHP:
                        m = min(n, CHP - n)
                        cr = en[:, cur, :].unsqueeze(2).to_broadcast([P, NPAIR, m])
                        ci = en[:, cur + 1, :].unsqueeze(2).to_broadcast([P, NPAIR, m])
                        sc = [Zs[:, r, :, 0:m] for r in range(2)]
                        cmul(Etab[:, 0, :, n:n + m], Etab[:, 1, :, n:n + m], Etab[:, 0, :, 0:m], Etab[:, 1, :, 0:m],
                             cr, ci, sc[0], sc[1])
                        nxt = 2 - cur
                        cmul(en[:, nxt, :], en[:, nxt + 1, :], en[:, cur, :], en[:, cur + 1, :],
                             en[:, cur, :], en[:, cur + 1, :], en[:, 4, :], en[:, 5, :])
                        n, cur = n + m, nxt

                def history():
                    dve.wait_ge(s_tr, 4)
                    for m in range(2):
                        ins = V.tensor_copy(
                            line[:, m, PBUF + NPR:LINE].rearrange("p (b r) -> p b r", b=BS)[:, :, 0:PBUF],
                            bank[7][:, m * P:m * P + BS * PBUF].rearrange("p (b r) -> p b r", b=BS))

                stats(0)
                dve.wait_ge(s_gain, 16)
                for t in range(NT):
                    if t == 0:
                        parameters()
                    centre(t)
                    if t + 1 < NT:
                        stats(t + 1)
                    gain(t)
                    if t == 2:
                        angles()
                    if t == 4:
                        powers()
                    if t == 5:
                        input_gain()
                    if t == 6:
                        input_matrix()
                        history()
                    if t == 7:
                        block_matrices()
                turns()
                dve.wait_ge(s_ld["bf"], 16)
                dve.wait_ge(s_f, 3)
                V.tensor_tensor(lfT[:, :, :], bank[4][:, 0:NT * H].rearrange("p (t h) -> p t h", t=NT),
                                bf[:, :].unsqueeze(1).to_broadcast([P, NT, H]), ALU.add).then_inc(s_z, 1)
                dve.wait_ge(s_a, 6)
                V.scalar_tensor_tensor(lfT[:, :, :], lfT[:, :, :], 0.0, soft[:, :, :], ALU.min,
                                       ALU.subtract).then_inc(s_lf, 1)
                dve.wait_ge(s_lft, 1)
                for n in range(2):
                    V.tensor_copy(lf[:, 512 * n:512 * n + 512], bank[n][0:H, :])
                V.tensor_copy(lf[:, 1024:TP], bank[5][0:H, 0:TP - 1024]).then_inc(s_cum, 1)
                dve.wait_ge(s_cum, 1)
                V.tensor_copy(cum[:, NPR:TP], lf[:, NPR:TP])
                V.tensor_copy(ncum[:, NPR:TP], lf[:, NPR:TP])
                V.tensor_tensor_scan(cum[:, 0:NPR], ones_col[0:H, :].to_broadcast([H, NPR]), lf[:, 0:NPR],
                                     0.0, ALU.mult, ALU.add).then_inc(s_lfc, 1)
                dve.wait_ge(s_lfc, 1)
                V.tensor_scalar(ncum[:, 0:NPR], cum[:, 0:NPR], -1.0, None, ALU.mult).then_inc(s_cum, 1)
                dve.wait_ge(s_free, 4 * 2 + 2)
                for s in (4, 5):
                    dve.wait_ge(s_stored[s], 16)
                by_chunk(V, 1)

        XI = sb("XI", [P, 2, NPAIR, CHS])

        with phase() as (mem, block):
            fin_t = mem.enter_context(nc.sbuf_tensor("fin_t", [(BS + 1) * NPAIR, 2, P], F32))
            s_wv = sem("s_values_weights")
            s_wt = sem("s_W_turned")
            s_wc = sem("s_W_copied")
            s_tb = sem("s_T_built")
            s_tc = sem("s_T_ready")
            s_in = sem("s_inputs_summed")
            s_ic = sem("s_inputs_copied")
            s_v = sem("s_vector_chain")
            s_xs = sem("s_states_ready")
            s_fi = sem("s_finals_ready")
            s_y = sem("s_outputs_summed")
            s_ge = sem("s_gelu_done")
            s_ft = sem("s_finals_turned")
            s_fc = sem("s_finals_copied")
            s_o = [sem(f"s_out_state{n}") for n in range(4)]
            s_vm = sem("s_values_projected")
            s_vc = sem("s_values_copied")
            s_vo = [sem(f"s_out_values{n}") for n in range(5)]
            V_PARTS = ((0, 3), (3, 6), (6, 8))
            V_EARLY = 6
            V_AFTER = {3: 6, 5: 7, 7: 8}

            @block.sync
            def _(sp):
                sp.dma_start(w_v, A["w_in"][0].rearrange("(k p) n -> p k n", p=P)[:, :, 2 * DA:3 * DA]).then_inc(s_wv, 16)
                vp = O["v_prompt"][0, 0].rearrange("t h d -> t (h d)")
                for n, (t0, t1) in enumerate(V_PARTS):
                    sp.wait_ge(s_vc, t1)
                    sp.dma_start(vp[t0 * P:t1 * P, :].rearrange("(t p) n -> p t n", p=P),
                                 v_tok[:, t0:t1, :]).then_inc(s_vo[n], 16)
                sp.wait_ge(s_vc, NT)
                sp.dma_start(vp[8 * P:NPR, :], v_tok[0:META, 8, :]).then_inc(s_vo[3], 16)
                sp.dma_start(O["v_sample"].rearrange("b l t h d -> (b l t) (h d)"),
                             v_tok[META:META + NSA, 8, :]).then_inc(s_vo[4], 16)
                sp.wait_ge(s_fc, 1)
                for r, nm in enumerate(("re", "im")):
                    sp.dma_start(O[f"ssm_{nm}_prompt"][0, 0].rearrange("(q g) p -> q (g p)", g=2),
                                 fin_t[0:NPAIR, r, :]).then_inc(s_o[r], 16)
                    sp.dma_start(O[f"ssm_{nm}_sample"].rearrange("b l (q g) p -> (b l q) (g p)", g=2),
                                 fin_t[NPAIR:(BS + 1) * NPAIR, r, :]).then_inc(s_o[2 + r], 16)
                for s in s_o:
                    sp.wait_ge(s, 16)
                for s in s_vo:
                    sp.wait_ge(s, 16)

            @block.tensor
            def _(pe):
                def values(t):
                    if t >= 4:
                        pe.wait_ge(s_vc, t - 3)
                    for k in range(KD):
                        last = nc.tensor.matmul(bank[t % 4][:, :], xT[:, k, t * P:(t + 1) * P], w_v[:, k, :],
                                                start=(k == 0), stop=(k == KD - 1))
                    last.then_inc(s_vm, 1)

                for q in range(NPAIR):
                    for r in range(2):
                        last = nc.tensor.transpose(bank[q // 2][:, (2 * (q % 2) + r) * P:(2 * (q % 2) + r + 1) * P],
                                                   Wbd[:, r, q, :], ident[:, :])
                    if q % 2:
                        last.then_inc(s_wt, 1)
                for q in range(NPAIR):
                    for j in range(L):
                        for r in range(2):
                            last = nc.tensor.matmul(
                                bank[4 + q // 4][32 * j:32 * j + 32, (q % 4) * P + 32 * j:(q % 4 + 1) * P],
                                Wbd[:, r, q, 32 * (L - 1):32 * L], CA[:, r, q, 0:32 * (L - j)],
                                start=(r == 0), stop=(r == 1))
                last.then_inc(s_tb, 1)
                for n in range(2 * NPAIR):
                    q, r = n // 2, n % 2
                    pe.wait_ge(s_wc, q // 2 + 1)
                    if n < 4:
                        pe.wait_ge(s_wc, n + 1)
                    if n >= 4:
                        pe.wait_ge(s_ic, n - 3)
                    nc.tensor.matmul(bank[n % 4][:, 0:CH], WT[:, q, r, :], U4[:, q, :],
                                     start=True, stop=True).then_inc(s_in, 1)
                pe.wait_ge(s_ic, 2 * NPAIR)
                pe.wait_ge(s_wv, 16)
                for t in range(V_EARLY):
                    values(t)
                pe.wait_ge(s_tc, 1)
                for q in range(NPAIR):
                    b = bank[4 + q % 4]
                    if q >= 4:
                        pe.wait_ge(s_ge, q - 3)
                    nc.tensor.matmul(b[:, 0:CH], Tm[:, q, :], U4[:, q, :], start=True, stop=False)
                    if q == 0:
                        pe.wait_ge(s_xs, 1)
                    for r in range(2):
                        lhs = CA[:, r, q, 32:32 * (L + 1)]
                        nc.tensor.matmul(b[:, 0:CHP], lhs, XS[:, r, q, 0:CHP], start=False, stop=False)
                        last = nc.tensor.matmul(b[:, CHP:CH], lhs, XI[:, r, q, :], start=False, stop=(r == 1))
                    last.then_inc(s_y, 1)
                    if q in V_AFTER:
                        values(V_AFTER[q])
                pe.wait_ge(s_vc, NT)
                pe.wait_ge(s_fi, 1)
                for r in range(2):
                    last = nc.tensor.transpose(bank[0][0:(BS + 1) * NPAIR, r * P:(r + 1) * P],
                                               finals[:, r, :, :].rearrange("p b q -> p (b q)"), ident[:, :])
                last.then_inc(s_ft, 1)

            @block.scalar
            def _(act):
                for b in range(4):
                    act.wait_ge(s_wt, b + 1)
                    nc.scalar.copy(WT[:, 2 * b:2 * b + 2, :, :].rearrange("p q r n -> p (q r n)"),
                                   bank[b][:, :]).then_inc(s_wc, 1)
                for n in range(2 * NPAIR):
                    act.wait_ge(s_in, n + 1)
                    nc.scalar.copy(Sin[:, n % 2, n // 2, :], bank[n % 4][:, 0:CH]).then_inc(s_ic, 1)
                def values(t):
                    act.wait_ge(s_vm, t + 1)
                    nc.scalar.copy(v_tok[:, t, :], bank[t % 4][:, :]).then_inc(s_vc, 1)

                for t in range(V_EARLY):
                    values(t)
                for q in range(NPAIR):
                    act.wait_ge(s_y, q + 1)
                    for i in range(L):
                        rows = uT[32 * (q % 4):32 * (q % 4) + 32, q // 4, 0:TOK].rearrange("p (c j) -> p c j", j=L)
                        last = nc.scalar.activation(rows[:, :, i], bank[4 + q % 4][32 * i:32 * i + 32, 0:CH],
                                                    ACT.Gelu_apprx_tanh)
                    last.then_inc(s_ge, 1)
                    if q in V_AFTER:
                        values(V_AFTER[q])

            @block.vector
            def _(dve):
                V = nc.vector
                chain = Link(dve, s_v)
                dve.wait_ge(s_tb, 1)
                for h in range(2):
                    for j in range(L):
                        sl = slice(32 * j, 32 * j + 32)
                        last = V.tensor_copy(Tm[sl, 4 * h:4 * h + 4, 32 * j:P],
                                             bank[4 + h][sl, :].rearrange("p (q n) -> p q n", q=4)[:, :, 32 * j:P])
                chain(last)
                for q in range(NPAIR):
                    last = V.scalar_tensor_tensor(Tm[:, q, :], ident[:, :], dcol[:, q:q + 1], Tm[:, q, :],
                                                  ALU.mult, ALU.add)
                last.then_inc(s_tc, 1)
                dve.wait_ge(s_ic, 2 * NPAIR)
                c_, s_ = Etab[:, 0, :, :], Etab[:, 1, :, :]
                S_ = [Sin[:, r, :, 0:CHP] for r in range(2)]
                Ss = [Sin[:, r, :, CHP:CH].rearrange("p q (b h) -> p q b h", h=2) for r in range(2)]
                Xi = [XI[:, r, :, :].rearrange("p q (b h) -> p q b h", h=2) for r in range(2)]
                xq = [x0[:, r, :, :].rearrange("p b q -> p q b") for r in range(2)]
                fq = [finals[:, r, 1:BS + 1, :].rearrange("p b q -> p q b") for r in range(2)]
                A4 = [pw[:, r, L, :].unsqueeze(2).to_broadcast([P, NPAIR, BS]) for r in range(2)]
                t_ = [par[:, 22 + 8 * r:30 + 8 * r, :] for r in range(2)]
                for r in range(2):
                    V.tensor_copy(Xi[r][:, :, :, 0], xq[r])
                for h, xin_, xout in ((0, xq, [Xi[r][:, :, :, 1] for r in range(2)]),
                                      (1, [Xi[r][:, :, :, 1] for r in range(2)], fq)):
                    for r in range(2):
                        V.tensor_tensor(t_[0], A4[0], xin_[r], ALU.mult)
                        chain(V.tensor_tensor(t_[1], A4[1], xin_[1 - r], ALU.mult))
                        chain(V.tensor_tensor(t_[0], t_[0], t_[1], ALU.subtract if r == 0 else ALU.add))
                        chain(V.tensor_tensor(xout[r], t_[0], Ss[r][:, :, :, h], ALU.add))
                def turn(a, t, ops):
                    V.tensor_tensor(t[0], s_, a[1], ALU.mult)
                    chain(V.tensor_tensor(t[1], s_, a[0], ALU.mult))
                    V.tensor_tensor(a[0], c_, a[0], ALU.mult)
                    chain(V.tensor_tensor(a[1], c_, a[1], ALU.mult))
                    V.tensor_tensor(a[0], a[0], t[0], ops[0])
                    return V.tensor_tensor(a[1], a[1], t[1], ops[1])

                Xn = [XS[:, r, :, 1:CHP + 1] for r in range(2)]
                chain(turn(S_, Xn, (ALU.add, ALU.subtract)))
                for r in range(2):
                    for q in range(NPAIR):
                        last = V.tensor_tensor_scan(XS[:, r, q, 1:CHP + 1],
                                                    par[:, MAG4, q:q + 1].to_broadcast([P, CHP]),
                                                    Sin[:, r, q, 0:CHP], 0.0, ALU.mult, ALU.add)
                chain(last)
                V.memset(XS[:, :, :, 0:1], 0.0)
                turn(Xn, S_, (ALU.subtract, ALU.add)).then_inc(s_xs, 1)
                dve.wait_ge(s_xs, 1)
                for r in range(2):
                    last = V.tensor_copy(finals[:, r, 0, :], XS[:, r, :, CHP])
                last.then_inc(s_fi, 1)
                dve.wait_ge(s_ft, 1)
                V.tensor_copy(fin_t[:, :, :].rearrange("p r n -> p (r n)"),
                              bank[0][0:(BS + 1) * NPAIR, 0:2 * P]).then_inc(s_fc, 1)

        with phase() as (mem, block):
            def tmp(name, shape):
                return mem.enter_context(nc.sbuf_tensor(name, shape, F32))
            la = arena[:, at_CA:at_CA + LINE]
            lb = arena[:, at_XS:at_XS + LINE]
            pooled = Etab.rearrange("p r q c -> p (r q c)")[:, 0:2 * TOK].rearrange("p (m t) -> p m t", m=2)
            at_w = at_CA + 2 * NPAIR * (L + 1) * 32 + P
            w_g = arena[:, at_w:at_w + 2 * DS].rearrange("p (m n) -> p m n", m=2)
            bg = tmp("bg", [P, 2])
            w_pl = tmp("w_pl", [P, 2, P])
            spc = tmp("spc", [P, 2])
            gate = [tmp(f"gate{n}", [P, 384]) for n in range(2)]
            fix = tmp("fix", [P, 2, PBUF])
            prow = tmp("prow", [NSA, 2, P])
            prowp = tmp("prowp", [PBUF, 2, P])

            s_ld = {n: sem("r_loaded_" + n) for n in ("wg", "bg", "p0", "p1", "p2", "p3", "sp")}
            at_WT = at_CA + 2 * NPAIR * (L + 1) * 32
            plast = arena[:, at_WT:at_WT + 2 * NSA].rearrange("p (m n) -> p m n", m=2)
            s_pl = sem("r_sample_rows_packed")
            s_pz = sem("r_pool_weights_cleared")
            s_gm = sem("r_gate_projected")
            s_gs = sem("r_gate_ready")
            s_gd = sem("r_gate_used")
            s_v = sem("r_vector_chain")
            s_g = sem("r_pool_chain")
            s_pd = sem("r_pooled_ready")
            s_pm = sem("r_pool_projected")
            s_pc = sem("r_pool_copied")
            s_pt = sem("r_pool_rows_turned")
            s_pr = sem("r_pool_rows_copied")
            s_o = [sem(f"r_out_pool{n}") for n in range(3)]

            @block.sync
            def _(sp):
                sp.dma_start(w_g, A["w_glu"][0].rearrange("(k p) n -> p k n", p=P)).then_inc(s_ld["wg"], 16)
                sp.dma_start(bg[:, :], A["b_glu"][0].rearrange("(m p) -> p m", p=P)).then_inc(s_ld["bg"], 16)
                sp.dma_start(spc[:, :], A["s_pool"][0].rearrange("(m p) -> p m", p=P)).then_inc(s_ld["sp"], 16)
                sp.wait_ge(s_pz, 1)
                for g in range(4):
                    h = 64 * (g % 2)
                    sp.dma_start(w_pl[h:h + 64, g // 2, h:h + 64], A["w_pool"][0, g]).then_inc(s_ld[f"p{g}"], 16)
                sp.dma_start(O["pool_sample"][:, 0, 0:PBUF - TS, :], A["state_pool"][:, 0, TS:PBUF, :]).then_inc(s_o[0], 16)
                sp.wait_ge(s_pr, 1)
                sp.dma_start(O["pool_prompt"][0, 0], prowp[:, :, :].rearrange("t m c -> t (m c)")).then_inc(s_o[1], 16)
                sp.dma_start(O["pool_sample"][:, 0, PBUF - TS:PBUF, :],
                             prow[:, :, :].rearrange("t m c -> t (m c)")).then_inc(s_o[2], 16)
                sp.wait_ge(s_o[0], 16)
                sp.wait_ge(s_o[1], 16)
                sp.wait_ge(s_o[2], 16)

            @block.tensor
            def _(pe):
                pe.wait_ge(s_pl, 1)
                for m in range(2):
                    nc.tensor.transpose(bank[6][0:PBUF, m * P:(m + 1) * P], line[:, m, NPR:NPR + PBUF], ident[:, :])
                    last = nc.tensor.transpose(
                        bank[7][0:NSA, m * P:(m + 1) * P], plast[:, m, :], ident[:, :])
                last.then_inc(s_pt, 1)
                pe.wait_ge(s_ld["wg"], 16)
                n = 0
                for m in range(2):
                    for c0, cn in CHUNKS_T:
                        if n >= 2:
                            pe.wait_ge(s_gs, n - 1)
                        for k in range(2):
                            last = nc.tensor.matmul(bank[4 + n % 2][:, 0:cn], w_g[:, k, m * P:(m + 1) * P],
                                                    uT[:, k, c0:c0 + cn], start=(k == 0), stop=(k == 1))
                        last.then_inc(s_gm, 1)
                        n += 1
                for g in range(4):
                    pe.wait_ge(s_ld[f"p{g}"], 16)
                pe.wait_ge(s_pd, 1)
                pe.wait_ge(s_pr, 1)
                n = 0
                for m in range(2):
                    for c0, cn in CHUNKS_T:
                        if n >= 2:
                            pe.wait_ge(s_pc, n - 1)
                        nc.tensor.matmul(bank[6 + n % 2][:, 0:cn], w_pl[:, m, :], pooled[:, m, c0:c0 + cn],
                                         start=True, stop=True).then_inc(s_pm, 1)
                        n += 1

            @block.scalar
            def _(act):
                act.wait_ge(s_ld["bg"], 16)
                n = 0
                for m in range(2):
                    for c0, cn in CHUNKS_T:
                        act.wait_ge(s_gm, n + 1)
                        if n >= 2:
                            act.wait_ge(s_gd, n - 1)
                        nc.scalar.activation(gate[n % 2][:, 0:cn], bank[4 + n % 2][:, 0:cn], ACT.Sigmoid,
                                             bias=bg[:, m:m + 1]).then_inc(s_gs, 1)
                        n += 1
                act.wait_ge(s_ld["sp"], 16)
                n = 0
                for m in range(2):
                    for c0, cn in CHUNKS_T:
                        act.wait_ge(s_pm, n + 1)
                        nc.scalar.activation(mixT[:, 6 + m, c0:c0 + cn], bank[6 + n % 2][:, 0:cn], ACT.Copy,
                                             scale=spc[:, m:m + 1]).then_inc(s_pc, 1)
                        n += 1

            @block.gpsimd
            def _(pool):
                G = nc.gpsimd
                chain = Link(pool, s_g)
                G.memset(w_pl[:, :, :], 0.0).then_inc(s_pz, 1)
                G.memset(mixT[:, 4:8, TOK:TP], 0.0)
                chain(G.iota(fix[:, :, :], [[0, 2], [1, PBUF]], base=1, channel_multiplier=0,
                             allow_small_or_imprecise_dtypes=True))
                for g, w in enumerate((2, 4, 8, 16)):
                    f = fix[64 * (g % 2):64 * (g % 2) + 64, g // 2, :]
                    last = G.tensor_scalar(f, f, float(w), None, ALU.min)
                chain(last)

            @block.vector
            def _(dve):
                V = nc.vector
                chain = Link(dve, s_v)
                for m in range(2):
                    last = V.tensor_copy(
                        plast[:, m, :].rearrange("p (b r) -> p b r", b=BS),
                        line[:, m, PBUF + NPR:LINE].rearrange("p (b r) -> p b r", b=BS)[:, :, PBUF:PBUF + TS])
                last.then_inc(s_pl, 1)
                dve.wait_ge(s_pt, 1)
                V.tensor_copy(prowp[:, :, :].rearrange("t m c -> t (m c)"), bank[6][0:PBUF, 0:2 * P])
                V.tensor_copy(prow[:, :, :].rearrange("t m c -> t (m c)"), bank[7][0:NSA, 0:2 * P]).then_inc(s_pr, 1)
                dve.wait_ge(s_g, 2)
                chain(V.reciprocal(fix[:, :, :], fix[:, :, :]))
                for g, w in enumerate((2, 4, 8, 16)):
                    f = fix[64 * (g % 2):64 * (g % 2) + 64, g // 2, :]
                    last = V.tensor_scalar(f, f, float(w), None, ALU.mult)
                chain(last)

                def shifted(o_, i_, s, rows=slice(0, P)):
                    V.tensor_copy(o_[rows, 0:s], i_[rows, 0:s])
                    chain(V.tensor_tensor(o_[rows, s:LINE], i_[rows, s:LINE], i_[rows, 0:LINE - s], ALU.add))

                def average(m, half, sums, w):
                    r = slice(64 * half, 64 * half + 64)
                    chain(V.tensor_tensor(sums[r, PBUF:2 * PBUF], sums[r, PBUF:2 * PBUF], fix[r, m, :], ALU.mult))
                    V.scalar_tensor_tensor(pooled[r, m, 0:NPR], sums[r, PBUF:PBUF + NPR], 1.0 / w,
                                           line[r, m, PBUF:PBUF + NPR], ALU.mult, ALU.subtract)

                    def new(x):
                        return x.rearrange("p (b r) -> p b r", b=BS)[:, :, PBUF:PBUF + TS]
                    return V.scalar_tensor_tensor(
                        pooled[r, m, NPR:TOK].rearrange("p (b r) -> p b r", b=BS), new(sums[r, PBUF + NPR:LINE]),
                        1.0 / w, new(line[r, m, PBUF + NPR:LINE]), ALU.mult, ALU.subtract)

                def gates(n):
                    m, (c0, cn) = n // 3, CHUNKS_T[n % 3]
                    dve.wait_ge(s_gs, n + 1)
                    V.tensor_tensor(mixT[:, 4 + m, c0:c0 + cn], gate[n % 2][:, 0:cn], uT[:, m, c0:c0 + cn],
                                    ALU.mult).then_inc(s_gd, 1)

                shifted(la, line[:, 0, :], 1)
                shifted(lb, la, 2)
                average(0, 0, la, 2)
                chain(average(0, 1, lb, 4))
                gates(0)
                gates(1)
                shifted(la, line[:, 1, :], 1)
                shifted(lb, la, 2)
                gates(2)
                gates(3)
                shifted(la, lb, 4)
                shifted(lb, la, 8, slice(64, P))
                average(1, 0, la, 8)
                average(1, 1, lb, 16).then_inc(s_pd, 1)
                gates(4)
                gates(5)

        W_O_AT = AR - KD * D
        w_o = arena[:, W_O_AT:AR].rearrange("p (k n) -> p k n", k=KD)
        with phase() as (mem, block):
            o = 0
            a_, o = carve(o, 2, TP)
            qb = a_.rearrange("p (h t) -> p h t", h=2)
            a_, o = carve(o, 2, TP)
            kb = a_.rearrange("p (h t) -> p h t", h=2)
            pbuf = []
            for _n in range(2):
                a_, o = carve(o, NPR)
                pbuf.append(a_)
            pt = []
            for _n in range(2):
                a_, o = carve(o, 4, P)
                pt.append(a_)
            a_, o = carve(o, KD, P)
            wk_s = a_.rearrange("p (k n) -> p k n", k=KD)
            a_, o = carve(o, KD, P)
            wq_s = a_.rearrange("p (k n) -> p k n", k=KD)
            a_, o = carve(o, NT, P)
            att = a_.rearrange("p (t n) -> p t n", t=NT)
            a_, o = carve(o, NT, P)
            k_tok = a_.rearrange("p (t n) -> p t n", t=NT)
            a_, o = carve(o, 4, 2 * NT)
            sm = a_.rearrange("p (r n) -> p r n", r=4)
            a_, o = carve(o, 2, 2)
            sm2 = a_.rearrange("p (r n) -> p r n", r=2)
            a_, o = carve(o, META)
            ptail = a_
            assert o <= W_O_AT

            NST, QT = 2 * NT, NT
            steps = [(h, i) for h in range(2) for i in range(QT)]
            groups = [(n, g) for n, (h, i) in enumerate(steps) for g in range(i // 4 + 1)]
            NG = len(groups)
            upto = [sum(1 for m, _ in groups if m <= n) for n in range(NST)]

            def nq(i):
                return min(P, NPR - i * P)

            def blocks(n, g):
                return range(4 * g, min(4 * g + 4, steps[n][1] + 1))

            s_w = {k: sem("a_weights_" + k) for k in "kq"}
            s_pj = sem("a_projected")
            s_kev = sem("a_k_rows_ready")
            s_qev = sem("a_q_rows_ready")
            s_rw = [sem(f"a_gate_rows{n}") for n in range(2)]
            s_zero = [sem("a_zero_rows_q"), sem("a_zero_rows_k")]
            s_one = [sem("a_ones_rows_q"), sem("a_ones_rows_k")]
            s_round = sem("a_keys_out")
            s_tail = sem("a_tail_cleared")
            s_fill = [sem(f"a_unused_rows_filled{n}") for n in range(2)]
            s_wo = [sem(f"a_out_weights{n}") for n in range(2)]
            s_hold = sem("a_waits_held")
            s_ktt = sem("a_k_turned")
            s_ktA = sem("a_k_tok_by_scalar")
            s_ktD = sem("a_k_tok_by_vector")
            s_ko = [sem(f"a_out_k{n}") for n in range(3)]
            s_S = sem("a_scores")
            s_mx = sem("a_maxima")
            s_mp = sem("a_max_parts")
            s_ex = sem("a_exponentials")
            s_T = sem("a_turned")
            s_E = [sem("a_turned_copied_by_vector"), sem("a_turned_copied_by_scalar")]
            s_PV = sem("a_weighted")
            s_rc = sem("a_inverse_sums")
            s_att = sem("a_outputs")
            s_at = sem("a_outputs_turned")
            s_aeA = sem("a_mix_by_scalar")
            s_aeD = sem("a_mix_by_vector")

            w_in = A["w_in"][0].rearrange("(k p) n -> p k n", p=P)
            score = [(0, 1), (2, 3)]

            def pieces(n):
                nk = min((steps[n][1] + 1) * P, NPR)
                out = [(score[n % 2][c], 512 * c, min(512, nk - 512 * c)) for c in range(2) if nk > 512 * c]
                return out + ([(6 + n % 2, 1024, NPR - 1024)] if nk > 1024 else [])

            @block.gpsimd
            def _(pool):
                G = nc.gpsimd
                pool.dma_start(wk_s, w_in[:, :, DA:DA + P]).then_inc(s_w["k"], 16)
                pool.dma_start(wq_s, w_in[:, :, 0:P]).then_inc(s_w["q"], 16)
                G.memset(mixT[:, 0:4, TOK:TP], 0.0)
                G.memset(ptail, 0.0).then_inc(s_tail, 1)
                pool.wait_ge(s_tail, 1)
                G.memset(qb[64:P, :, :], 0.0).then_inc(s_zero[0], 1)
                pool.wait_ge(s_zero[0], 1)
                G.memset(qb[64:66, :, :], 1.0).then_inc(s_one[0], 1)
                with pool.Fori(0, 3) as i:
                    pool.wait_ge(s_pj, i * 6 + 6)
                    pool.dma_start(wk_s, w_in[:, :, bass.ds(i * P + (DA + P), P)]).then_inc(s_w["k"], 16)
                    pool.dma_start(wq_s, w_in[:, :, bass.ds(i * P + P, P)]).then_inc(s_w["q"], 16)

            @block.sync
            def _(sp):
                kp = O["k_prompt"][0, 0].rearrange("t h d -> t (h d)")
                ks = O["k_sample"].rearrange("b l t h d -> (b l t) (h d)")

                def pair(i):
                    if not isinstance(i, int):
                        sp.wait_ge(s_pj, i * 6 + 6)
                        sp.sem_inc(s_round, 1)
                    heads = slice(2 * i, 2 * i + 2) if isinstance(i, int) else bass.ds(i * 2, 2)
                    sp.dma_start(qb[65:66, :, :], gate_sums[0:1, heads, :]).then_inc(s_rw[0], 16)
                    sp.dma_start(kb[64:65, :, :], gate_sums[1:2, heads, :]).then_inc(s_rw[1], 16)
                    sp.wait_ge(s_ktA, i + 1)
                    sp.sem_inc(s_round, 1)
                    sp.wait_ge(s_ktD, i * 2 + 2)
                    sp.sem_inc(s_round, 1)
                    cols = slice(i * P, i * P + P) if isinstance(i, int) else bass.ds(i * P, P)
                    sp.dma_start(kp[0:8 * P, cols].rearrange("(t p) n -> p t n", p=P), k_tok[:, 0:8, :]).then_inc(s_ko[0], 16)
                    sp.dma_start(kp[8 * P:NPR, cols], k_tok[0:META, 8, :]).then_inc(s_ko[1], 16)
                    sp.dma_start(ks[:, cols], k_tok[META:META + NSA, 8, :]).then_inc(s_ko[2], 16)
                    for s in s_ko:
                        sp.wait_ge(s, i * 16 + 16)
                        sp.sem_inc(s_round, 1)

                for s in s_one:
                    sp.wait_ge(s, 1)
                pair(0)
                wo = A["w_out"][0].rearrange("(k p) n -> p k n", p=P)
                for n in range(2):
                    sp.dma_start(w_o[:, 4 * n:4 * n + 4, :], wo[:, 4 * n:4 * n + 4, :]).then_inc(s_wo[n], 16)
                fill = xT[:, :, :].rearrange("p k t -> p (k t)")[:, 0:8 * D].rearrange("p (s d) -> p s d", s=8)
                for n in range(2):
                    t0, t1 = LEAST + 8 * n, min(LEAST + 8 * n + 8, SLOTT)
                    sp.dma_start(y_park[t0 * P:t1 * P, :].rearrange("(s p) d -> p s d", p=P),
                                 fill[:, 0:t1 - t0, :]).then_inc(s_fill[n], 16)
                with sp.Fori(1, 4) as i:
                    pair(i)
                for n in range(2):
                    sp.wait_ge(s_fill[n], 16)
                    sp.wait_ge(s_wo[n], 16)

            @block.tensor
            def _(pe):
                T = nc.tensor

                def waited():
                    pe.sem_inc(s_hold, 1)

                def project(i):
                    n = 0
                    for key, w in (("k", wk_s), ("q", wq_s)):
                        pe.wait_ge(s_w[key], i * 16 + 16)
                        for c0, cn in CHUNKS_T:
                            if n >= 4:
                                pe.wait_ge(s_kev, i * 3 + (n - 3))
                            for k in range(KD):
                                last = T.matmul(bank[n % 4][:, 0:cn], w[:, k, :], xT[:, k, c0:c0 + cn],
                                                start=(k == 0), stop=(k == KD - 1))
                            last.then_inc(s_pj, 1)
                            n += 1

                def turn_k(i):
                    pe.wait_ge(s_kev, i * 3 + 3)
                    waited()
                    for t in range(NT):
                        w = min(P, TOK - t * P)
                        for h in range(2):
                            last = T.transpose(bank[4 + t // 4][0:w, (t % 4) * P + h * HD:(t % 4) * P + (h + 1) * HD],
                                               kb[0:HD, h, t * P:t * P + w], ident[0:HD, 0:HD])
                        if t % 4 == 3 or t == NT - 1:
                            last.then_inc(s_ktt, 1)

                def scores(i, n):
                    h, t = steps[n]
                    if n == 0:
                        pe.wait_ge(s_qev, i * 3 + 3)
                        for s in s_rw:
                            pe.wait_ge(s, i * 16 + 16)
                    if n >= 2:
                        pe.wait_ge(s_ex, i * NST + (n - 1))
                    if t == QT - 1:
                        pe.wait_ge(s_att, i * NST + (n - 1))
                    for b, k0, kn in pieces(n):
                        diag = k0 + kn > t * P
                        T.matmul(bank[b][0:nq(t), 0:kn], qb[:, h, t * P:t * P + nq(t)],
                                 kb[:, h, k0:k0 + kn], start=True, stop=not diag)
                    o0, w = t * P - k0, min(P, NPR - t * P)
                    T.matmul(bank[b][0:nq(t), o0:o0 + w], ident[:, 0:nq(t)], causal[:, 0:w],
                             start=False, stop=True).then_inc(s_S, 1)

                def turn(i, k):
                    n, g = groups[k]
                    t = steps[n][1]
                    pe.wait_ge(s_ex, i * NST + (n + 1))
                    if k < 2:
                        pe.wait_ge((s_ktA, s_ktD)[k], i * (1 + k) + 1)
                    else:
                        pe.wait_ge(s_E[k % 2], i * (NG // 2) + k // 2)
                    waited()
                    for j, b in enumerate(blocks(n, g)):
                        w = min(P, NPR - b * P)
                        last = T.transpose(bank[4 + k % 2][0:w, j * P:j * P + nq(t)],
                                           pbuf[n % 2][0:nq(t), b * P:b * P + w], ident[0:nq(t), 0:nq(t)])
                    last.then_inc(s_T, 1)

                def weigh(i, k):
                    n, g = groups[k]
                    h, t = steps[n]
                    pe.wait_ge(s_E[k % 2], i * (NG // 2) + (k // 2 + 1))
                    if g == 0 and n >= 2:
                        pe.wait_ge(s_att, i * NST + (n - 1))
                    if g == 0 and n == 0:
                        pe.wait_ge(s_ktD, i * 2 + 2)
                    waited()
                    for j, b in enumerate(blocks(n, g)):
                        lhs = pt[k % 2][:, j * P:j * P + nq(t)] if b < NT - 1 else ptail
                        last = T.matmul(bank[6 + n % 2][0:nq(t), 0:HD], lhs, v_tok[:, b,bass.ds(i * P + h * HD, HD)],
                                        start=(b == 0), stop=(b == t))
                    last.then_inc(s_PV, 1)

                with pe.Fori(0, 4) as i:
                    project(i)
                    turn_k(i)
                    scores(i, 0)
                    k = 0
                    weighed = 0
                    for n in range(NST):
                        if n + 1 < NST:
                            if steps[n + 1][1] == QT - 1:
                                weigh(i, k - 1)
                                weighed = k
                            scores(i, n + 1)
                        for _ in range(steps[n][1] // 4 + 1):
                            turn(i, k)
                            if k > weighed:
                                weigh(i, k - 1)
                                weighed = k
                            k += 1
                    weigh(i, NG - 1)
                    pe.wait_ge(s_att, i * NST + NST)
                    waited()
                    for t in range(QT):
                        b = (4, 5, 7)[t // 4]
                        last = T.transpose(bank[b][:, (t % 4) * P:(t % 4) * P + nq(t)], att[0:nq(t), t, :],
                                           ident[0:nq(t), 0:nq(t)])
                        if t % 4 == 3 or t == QT - 1:
                            last.then_inc(s_at, 1)
                    pe.wait_ge(s_aeA, i + 1)
                    pe.wait_ge(s_aeD, i * 2 + 2)

            def copy_turned(eng, copy, i, k):
                n, g = groups[k]
                t, bl = steps[n][1], blocks(n, g)
                eng.wait_ge(s_T, i * NG + (k + 1))
                full = [b for b in bl if NPR - b * P >= P]
                if nq(t) == P:
                    last = copy(pt[k % 2][:, 0:len(bl) * P], bank[4 + k % 2][:, 0:len(bl) * P])
                elif full:
                    last = copy(pt[k % 2].rearrange("p (j n) -> p j n", j=4)[:, 0:len(full), 0:nq(t)],
                                bank[4 + k % 2][:, :].rearrange("p (j n) -> p j n", j=4)[:, 0:len(full), 0:nq(t)])
                else:
                    w = NPR - bl[0] * P
                    last = copy(ptail[0:w, :], bank[4 + k % 2][0:w, 0:nq(t)])
                last.then_inc(s_E[k % 2], 1)

            @block.scalar
            def _(act):
                S = nc.scalar

                def exps(i, n):
                    h, t = steps[n]
                    q = nq(t)
                    act.wait_ge(s_mx, i * NST + (n + 1))
                    if n >= 2:
                        act.wait_ge(s_T, i * NG + upto[n - 2])
                    nk = min((t + 1) * P, 1024)
                    src = score_slot[n % 2][0:q, 0:nk]
                    if nk < (t + 1) * P:
                        last = S.activation(pbuf[n % 2][0:q, 1024:NPR], bank[6 + n % 2][0:q, 0:NPR - 1024], ACT.Exp,
                                            bias=sm[0:q, 0, n:n + 1], accum_out=sm2[0:q, 1, h:h + 1])
                    last = S.activation(pbuf[n % 2][0:q, 0:nk], src, ACT.Exp, bias=sm[0:q, 0, n:n + 1],
                                        accum_out=sm[0:q, 1, n:n + 1])
                    last.then_inc(s_ex, 1)

                act.wait_ge(s_tail, 1)
                with act.Fori(0, 4) as i:
                    for c, (c0, cn) in enumerate(CHUNKS_T):
                        n = 3 + c
                        act.wait_ge(s_pj, i * 6 + (n + 1))
                        pn = min(cn, NPR - c0)
                        if pn < cn:
                            S.mul(qs_T[:, bass.ds(i, 1), :], bank[n % 4][:, pn:cn].unsqueeze(1), SCALE)
                        for h in range(2):
                            last = S.mul(qb[0:HD, h, c0:c0 + pn], bank[n % 4][HD * h:HD * h + HD, 0:pn], SCALE)
                        last.then_inc(s_qev, 1)
                    act.wait_ge(s_rw[0], i * 16 + 16)
                    act.wait_ge(s_ktt, i * 3 + 1)
                    S.copy(k_tok[:, 0:4, :], bank[4][:, :].rearrange("p (t n) -> p t n", t=4)).then_inc(s_ktA, 1)
                    exps(i, 0)
                    for n in range(NST):
                        for k, (m, g) in enumerate(groups):
                            if m == n and k % 2:
                                copy_turned(act, S.copy, i, k)
                        if n + 1 < NST:
                            exps(i, n + 1)
                    act.wait_ge(s_at, i * 3 + 1)
                    S.copy(mixT[:, bass.ds(i, 1), 0:512], bank[4][:, :].unsqueeze(1)).then_inc(s_aeA, 1)

            @block.vector
            def _(dve):
                V = nc.vector
                V.memset(kb[64:P, :, :], 0.0).then_inc(s_zero[1], 1)
                dve.wait_ge(s_zero[1], 1)
                V.memset(kb[64:66, :, :], 1.0).then_inc(s_one[1], 1)
                dve.wait_ge(s_tail, 1)

                def maxima(i, n):
                    h, t = steps[n]
                    q = nq(t)
                    dve.wait_ge(s_S, i * NST + (n + 1))
                    nk = min((t + 1) * P, 1024)
                    src = score_slot[n % 2][0:q, 0:nk]
                    if nk == (t + 1) * P:
                        V.tensor_reduce(sm[0:q, 0, n:n + 1], src, AX, ALU.max, negate=True).then_inc(s_mx, 1)
                        return
                    V.tensor_reduce(sm[0:q, 3, 0:1], src, AX, ALU.max).then_inc(s_mp, 1)
                    V.tensor_reduce(sm[0:q, 3, 1:2], bank[pieces(n)[-1][0]][0:q, 0:NPR - t * P], AX,
                                    ALU.max).then_inc(s_mp, 1)
                    dve.wait_ge(s_mp, i * 4 + (2 * h + 2))
                    V.tensor_reduce(sm[0:q, 0, n:n + 1], sm[0:q, 3, 0:2], AX, ALU.max, negate=True).then_inc(s_mx, 1)

                def outputs(i, n):
                    h, t = steps[n]
                    q = nq(t)
                    dve.wait_ge(s_PV, i * NG + upto[n])
                    base = i * (NST + 2) + n + h
                    if t == QT - 1:
                        V.tensor_tensor(sm[0:q, 1, n:n + 1], sm[0:q, 1, n:n + 1], sm2[0:q, 1, h:h + 1],
                                        ALU.add).then_inc(s_rc, 1)
                        dve.wait_ge(s_rc, base + 1)
                        base = base + 1
                    V.reciprocal(sm[0:q, 2, n:n + 1], sm[0:q, 1, n:n + 1]).then_inc(s_rc, 1)
                    dve.wait_ge(s_rc, base + 1)
                    V.tensor_scalar(att[0:q, t, h * HD:(h + 1) * HD], bank[6 + n % 2][0:q, 0:HD],
                                    sm[0:q, 2, n:n + 1], None, ALU.mult).then_inc(s_att, 1)

                with dve.Fori(0, 4) as i:
                    for c, (c0, cn) in enumerate(CHUNKS_T):
                        dve.wait_ge(s_pj, i * 6 + (c + 1))
                        pn = min(cn, NPR - c0)
                        if pn < cn:
                            V.tensor_copy(ks_T[:, bass.ds(i, 1), :], bank[c][:, pn:cn].unsqueeze(1))
                        for h in range(2):
                            last = V.tensor_copy(kb[0:HD, h, c0:c0 + cn], bank[c][HD * h:HD * h + HD, 0:cn])
                        last.then_inc(s_kev, 1)
                    dve.wait_ge(s_rw[0], i * 16 + 16)
                    dve.wait_ge(s_ktt, i * 3 + 2)
                    V.tensor_copy(k_tok[:, 4:8, :], bank[5][:, :].rearrange("p (t n) -> p t n", t=4)).then_inc(s_ktD, 1)
                    dve.wait_ge(s_ktt, i * 3 + 3)
                    w = META + NSA
                    V.tensor_copy(k_tok[0:w, 8, :], bank[6][0:w, 0:P]).then_inc(s_ktD, 1)
                    maxima(i, 0)
                    for n in range(NST):
                        early = n + 1 < NST and steps[n + 1][1] == QT - 1
                        if early:
                            outputs(i, n - 1)
                        if n + 1 < NST:
                            maxima(i, n + 1)
                        for k, (m, g) in enumerate(groups):
                            if m == n and k % 2 == 0:
                                copy_turned(dve, V.tensor_copy, i, k)
                        if n and not early:
                            outputs(i, n - 1)
                    outputs(i, NST - 1)
                    for j, (c0, b, w) in enumerate(((512, 5, 512), (1024, 7, META))):
                        dve.wait_ge(s_at, i * 3 + (j + 2))
                        V.tensor_copy(mixT[:, bass.ds(i, 1), c0:c0 + w], bank[b][:, 0:w].unsqueeze(1)).then_inc(s_aeD, 1)

        logits = sb("logits", [P, NT, E])
        wsel = sb("wsel", [P, NT, 2])
        slot_i = sb("slot_i", [P, NT, 2], I32)
        tab_i = sb("tab_i", [1, 3, TT], I32)
        rounds_i = sb("rounds_i", [1, 1], I32)

        with phase() as (mem, block):
            o = 0
            NK = PAST + TS
            kc, vc, lc, vn = [], [], [], []
            for _s in range(2):
                a_, o = carve(o, NPAGE, DA)
                kc.append(a_.rearrange("p (j n) -> p j n", j=NPAGE))
                a_, o = carve(o, NPAGE, DA)
                vc.append(a_.rearrange("p (j n) -> p j n", j=NPAGE))
                a_, o = carve(o, NPAGE, H)
                lc.append(a_.rearrange("p (j n) -> p j n", j=NPAGE))
                a_, o = carve(o, DA)
                vn.append(a_)
            a_, o = carve(o, 4, NK)
            kT = a_.rearrange("p (a n) -> p a n", a=4)
            a_, o = carve(o, 320)
            qbd = a_
            qdiag = a_.rearrange("p (a n) -> p a n", n=80)
            a_, o = carve(o, NK)
            gates = a_
            a_, o = carve(o, NK)
            sums = a_
            a_, o = carve(o, NK)
            nsums = a_
            a_, o = carve(o, 64)
            qsum = a_
            a_, o = carve(o, 64)
            by_head = a_
            a_, o = carve(o, 64)
            by_query = a_
            a_, o = carve(o, NK)
            ones8 = a_
            a_, o = carve(o, NK)
            pr_ = a_
            a_, o = carve(o, 3, 64)
            pT = a_
            a_, o = carve(o, 3, 2)
            st = a_.rearrange("p (r s) -> p r s", r=3)
            xs_ = []
            for _s in range(3):
                a_, o = carve(o, D)
                xs_.append(a_)
            assert o <= W_O_AT
            ptab = mem.enter_context(nc.sbuf_tensor("ptab", [1, BS * NPAGE], I32))
            w_r = mem.enter_context(nc.sbuf_tensor("w_r", [P, KD, E], F32))
            zero_i = mem.enter_context(nc.sbuf_tensor("zero_i", [P, SLOTT], I32))
            ln = [mem.enter_context(nc.sbuf_tensor(f"ln1_st{s}", [P, 20], F32)) for s in range(3)]
            B_HT, B_LG, B_SC, B_K, B_PT, B_OUT = 2, 4, 5, (6, 7), 6, 7

            kinds = ("k0", "k1", "v0", "v1", "l0", "l1", "vn")
            s_ld = [{k: sem(f"d_loaded_{k}_{s}") for k in kinds} for s in range(2)]
            s_tab = sem("d_page_table")
            s_cst = sem("d_constants")
            s_lt = sem("d_gates_turned")
            s_kt = sem("d_keys_turned")
            s_kc = sem("d_keys_copied")
            s_q = sem("d_queries_placed")
            s_gc = sem("d_gates_copied")
            s_dc = sem("d_sums_made")
            s_cq = sem("d_sums_ready")
            s_sc = sem("d_scores")
            s_mx = sem("d_maxima")
            s_ex = sem("d_exponentials")
            s_rc = sem("d_inverse_sums")
            s_ps = sem("d_probabilities")
            s_tt = sem("d_turned")
            s_tc = sem("d_turned_copied")
            s_pv = sem("d_weighted")
            s_uc = sem("d_outputs")
            s_gz = sem("d_queries_cleared")
            s_wr = sem("c_router_weights")
            s_gb = [sem(f"c_gain_shift{n}") for n in range(2)]
            s_zi = sem("c_zeros_ready")
            s_zo = sem("c_slots_zeroed")
            s_x = [sem(f"c_stream{s}") for s in range(3)]
            s_mm = sem("c_projected")
            s_res = sem("c_residual_added")
            s_v = sem("c_vector_chain")
            s_var = sem("c_variance")
            s_std = sem("c_std")
            s_nb = sem("c_bias")
            s_cen = sem("c_centred")
            s_gn = sem("c_gained")
            s_h = sem("c_h_ready")
            s_ht = sem("c_h_turned")
            s_hc = sem("c_hT_copied")
            s_ho = [sem(f"c_h_parked{s}") for s in range(3)]
            s_lg = sem("c_logits")
            s_lc = sem("c_logits_copied")

            @block.sync
            def _(sp):
                sp.dma_start(ptab[:, :], A["page_table"].rearrange("(a b) j -> a (b j)", a=1)).then_inc(s_tab, 16)

                def load_x(t):
                    if t >= 3:
                        sp.wait_ge(s_ht, 2 * (t - 2))
                        sp.wait_ge(s_ho[t % 3], 16 * (t // 3))
                    sp.dma_start(xs_[t % 3], x_park[t]).then_inc(s_x[t % 3], 16)

                def load_past(b):
                    s = b % 2
                    ck = A["cache_k"].rearrange("n l p h d -> n (l p) (h d)")
                    cv = A["cache_v"].rearrange("n l p h d -> n (l p) (h d)")
                    cl = A["cache_logf"].rearrange("n l p h -> n (l p) h")
                    if b >= 2:
                        sp.wait_ge(s_pv, b - 1)
                    for j in range(NPAGE):
                        page = sp.value_load(ptab[0:1, b * NPAGE + j:b * NPAGE + j + 1], min_val=0, max_val=NPOOL - 1)
                        for key, src, dst in (("l", cl, lc), ("k", ck, kc), ("v", cv, vc)):
                            sp.dma_start(dst[s][:, j, :], src[bass.ds(page, 1), :, :].rearrange("a p n -> p (a n)")
                                         ).then_inc(s_ld[s][f"{key}{j}"], 16)
                    sp.dma_start(vn[s][0:TS, :], O["v_sample"][b, 0].rearrange("t h d -> t (h d)")
                                 ).then_inc(s_ld[s]["vn"], 16)

                sp.wait_ge(s_tab, 16)
                load_past(0)
                load_x(0)
                sp.dma_start(gb[:, 0, :], bcast_rows(A["ln1_g"][0], P)).then_inc(s_gb[0], 16)
                sp.dma_start(gb[:, 1, :], bcast_rows(A["ln1_b"][0], P)).then_inc(s_gb[1], 16)
                sp.dma_start(w_r[:, :, :], A["w_router"].rearrange("(k p) n -> p k n", p=P)).then_inc(s_wr, 16)
                load_past(1)
                load_x(1)
                load_x(2)
                sp.wait_ge(s_zi, 1)
                sp.dma_start(slot_tok.rearrange("(p n) a -> p (n a)", p=P), zero_i[:, :]).then_inc(s_zo, 16)
                for t in range(NT):
                    if t + 2 < BS:
                        load_past(t + 2)
                    sp.wait_ge(s_h, t + 1)
                    sp.dma_start(h_park[t * P:(t + 1) * P, :], xs_[t % 3]).then_inc(s_ho[t % 3], 16)
                    if t + 3 < NT:
                        load_x(t + 3)
                for s in range(3):
                    sp.wait_ge(s_ho[s], 16 * (NT // 3))
                sp.wait_ge(s_zo, 16)

            @block.tensor
            def _(pe):
                T = nc.tensor

                def project(t, quarter):
                    if quarter == 0:
                        if t >= 1:
                            pe.wait_ge(s_res, t)
                        if t == NT - 1:
                            pe.wait_ge(s_uc, BS)
                    half = quarter // 2
                    for k in range(4 * (quarter % 2), 4 * (quarter % 2) + 4):
                        last = T.matmul(bank[half], mixT[:, k, t * P:(t + 1) * P],
                                        w_o[:, k, 512 * half:512 * half + 512], start=(k == 0), stop=(k == KD - 1))
                    if quarter == 3:
                        last.then_inc(s_mm, 1)

                def turn(t):
                    pe.wait_ge(s_h, t + 1)
                    for half in range(2):
                        if t >= 1:
                            pe.wait_ge(s_hc, 2 * t - 1 + half)
                        for k in range(4):
                            kk = 4 * half + k
                            last = T.transpose(bank[B_HT + half][:, k * P:(k + 1) * P],
                                               xs_[t % 3][:, kk * P:(kk + 1) * P], ident[:, :])
                        last.then_inc(s_ht, 1)

                def route(t):
                    pe.wait_ge(s_hc, 2 * t + 2)
                    if t >= 1:
                        pe.wait_ge(s_lc, t)
                    for k in range(KD):
                        last = T.matmul(bank[B_LG][:, 0:E], xT[:, k, t * P:(t + 1) * P], w_r[:, k, :],
                                        start=(k == 0), stop=(k == KD - 1))
                    last.then_inc(s_lg, 1)

                def turn_past(b):
                    s, use = b % 2, b // 2 + 1
                    for j in range(NPAGE):
                        pe.wait_ge(s_ld[s][f"l{j}"], use * 16)
                    if b >= 1:
                        pe.wait_ge(s_ex, b)
                        pe.wait_ge(s_tc, b)
                    for j in range(NPAGE):
                        last = T.transpose(bank[B_SC][0:H, j * P:(j + 1) * P], lc[s][:, j, :], ident[:, :])
                    last.then_inc(s_lt, 1)
                    for j in range(NPAGE):
                        pe.wait_ge(s_ld[s][f"k{j}"], use * 16)
                    for a in range(4):
                        if a == 2 and b >= 1:
                            pe.wait_ge(s_uc, b)
                        for j in range(NPAGE):
                            last = T.transpose(bank[B_K[a // 2]][:, ((a % 2) * 2 + j) * P:((a % 2) * 2 + j + 1) * P],
                                               kc[s][:, j, a * P:(a + 1) * P], ident[:, :])
                        if a % 2:
                            last.then_inc(s_kt, 1)

                def scores(b):
                    pe.wait_ge(s_q, b + 1)
                    pe.wait_ge(s_kc, b * 2 + 2)
                    pe.wait_ge(s_cq, b + 1)
                    z = bank[B_SC]
                    for a in range(4):
                        T.matmul(z[0:64, 0:NK], qbd[:, 64 * a:64 * a + 64], kT[:, a, :], start=(a == 0), stop=False)
                    T.matmul(z[0:64, 0:NK], by_head[0:H, :], nsums[0:H, :], start=False, stop=False)
                    T.matmul(z[0:64, 0:NK], qsum[0:H, :], ones8[0:H, :], start=False, stop=False)
                    T.matmul(z[0:64, PAST:NK], by_query[0:TS, :], causal[0:TS, 0:TS],
                             start=False, stop=True).then_inc(s_sc, 1)

                def turn_probabilities(b):
                    pe.wait_ge(s_ps, b + 1)
                    for j in range(3):
                        w = min(P, NK - j * P)
                        last = T.transpose(bank[B_PT][0:w, j * 64:(j + 1) * 64], pr_[0:64, j * P:j * P + w],
                                           ident[0:64, 0:64])
                    last.then_inc(s_tt, 1)

                def weigh(b):
                    s, use = b % 2, b // 2 + 1
                    for k in ("v0", "v1", "vn"):
                        pe.wait_ge(s_ld[s][k], use * 16)
                    pe.wait_ge(s_tc, b + 1)
                    for a in range(4):
                        for j in range(3):
                            w = min(P, NK - j * P)
                            lhs = vc[s][:, j, a * P:(a + 1) * P] if j < 2 else vn[s][0:TS, a * P:(a + 1) * P]
                            last = T.matmul(bank[B_OUT][:, a * 16:a * 16 + 16], lhs,
                                            pT[0:w, 64 * j + 16 * a:64 * j + 16 * a + 16],
                                            start=(j == 0), stop=(j == 2))
                    last.then_inc(s_pv, 1)

                pe.wait_ge(s_cst, 1)
                for t in range(NT):
                    project(t, 0)
                    if t < BS:
                        turn_past(t)
                    project(t, 1)
                    if t < BS:
                        scores(t)
                    project(t, 2)
                    if t >= 1:
                        turn(t - 1)
                    if t < BS:
                        turn_probabilities(t)
                    project(t, 3)
                    if t == 1:
                        pe.wait_ge(s_wr, 16)
                    if t >= 1:
                        route(t - 1)
                    if t < BS:
                        weigh(t)
                turn(NT - 1)
                route(NT - 1)

            @block.scalar
            def _(act):
                S = nc.scalar

                def centre(t):
                    s = t % 3
                    act.wait_ge(s_var, t + 1)
                    S.activation(ln[s][:, 15:16], ln[s][:, 14:15], ACT.Sqrt).then_inc(s_std, 1)
                    act.wait_ge(s_nb, t + 1)
                    S.activation(xs_[s], xs_[s], ACT.Identity, bias=ln[s][:, 17:18],
                                 scale=ln[s][:, 16:17]).then_inc(s_cen, 1)

                def h_turned(t):
                    for half in range(2):
                        act.wait_ge(s_ht, 2 * t + half + 1)
                        S.copy(xT[:, 4 * half:4 * half + 4, t * P:(t + 1) * P],
                               bank[B_HT + half].rearrange("p (k n) -> p k n", k=4)).then_inc(s_hc, 1)

                def keys(b):
                    if b >= 1:
                        act.wait_ge(s_sc, b)
                    for c in range(2):
                        act.wait_ge(s_kt, b * 2 + (c + 1))
                        S.copy(kT[:, 2 * c:2 * c + 2, 0:PAST],
                               bank[B_K[c]][:, :].rearrange("p (a n) -> p a n", a=2)).then_inc(s_kc, 1)

                for t in range(NT + 1):
                    if t >= 1:
                        centre(t - 1)
                    if t < BS:
                        keys(t)
                        act.wait_ge(s_mx, t + 1)
                        S.activation(pr_[0:64, :], bank[B_SC][0:64, 0:NK], ACT.Exp, bias=st[0:64, 0, 0:1],
                                     accum_out=st[0:64, 1, 0:1]).then_inc(s_ex, 1)
                    if t >= 1:
                        h_turned(t - 1)
                    if t < BS:
                        act.wait_ge(s_tt, t + 1)
                        S.copy(pT[:, 0:128], bank[B_PT][:, 0:128])
                        S.copy(pT[0:TS, 128:192], bank[B_PT][0:TS, 128:192]).then_inc(s_tc, 1)

            @block.gpsimd
            def _(pool):
                G = nc.gpsimd
                G.memset(qbd, 0.0).then_inc(s_gz, 1)
                G.memset(zero_i[:, :], 0).then_inc(s_zi, 1)
                pool.wait_ge(s_gb[1], 16)
                for t in range(NT):
                    pool.wait_ge(s_gn, t + 1)
                    G.tensor_tensor(xs_[t % 3], xs_[t % 3], gb[:, 1, :], ALU.add).then_inc(s_h, 1)

            @block.vector
            def _(dve):
                V = nc.vector
                chain = Link(dve, s_v)

                def residual(t):
                    s = t % 3
                    dve.wait_ge(s_x[s], 16 * (t // 3 + 1))
                    dve.wait_ge(s_mm, t + 1)
                    V.scalar_tensor_tensor(xs_[s], xs_[s], ALPHA, duo[0][:, :], ALU.mult, ALU.add).then_inc(s_res, 1)

                def normalise(t):
                    s = t % 3
                    dve.wait_ge(s_res, t + 1)
                    V.bn_stats(ln[s][:, 0:6], xs_[s][:, 0:512])
                    chain(V.bn_stats(ln[s][:, 6:12], xs_[s][:, 512:1024]))
                    chain(V.bn_aggr(ln[s][:, 12:14], ln[s][:, 0:12]))
                    V.tensor_scalar_add(ln[s][:, 14:15], ln[s][:, 13:14], EPS).then_inc(s_var, 1)
                    dve.wait_ge(s_std, t + 1)
                    chain(V.reciprocal(ln[s][:, 16:17], ln[s][:, 15:16]))
                    V.tensor_scalar(ln[s][:, 17:18], ln[s][:, 12:13], ln[s][:, 16:17], -1.0,
                                    ALU.mult, ALU.mult).then_inc(s_nb, 1)
                    dve.wait_ge(s_cen, t + 1)
                    V.tensor_tensor(xs_[s], xs_[s], gb[:, 0, :], ALU.mult).then_inc(s_gn, 1)

                def take_logits(t):
                    dve.wait_ge(s_lg, t + 1)
                    V.tensor_copy(logits[:, t, :], bank[B_LG][:, 0:E]).then_inc(s_lc, 1)

                def sequence(b):
                    if b >= 1:
                        dve.wait_ge(s_sc, b)
                    new = slice(b * TS, b * TS + TS)
                    newc = slice(b * TS + NPR, b * TS + NPR + TS)
                    V.tensor_copy(qdiag[0:64, :, 0:TS], qs_T[0:64, :, new])
                    V.tensor_copy(qdiag[64:P, :, TS:2 * TS], qs_T[64:P, :, new])
                    V.tensor_copy(kT[:, :, PAST:NK], ks_T[:, :, new]).then_inc(s_q, 1)
                    V.tensor_copy(gates[0:H, PAST:NK], cum[:, newc])
                    dve.wait_ge(s_lt, b + 1)
                    V.tensor_copy(gates[0:H, 0:PAST], bank[B_SC][0:H, 0:PAST]).then_inc(s_gc, 1)
                    dve.wait_ge(s_gc, b + 1)
                    V.tensor_tensor_scan(sums[0:H, :], ones8[0:H, :], gates[0:H, :], 0.0, ALU.mult, ALU.add).then_inc(s_dc, 1)
                    dve.wait_ge(s_dc, b + 1)
                    V.tensor_scalar(nsums[0:H, :], sums[0:H, :], -1.0, None, ALU.mult)
                    V.tensor_tensor(qsum[0:H, :].rearrange("h (g q) -> h g q", g=H),
                                    by_head[0:H, :].rearrange("h (g q) -> h g q", g=H),
                                    sums[0:H, PAST:NK].unsqueeze(1).to_broadcast([H, H, TS]),
                                    ALU.mult).then_inc(s_cq, 1)
                    dve.wait_ge(s_sc, b + 1)
                    V.tensor_reduce(st[0:64, 0, 0:1], bank[B_SC][0:64, 0:NK], AX, ALU.max,
                                    negate=True).then_inc(s_mx, 1)
                    dve.wait_ge(s_ex, b + 1)
                    V.reciprocal(st[0:64, 2, 0:1], st[0:64, 1, 0:1]).then_inc(s_rc, 1)
                    dve.wait_ge(s_rc, b + 1)
                    V.tensor_scalar(pr_[0:64, :], pr_[0:64, :], st[0:64, 2, 0:1], None,
                                    ALU.mult).then_inc(s_ps, 1)

                def outputs(b):
                    dve.wait_ge(s_pv, b + 1)
                    newc = slice(b * TS + NPR, b * TS + NPR + TS)
                    u = bank[B_OUT][:, 0:64].rearrange("p (a n) -> p a n", a=4)
                    V.tensor_copy(mixT[0:64, 0:4, newc], u[0:64, :, 0:TS])
                    V.tensor_copy(mixT[64:P, 0:4, newc], u[64:P, :, TS:2 * TS]).then_inc(s_uc, 1)

                V.memset(ones8[0:H, :], 1.0)
                V.tensor_copy(by_head[0:H, :].rearrange("h (g q) -> h g q", g=H),
                              ident[0:H, 0:H].unsqueeze(2).to_broadcast([H, H, TS]))
                V.tensor_copy(by_query[0:TS, :].rearrange("h (g q) -> h g q", g=H),
                              ident[0:TS, 0:TS].unsqueeze(1).to_broadcast([TS, H, TS])).then_inc(s_cst, 1)
                dve.wait_ge(s_cst, 1)
                dve.wait_ge(s_gz, 1)
                dve.wait_ge(s_gb[0], 16)
                for t in range(NT + 1):
                    if t >= 1:
                        normalise(t - 1)
                    if t < BS:
                        sequence(t)
                    if t < NT:
                        residual(t)
                    if t >= 1:
                        take_logits(t - 1)
                    if t < BS:
                        outputs(t)

        weights, o = [], 0
        DW = KD * DE
        for _n in range(3):
            a_, o = carve(o, 3, DW)
            weights.append(a_.rearrange("p (s n) -> p s n", s=3))
        assert o <= AR
        srcs = (A["w_gate"][0].rearrange("e (p k) f -> e p (k f)", p=P),
                A["w_up"][0].rearrange("e (p k) f -> e p (k f)", p=P),
                A["w_down"][0].rearrange("e (p j) d -> e p (j d)", p=P))

        with phase() as (mem, block):
            def small(*shape):
                at = cursor[0]
                n = math.prod(shape)
                cursor[0] += n
                ap = vflat[:, at:at + n]
                if len(shape) == 1:
                    return ap
                if len(shape) == 2:
                    return ap.rearrange("p (a b) -> p a b", b=shape[1])
                return ap.rearrange("p (a b c) -> p a b c", b=shape[1], c=shape[2])

            cursor = [0]
            NG4 = E // EG
            before = small(P)
            all1 = small(P)
            valid = small(NT)
            aff, biased, masked, sel1, sel2, both = (small(NT, E) for _ in range(6))
            pairs = small(NT * NG4, 6)
            gscore = small(NT, NG4)
            best = small(NT)
            key4 = small(NT, NG4)
            pref4 = small(NG4)
            pref16 = small(E)
            scr = small(NT, E)
            rank, prior = small(NT, E), small(NT + 1, E)
            over = small(E, NT)
            thr = small(NT)
            tiles, upto_, base = small(E), small(E), small(E)
            slotf = small(NT, 2)
            tau = small(TT)
            cmp = small(TT, E)
            ef, chg, run = small(TT), small(TT + 1), small(TT)
            th3 = small(5)
            cmp3 = small(TT, 5)
            r3 = small(TT)
            th11 = small(ROUNDS)
            c11 = small(ROUNDS)
            nr = small(1)
            wsum = small(NT)
            br = mem.enter_context(nc.sbuf_tensor("br", [P, E], F32))
            tok_i = mem.enter_context(nc.sbuf_tensor("tok_i", [P, NT], I32))
            s_br = sem("t_router_bias")
            s_p = sem("t_pool_chain")
            s_v = sem("t_vector_chain")
            s_sg = sem("t_sigmoids")
            s_both = sem("t_choices")
            s_rk = sem("t_ranks")
            s_sl = sem("t_slots")
            s_sc = sem("t_scattered")
            s_tb = sem("t_tables_ready")
            s_w = [[sem(f"t_{k}_weights{s}") for s in range(3)] for k in ("gate", "up", "down")]

            @block.sync
            def _(sp):
                sp.dma_start(br[:, :], bcast_rows(A["b_router"], P)).then_inc(s_br, 16)
                sp.wait_ge(s_tb, 1)
                for s in range(3):
                    e, slot, new = (sp.value_load(tab_i[0:1, r, s:s + 1], min_val=0, max_val=m)
                                    for r, m in enumerate((E - 1, 2, 1)))
                    for k in range(3):
                        sp.dma_start(weights[k][:, bass.ds(slot, 1), :],
                                     srcs[k][bass.ds(e, 1), :, :].rearrange("a p n -> p a n"),
                                     cond=new > 0).then_inc(s_w[k][s], 16)
                sp.wait_ge(s_br, 16)
                for k in range(3):
                    for s in range(3):
                        sp.wait_ge(s_w[k][s], 16)

            @block.scalar
            def _(act):
                nc.scalar.activation(aff, logits[:, :, :], ACT.Sigmoid).then_inc(s_sg, 1)

            @block.tensor
            def _(pe):
                pe.wait_ge(s_p, 9)
                pe.wait_ge(s_both, 1)
                flat = both.rearrange("p t e -> p (t e)")
                nc.tensor.matmul(bank[0][:, 0:NT * E], before, flat, start=True, stop=True)
                nc.tensor.matmul(bank[1][:, 0:NT * E], all1, flat, start=True, stop=True).then_inc(s_rk, 1)

            @block.gpsimd
            def _(pool):
                G = nc.gpsimd
                chain = Link(pool, s_p)
                imp = dict(allow_small_or_imprecise_dtypes=True)
                chain(G.memset(all1, 1.0))
                chain(G.affine_select(out=before, in_=all1, compare_op=ALU.is_gt, fill=0.0, base=0,
                                      pattern=[[1, P]], channel_multiplier=-1))
                chain(G.affine_select(out=valid, in_=all1[:, 0:NT], compare_op=ALU.is_gt, fill=0.0, base=TOK,
                                      pattern=[[-P, NT]], channel_multiplier=-1))
                chain(G.iota(pref4, [[-1, NG4]], base=NG4, channel_multiplier=0, **imp))
                chain(G.iota(pref16, [[-1, E]], base=E, channel_multiplier=0, **imp))
                chain(G.iota(thr, [[P, NT]], base=0, channel_multiplier=0, **imp))
                chain(G.iota(tau, [[1, TT]], base=0, channel_multiplier=0, **imp))
                chain(G.iota(th3, [[3, 5]], base=3, channel_multiplier=0, **imp))
                chain(G.iota(th11, [[3, ROUNDS]], base=0, channel_multiplier=0, **imp))
                chain(G.iota(tok_i[:, :], [[P, NT]], base=0, channel_multiplier=1))
                pool.wait_ge(s_sl, 1)
                n = 0
                for t in range(NT):
                    rows = min(P, TOK - t * P)
                    for c in range(2):
                        G.indirect_dma_start(
                            out=slot_tok, out_offset=bass.IndirectOffsetOnAxis(ap=slot_i[0:rows, t, c:c + 1], axis=0),
                            in_=tok_i[0:rows, t:t + 1], in_offset=None).then_inc(s_sc, 16)
                        n += 1
                pool.wait_ge(s_sc, 16 * n)

            @block.vector
            def _(dve):
                V = nc.vector
                link = Link(dve, s_v)

                def tt(o_, a, b, op):
                    link(V.tensor_tensor(o_, a, b, op))

                def mx(o_, a):
                    link(V.tensor_reduce(o_, a, AX, ALU.max))

                def sm_(o_, a):
                    link(V.tensor_reduce(o_, a, AX, ALU.add))

                def inner(x, n):
                    return x.unsqueeze(len(x.shape)).to_broadcast(list(x.shape) + [n])

                def outer(x, n):
                    return x.unsqueeze(1).to_broadcast([P, n, x.shape[1]])

                dve.wait_ge(s_p, 10)
                dve.wait_ge(s_br, 16)
                dve.wait_ge(s_sg, 1)
                tt(biased, aff, outer(br[:, :], NT), ALU.add)
                b4 = biased.rearrange("p t (g e) -> p (t g) e", e=EG)
                V.tensor_tensor(pairs[:, :, 0:3], b4[:, :, 0:3], b4[:, :, 1:4], ALU.add)
                V.tensor_tensor(pairs[:, :, 3:5], b4[:, :, 0:2], b4[:, :, 2:4], ALU.add)
                tt(pairs[:, :, 5:6], b4[:, :, 0:1], b4[:, :, 3:4], ALU.add)
                mx(gscore.rearrange("p t g -> p (t g)"), pairs)
                mx(best, gscore)
                tt(key4, gscore, inner(best, NG4), ALU.is_ge)
                tt(key4, key4, outer(pref4, NT), ALU.mult)
                mx(best, key4)
                tt(key4, key4, inner(best, NG4), ALU.is_equal)
                g4 = key4.rearrange("p t g -> p (t g)")
                m4 = masked.rearrange("p t (g e) -> p (t g) e", e=EG)
                s4 = scr.rearrange("p t (g e) -> p (t g) e", e=EG)
                V.tensor_tensor(m4, b4, inner(g4, EG), ALU.mult)
                link(V.tensor_scalar(s4, inner(g4, EG), -NEG, NEG, ALU.mult, ALU.add))
                tt(masked, masked, scr, ALU.add)
                for sel in (sel1, sel2):
                    mx(best, masked)
                    tt(sel, masked, inner(best, E), ALU.is_ge)
                    tt(sel, sel, outer(pref16, NT), ALU.mult)
                    mx(best, sel)
                    tt(sel, sel, inner(best, E), ALU.is_equal)
                    link(V.scalar_tensor_tensor(masked, sel, 3 * NEG, masked, ALU.mult, ALU.add))
                for c, sel in enumerate((sel1, sel2)):
                    tt(scr, sel, aff, ALU.mult)
                    sm_(wsel[:, :, c], scr)
                tt(wsum, wsel[:, :, 0], wsel[:, :, 1], ALU.add)
                link(V.reciprocal(wsum, wsum))
                tt(wsel[:, :, :], wsel[:, :, :], inner(wsum, 2), ALU.mult)
                tt(both, sel1, sel2, ALU.add)
                V.tensor_tensor(both, both, inner(valid, E), ALU.mult).then_inc(s_both, 1)
                dve.wait_ge(s_rk, 1)
                V.tensor_copy(rank.rearrange("p t e -> p (t e)"), bank[0][:, 0:NT * E])
                link(V.memset(prior[:, 0, :], 0.0))
                for t in range(NT):
                    tt(prior[:, t + 1, :], prior[:, t, :], bank[1][:, t * E:(t + 1) * E], ALU.add)
                tt(over, inner(prior[:, NT, :], NT), outer(thr, E), ALU.is_gt)
                sm_(tiles, over)
                link(V.tensor_tensor_scan(upto_, all1[:, 0:E], tiles, 0.0, ALU.mult, ALU.add))
                tt(base, upto_, tiles, ALU.subtract)
                link(V.tensor_scalar(base, base, float(P), None, ALU.mult))
                tt(rank, rank, prior[:, 0:NT, :], ALU.add)
                tt(rank, rank, outer(base, NT), ALU.add)
                for c, sel in enumerate((sel1, sel2)):
                    tt(scr, sel, rank, ALU.mult)
                    sm_(slotf[:, :, c], scr)
                V.tensor_copy(slot_i[:, :, :], slotf).then_inc(s_sl, 1)
                tt(cmp, outer(upto_, TT), inner(tau, E), ALU.is_le)
                sm_(ef, cmp)
                link(V.tensor_scalar(ef, ef, float(E - 1), None, ALU.min))
                link(V.memset(chg[:, 0:1], 1.0))
                tt(chg[:, 1:TT], ef[:, 1:TT], ef[:, 0:TT - 1], ALU.not_equal)
                link(V.tensor_tensor_scan(run, all1[:, 0:TT], chg[:, 0:TT], -1.0, ALU.mult, ALU.add))
                tt(cmp3, inner(run, 5), outer(th3, TT), ALU.is_ge)
                sm_(r3, cmp3)
                link(V.scalar_tensor_tensor(r3, r3, -3.0, run, ALU.mult, ALU.add))
                tt(c11, upto_[:, E - 1:E].to_broadcast([P, ROUNDS]), th11, ALU.is_gt)
                sm_(nr, c11)
                V.tensor_copy(tab_i[:, 0, :], ef[0:1, :])
                V.tensor_copy(tab_i[:, 1, :], r3[0:1, :])
                V.tensor_copy(tab_i[:, 2, :], chg[0:1, 0:TT])
                V.tensor_copy(rounds_i[:, :], nr[0:1, :]).then_inc(s_tb, 1)

        with phase() as (mem, block):
            w_gs, w_us, w_ds = weights
            xg = [vflat[:, D * s:D * (s + 1)] for s in range(3)]
            mall = mixT[:, :, :].rearrange("p k t -> p (k t)")
            xgT = [mall[:, D * s:D * (s + 1)] for s in range(3)]
            ysl = [mall[:, D * (3 + s):D * (4 + s)] for s in range(3)]
            rest = mall[:, 6 * D:]
            sil = [rest[:, DE * s:DE * (s + 1)] for s in range(3)]
            hid = [rest[:, DE * (3 + s):DE * (4 + s)] for s in range(3)]
            hidT = [rest[:, DE * (6 + s):DE * (7 + s)] for s in range(3)]
            h_all = xT[:, :, :].rearrange("p k t -> p (k t)").rearrange("p (t d) -> p t d", d=D)
            idx_all = mem.enter_context(nc.sbuf_tensor("idx_all", [P, TT], I32))
            idx = [mem.enter_context(nc.sbuf_tensor(f"idx{s}", [P, 1], I32)) for s in range(3)]
            s_ix = sem("e_slot_tokens")
            s_pad = sem("e_padding_zeroed")
            s_ic = [sem(f"e_index_copied{s}") for s in range(3)]
            s_g = [sem(f"e_gathered{s}") for s in range(3)]
            s_w = [[sem(f"e_{k}_weights{s}") for s in range(3)] for k in ("gate", "up", "down")]
            s_xt = sem("e_rows_turned")
            s_xc = sem("e_rows_copied")
            s_gu = sem("e_gate_up")
            s_si = sem("e_silu")
            s_hid = sem("e_hidden")
            s_ht = sem("e_hidden_turned")
            s_he = sem("e_hidden_copied")
            s_dn = sem("e_down")
            s_yA = sem("e_output_low")
            s_yD = sem("e_output_high")
            s_yo = [sem(f"e_output_stored{s}") for s in range(3)]
            s_hl = [sem(f"e_h_loaded{n}") for n in range(3)]
            s_gb = [sem(f"e_gain_shift{n}") for n in range(2)]
            s_hold = sem("e_waits_held_by_sync")
            s_holdp = sem("e_waits_held_by_tensor")
            s_holdg = sem("e_waits_held_by_pool")

            def rounds(eng, prologue, body, epilogue):
                n = eng.value_load(rounds_i[0:1, 0:1], min_val=1, max_val=ROUNDS)
                prologue()
                for s in range(3):
                    body(s, 0, s, True)
                with eng.Fori(1, ROUNDS) as i:
                    with eng.If(i < n):
                        for s in range(3):
                            body(i * 3 + s, i, s, False)
                epilogue(n)

            @block.sync
            def _(sp):
                sp.dma_start(idx_all[:, 0:SLOTT], slot_tok.rearrange("(t p) a -> p (t a)", p=P)).then_inc(s_ix, 16)
                def load(tau, s):
                    e, slot, new = (sp.value_load(tab_i[0:1, r, bass.ds(tau, 1)], min_val=0, max_val=m)
                                    for r, m in enumerate((E - 1, 2, 1)))
                    for k in range(3):
                        sp.dma_start(weights[k][:, bass.ds(slot, 1), :],
                                     srcs[k][bass.ds(e, 1), :, :].rearrange("a p n -> p a n"),
                                     cond=new > 0).then_inc(s_w[k][s], 16)

                def store(tau, s):
                    sp.wait_ge(s_yA, tau + 2)
                    sp.sem_inc(s_hold, 1)
                    sp.wait_ge(s_yD, tau + 2)
                    sp.sem_inc(s_hold, 1)
                    rows = slice(tau * P, tau * P + P) if isinstance(tau, int) else bass.ds(tau * P, P)
                    sp.dma_start(y_park[rows, :], ysl[s]).then_inc(s_yo[s], 16)

                def prologue():
                    for s in range(3):
                        sp.sem_inc(s_yo[s], 16)
                        for k in range(3):
                            sp.sem_inc(s_w[k][s], 16)

                def body(tau, i, s, first):
                    sp.wait_ge(s_dn, tau + 1)
                    sp.sem_inc(s_hold, 1)
                    load(tau + 3, s)
                    store(tau, s)
                    if first:
                        sp.dma_start(h_all[:, 3 * s:3 * s + 3, :],
                                     h_park[3 * s * P:(3 * s + 3) * P, :].rearrange("(t p) d -> p t d", p=P)
                                     ).then_inc(s_hl[s], 16)
                        if s < 2:
                            sp.dma_start(gb[:, s, :], bcast_rows(A[("ln2_g", "ln2_b")[s]][0], P)
                                         ).then_inc(s_gb[s], 16)

                def epilogue(n):
                    for x in s_hl + s_gb:
                        sp.wait_ge(x, 16)
                    for s in range(3):
                        sp.wait_ge(s_yo[s], n * 16 + 16)
                        sp.sem_inc(s_hold, 1)
                        for k in range(3):
                            sp.wait_ge(s_w[k][s], n * 16 + 16)
                            sp.sem_inc(s_hold, 1)
                rounds(sp, prologue, body, epilogue)

            @block.gpsimd
            def _(pool):
                G = nc.gpsimd

                def gather(tau, i, s):
                    src = idx_all[:, tau:tau + 1] if isinstance(tau, int) else idx_all[:, bass.ds(tau, 1)]
                    G.tensor_copy(idx[s][:, :], src).then_inc(s_ic[s], 1)
                    pool.wait_ge(s_ic[s], i + 1)
                    pool.sem_inc(s_holdg, 1)
                    G.indirect_dma_start(out=xg[s], out_offset=None, in_=h_park,
                                         in_offset=bass.IndirectOffsetOnAxis(ap=idx[s][:, 0:1], axis=0)
                                         ).then_inc(s_g[s], 16)

                def prologue():
                    G.memset(idx_all[:, SLOTT:TT], 0).then_inc(s_pad, 1)
                    pool.wait_ge(s_pad, 1)
                    pool.wait_ge(s_ix, 16)
                    for s in range(3):
                        gather(s, 0, s)

                def body(tau, i, s, first):
                    pool.wait_ge(s_xt, tau * 2 + 2)
                    pool.sem_inc(s_holdg, 1)
                    pool.wait_ge(s_g[s], i * 16 + 16)
                    pool.sem_inc(s_holdg, 1)
                    gather(tau + 3, i + 1, s)

                def epilogue(n):
                    for s in range(3):
                        pool.wait_ge(s_g[s], n * 16 + 16)
                        pool.sem_inc(s_holdg, 1)
                rounds(pool, prologue, body, epilogue)

            @block.tensor
            def _(pe):
                T = nc.tensor

                def waited():
                    pe.sem_inc(s_holdp, 1)

                def turn_x(tau, i, s):
                    pe.wait_ge(s_g[s], i * 16 + 16)
                    for half in range(2):
                        if not (isinstance(tau, int) and tau == 0):
                            pe.wait_ge(s_xc, tau * 2 - 1 + half)
                        waited()
                        for k in range(4):
                            last = T.transpose(bank[half][:, k * P:(k + 1) * P],
                                               xg[s][:, 4 * half + k::KD], ident[:, :])
                        last.then_inc(s_xt, 1)

                def half_gu(tau, i, s, which, slot):
                    if which == 0:
                        pe.wait_ge(s_xc, tau * 2 + 2)
                    pe.wait_ge(s_w[which][s], i * 16 + 16)
                    waited()
                    for k in range(KD):
                        last = T.matmul(bank[2 + s][:, DE * which:DE * (which + 1)], xgT[s][:, k * P:(k + 1) * P],
                                        weights[which][:, bass.ds(slot, 1), k * DE:(k + 1) * DE],
                                        start=(k == 0), stop=(k == KD - 1))
                    if which == 1:
                        last.then_inc(s_gu, 1)

                def turn_hidden(tau, s):
                    pe.wait_ge(s_hid, tau + 1)
                    pe.wait_ge(s_he, tau + 1)
                    waited()
                    for j in range(2):
                        last = T.transpose(bank[5][:, j * P:(j + 1) * P], hid[s][:, j::2], ident[:, :])
                    last.then_inc(s_ht, 1)

                def down(tau, i, off, s, slot):
                    pe.wait_ge(s_he, tau + 2)
                    pe.wait_ge(s_w[2][s], i * 16 + (16 * off + 16))
                    pe.wait_ge(s_yA, tau + 1)
                    pe.wait_ge(s_yD, tau + 1)
                    waited()
                    for half in range(2):
                        for j in range(2):
                            last = T.matmul(bank[6 + half], hidT[s][:, j * P:(j + 1) * P],
                                            w_ds[:, bass.ds(slot, 1), j * D + 512 * half:j * D + 512 * half + 512],
                                            start=(j == 0), stop=(j == 1))
                    last.then_inc(s_dn, 1)

                def slot_of(tau):
                    return pe.value_load(tab_i[0:1, 1, bass.ds(tau, 1)], min_val=0, max_val=2)

                def prologue():
                    turn_x(0, 0, 0)

                def body(tau, i, s, first):
                    back = not (first and s == 0)
                    slot = slot_of(tau)
                    half_gu(tau, i, s, 0, slot)
                    if back:
                        turn_hidden(tau - 1, (s - 1) % 3)
                    half_gu(tau, i, s, 1, slot)
                    turn_x(tau + 1, i + (1 if s == 2 else 0), (s + 1) % 3)
                    if back:
                        down(tau - 1, i, 0 if s else -1, (s - 1) % 3, slot_of(tau - 1))

                def epilogue(n):
                    turn_hidden(n * 3 - 1, 2)
                    down(n * 3 - 1, n, -1, 2, slot_of(n * 3 - 1))
                rounds(pe, prologue, body, epilogue)

            @block.scalar
            def _(act):
                S = nc.scalar

                def copy_x(tau, s):
                    for half in range(2):
                        act.wait_ge(s_xt, tau * 2 + (half + 1))
                        S.copy(xgT[s][:, 512 * half:512 * half + 512], bank[half]).then_inc(s_xc, 1)

                def low(tau, i, off, s):
                    act.wait_ge(s_dn, tau + 1)
                    act.wait_ge(s_yo[s], i * 16 + (16 * off + 16))
                    S.copy(ysl[s][:, 0:512], bank[6]).then_inc(s_yA, 1)

                def prologue():
                    act.sem_inc(s_yA, 1)
                    copy_x(0, 0)

                def body(tau, i, s, first):
                    act.wait_ge(s_gu, tau + 1)
                    S.activation(sil[s], bank[2 + s][:, 0:DE], ACT.Silu).then_inc(s_si, 1)
                    copy_x(tau + 1, (s + 1) % 3)
                    if not (first and s == 0):
                        low(tau - 1, i, 0 if s else -1, (s - 1) % 3)

                def epilogue(n):
                    low(n * 3 - 1, n, -1, 2)
                rounds(act, prologue, body, epilogue)

            @block.vector
            def _(dve):
                V = nc.vector

                def copy_hidden(tau, s):
                    dve.wait_ge(s_ht, tau + 1)
                    V.tensor_copy(hidT[s], bank[5][:, 0:DE]).then_inc(s_he, 1)

                def high(tau, i, off, s):
                    dve.wait_ge(s_dn, tau + 1)
                    dve.wait_ge(s_yo[s], i * 16 + (16 * off + 16))
                    V.tensor_copy(ysl[s][:, 512:D], bank[7]).then_inc(s_yD, 1)

                def body(tau, i, s, first):
                    back = not (first and s == 0)
                    if back:
                        copy_hidden(tau - 1, (s - 1) % 3)
                    dve.wait_ge(s_si, tau + 1)
                    V.tensor_tensor(hid[s], sil[s], bank[2 + s][:, DE:2 * DE], ALU.mult).then_inc(s_hid, 1)
                    if back:
                        high(tau - 1, i, 0 if s else -1, (s - 1) % 3)

                def epilogue(n):
                    copy_hidden(n * 3 - 1, 2)
                    high(n * 3 - 1, n, -1, 2)
                def prologue():
                    dve.sem_inc(s_he, 1)
                    dve.sem_inc(s_yD, 1)
                rounds(dve, prologue, body, epilogue)

        with phase() as (mem, block):
            o = 0
            SLOTS = 8
            ya, yb = [], []
            hh = [h_all[:, t, :] for t in range(NT)]
            for lst in (ya, yb):
                for _s in range(SLOTS):
                    a_, o = carve(o, D)
                    lst.append(a_)
            st = [mem.enter_context(nc.sbuf_tensor(f"ln2_st{s}", [P, 20], F32)) for s in range(SLOTS)]
            s_ya = [sem(f"f_first_rows{s}") for s in range(SLOTS)]
            s_yb = [sem(f"f_second_rows{s}") for s in range(SLOTS)]
            s_w1 = sem("f_first_weighted")
            s_sum = sem("f_summed")
            s_v = sem("f_vector_chain")
            s_var = sem("f_variance")
            s_std = sem("f_std")
            s_nb = sem("f_bias")
            s_cen = sem("f_centred")
            s_gn = sem("f_gained")
            s_y = sem("f_output_ready")
            s_o = [sem(f"f_output_stored{s}") for s in range(SLOTS)]

            @block.sync
            def _(sp):
                yp = O["y_prompt"][0]
                for t in range(NT):
                    s = t % SLOTS
                    sp.wait_ge(s_y, t + 1)
                    if t == 0:
                        sp.dma_start(yp[0:P - META, :], hh[t][META:P, :]).then_inc(s_o[s], 16)
                    elif t < NT - 1:
                        sp.dma_start(yp[t * P - META:(t + 1) * P - META, :], hh[t]).then_inc(s_o[s], 16)
                    else:
                        sp.dma_start(yp[t * P - META:SEQ, :], hh[t][0:META, :]).then_inc(s_o[s], 16)
                        sp.dma_start(O["y_sample"].rearrange("b t d -> (b t) d"),
                                     hh[t][META:META + NSA, :]).then_inc(s_o[s], 16)
                for s in range(SLOTS):
                    sp.wait_ge(s_o[s], 16 * len(range(s, NT, SLOTS)) + (16 if s == (NT - 1) % SLOTS else 0))

            @block.gpsimd
            def _(pool):
                G = nc.gpsimd

                def gather(t):
                    s = t % SLOTS
                    rows = min(P, TOK - t * P)
                    if t >= SLOTS:
                        pool.wait_ge(s_sum, 2 * (t - SLOTS + 1))
                    for c, (dst, sm_) in enumerate(((ya, s_ya), (yb, s_yb))):
                        G.indirect_dma_start(out=dst[s][0:rows, :], out_offset=None, in_=y_park,
                                             in_offset=bass.IndirectOffsetOnAxis(ap=slot_i[0:rows, t, c:c + 1], axis=0)
                                             ).then_inc(sm_[s], 16)
                for t in range(SLOTS):
                    gather(t)
                for t in range(NT):
                    rows = min(P, TOK - t * P)
                    pool.wait_ge(s_gn, t + 1)
                    G.tensor_tensor(hh[t][0:rows, :], hh[t][0:rows, :], gb[0:rows, 1, :], ALU.add).then_inc(s_y, 1)
                    if t + SLOTS < NT:
                        gather(t + SLOTS)

            @block.scalar
            def _(act):
                S = nc.scalar
                for t in range(NT + 1):
                    if t < NT:
                        s = t % SLOTS
                        rows = slice(0, min(P, TOK - t * P))
                        act.wait_ge(s_ya[s], 16 * (t // SLOTS + 1))
                        S.activation(ya[s][rows, :], ya[s][rows, :], ACT.Copy, scale=wsel[rows, t, 0:1]).then_inc(s_w1, 1)
                    if t:
                        u, s = t - 1, (t - 1) % SLOTS
                        rows = slice(0, min(P, TOK - u * P))
                        act.wait_ge(s_var, u + 1)
                        S.activation(st[s][rows, 15:16], st[s][rows, 14:15], ACT.Sqrt).then_inc(s_std, 1)
                        act.wait_ge(s_nb, u + 1)
                        S.activation(hh[u][rows, :], hh[u][rows, :], ACT.Identity, bias=st[s][rows, 17:18],
                                     scale=st[s][rows, 16:17]).then_inc(s_cen, 1)

            @block.vector
            def _(dve):
                V = nc.vector
                chain = Link(dve, s_v)

                def gain(t):
                    s = t % SLOTS
                    rows = slice(0, min(P, TOK - t * P))
                    dve.wait_ge(s_cen, t + 1)
                    V.tensor_tensor(hh[t][rows, :], hh[t][rows, :], gb[rows, 0, :], ALU.mult).then_inc(s_gn, 1)

                for t in range(NT):
                    s = t % SLOTS
                    rows = slice(0, min(P, TOK - t * P))
                    dve.wait_ge(s_yb[s], 16 * (t // SLOTS + 1))
                    dve.wait_ge(s_w1, t + 1)
                    V.scalar_tensor_tensor(yb[s][rows, :], yb[s][rows, :], wsel[rows, t, 1:2], ya[s][rows, :],
                                           ALU.mult, ALU.add).then_inc(s_sum, 1)
                    dve.wait_ge(s_sum, 2 * t + 1)
                    V.scalar_tensor_tensor(hh[t][rows, :], hh[t][rows, :], ALPHA, yb[s][rows, :],
                                           ALU.mult, ALU.add).then_inc(s_sum, 1)
                    dve.wait_ge(s_sum, 2 * t + 2)
                    V.bn_stats(st[s][rows, 0:6], hh[t][rows, 0:512])
                    chain(V.bn_stats(st[s][rows, 6:12], hh[t][rows, 512:1024]))
                    chain(V.bn_aggr(st[s][rows, 12:14], st[s][rows, 0:12]))
                    V.tensor_scalar_add(st[s][rows, 14:15], st[s][rows, 13:14], EPS).then_inc(s_var, 1)
                    if t:
                        gain(t - 1)
                    dve.wait_ge(s_std, t + 1)
                    chain(V.reciprocal(st[s][rows, 16:17], st[s][rows, 15:16]))
                    V.tensor_scalar(st[s][rows, 17:18], st[s][rows, 12:13], st[s][rows, 16:17], -1.0,
                                    ALU.mult, ALU.mult).then_inc(s_nb, 1)
                gain(NT - 1)


_INS = ["x_prompt", "x_sample", "cache_k", "cache_v", "cache_logf", "page_table", "state_ssm_re", "state_ssm_im",
        "state_pool", "meta_tokens", "ln0_g", "ln0_b", "w_in", "b_forget", "ssm_lam_re", "ssm_lam_im",
        "ssm_log_dt", "ssm_b_re", "ssm_b_im", "ssm_c_re", "ssm_c_im", "ssm_d", "w_glu", "b_glu", "w_pool",
        "s_pool", "w_out", "ln1_g", "ln1_b", "w_router", "b_router", "w_gate", "w_up", "w_down", "ln2_g", "ln2_b"]
_OUTS = [("y_prompt", (1, SEQ, D)), ("y_sample", (BS, TS, D)),
         ("k_prompt", (1, 1, NPR, H, HD)), ("v_prompt", (1, 1, NPR, H, HD)), ("logf_prompt", (1, 1, NPR, H)),
         ("ssm_re_prompt", (1, 1, 16, 64)), ("ssm_im_prompt", (1, 1, 16, 64)), ("pool_prompt", (1, 1, PBUF, DPL)),
         ("k_sample", (BS, 1, TS, H, HD)), ("v_sample", (BS, 1, TS, H, HD)), ("logf_sample", (BS, 1, TS, H)),
         ("ssm_re_sample", (BS, 1, 16, 64)), ("ssm_im_sample", (BS, 1, 16, 64)), ("pool_sample", (BS, 1, PBUF, DPL))]


def kernel(**inputs):
    import numpy as _np
    import concourse.bacc as _bacc
    from concourse.bass_utils import run_bass_kernel_spmd as _run

    nc = _bacc.Bacc("TRN2", target_bir_lowering=False, num_devices=1)
    arrays, ins, outs = {}, {}, {}
    for name in _INS:
        a = _np.ascontiguousarray(inputs[name])
        arrays[f"in_{name}"] = a
        ins[name] = nc.dram_tensor(f"in_{name}", a.shape, mybir.dt.from_np(a.dtype), kind="ExternalInput").ap()
    for name, shape in _OUTS:
        outs[name] = nc.dram_tensor(f"out_{name}", shape, F32, kind="ExternalOutput").ap()
    hybrid_step(nc, ins, outs)
    r = _run(nc, [arrays], core_ids=[0])
    return tuple(r.results[0][f"out_{name}"] for name, _ in _OUTS)
```
